# Optimizing a Trainium2 kernel written in Bass

```python
import math
import jax
import jax.numpy as jnp
from jax import lax
import numpy as np

D_MODEL = 1024
BATCH = 1
SEQ = 256
DEPTH = 2
DEC_BATCH = 8
DEC_SEQ = 4
PAST_LEN = 256
PAGE_SIZE = 128

HEAD_DIM = 64
H_A = 8
H_B = 8
MIX_W_EVEN = (H_A + H_B) * HEAD_DIM
DIL_PATTERNS = ((128, 1), (512, 4), (2048, 16))
WINDOW_MAX = 2048
DIL_Q_BLOCK = 64
SB_Q_BLOCK = 128
SB_BIAS_INIT = -6.0
H_C = 4
DK_C = 128
DV_C = 128
H_D = 16
P_D = 64
N_D = 64
G_D = 4
D_INNER_D = H_D * P_D
CONV_W = 4
CONV_DIM = D_INNER_D + 2 * G_D * N_D
MIX_W_ODD = H_C * DV_C + D_INNER_D
IN_W_ODD = 2 * H_C * DK_C + 2 * H_C * DV_C + D_INNER_D + CONV_DIM + H_D
CHUNK = 64
D_FF = 2816
N_EXPERTS = 8
TOP_K = 2
D_FF_E = 3584
N_EVEN = (DEPTH + 1) // 2
N_ODD = DEPTH // 2
EPS = 1e-6

kernel_name = 'hybrid_dilated_stickbreak_hgrn2_mamba2_step'

def rms_normalize(x):
    xf = x.astype(jnp.float32)
    return (xf * lax.rsqrt(jnp.mean(xf * xf, axis=-1, keepdims=True) + EPS)).astype(x.dtype)

def rms_norm(x, g):
    return rms_normalize(x) * g.astype(x.dtype)

def alibi_slopes(n):
    return jnp.exp2(-8.0 * jnp.arange(1, n + 1, dtype=jnp.float32) / n)

def split_even(xn, w_in):
    b, t, _ = xn.shape
    qkv = jnp.einsum('btd,de->bte', xn, w_in).reshape(b, t, 3, H_A + H_B, HEAD_DIM)
    q, k, v = qkv[:, :, 0], qkv[:, :, 1], qkv[:, :, 2]
    return (q[:, :, :H_A], k[:, :, :H_A], v[:, :, :H_A]), (q[:, :, H_A:], k[:, :, H_A:], v[:, :, H_A:])

def merge_even(o_a, o_b, w_out):
    b, t = o_a.shape[:2]
    o = jnp.concatenate([o_a, o_b], axis=2).reshape(b, t, MIX_W_EVEN)
    return jnp.einsum('bte,ed->btd', o, w_out)

def dilated_attention(q, k_buf, v_buf, q_row):
    slopes = alibi_slopes(H_A)
    scale = HEAD_DIM ** -0.5
    lses, outs = [], []
    for window, dil in DIL_PATTERNS:
        dist = jnp.arange(window // dil + 1, dtype=jnp.int32) * dil
        rows = q_row[:, None] - dist[None, :]
        valid = rows >= 0
        rows = jnp.maximum(rows, 0)
        kg = k_buf[:, rows]
        vg = v_buf[:, rows]
        s = jnp.einsum('bqhd,bqjhd->bhqj', q, kg).astype(jnp.float32) * scale
        s = s - slopes[:, None, None] * dist.astype(jnp.float32)
        s = jnp.where(valid, s, -jnp.inf)
        lse = jax.nn.logsumexp(s, axis=-1)
        p = jnp.exp(s - lse[..., None]).astype(v_buf.dtype)
        outs.append(jnp.einsum('bhqj,bqjhd->bqhd', p, vg))
        lses.append(lse)
    w = jax.nn.softmax(jnp.stack(lses, axis=0), axis=0)
    out = jnp.swapaxes(w[0], 1, 2)[..., None].astype(outs[0].dtype) * outs[0]
    for g in range(1, len(outs)):
        out = out + jnp.swapaxes(w[g], 1, 2)[..., None].astype(outs[g].dtype) * outs[g]
    return out

def stick_breaking(q, k, v, q_row, bias):
    scale = HEAD_DIM ** -0.5
    z = jnp.einsum('bqhd,bkhd->bhqk', q, k).astype(jnp.float32) * scale + bias.astype(jnp.float32)[:, None, None]
    causal = jnp.arange(k.shape[1], dtype=jnp.int32)[None, :] < q_row[:, None]
    log_keep = jnp.where(causal, jax.nn.log_sigmoid(-z), 0.0)
    after = lax.cumsum(log_keep, axis=3, reverse=True) - log_keep
    a = jnp.where(causal, jnp.exp(jax.nn.log_sigmoid(z) + after), 0.0)
    return jnp.einsum('bhqk,bkhd->bqhd', a.astype(v.dtype), v)

def map_query_blocks(fn, q, block):
    b, t, h, d = q.shape
    nb = t // block
    qb = jnp.swapaxes(q.reshape(b, nb, block, h, d), 0, 1)
    rows = jnp.arange(t, dtype=jnp.int32).reshape(nb, block)
    out = lax.map(lambda args: fn(args[0], args[1]), (qb, rows))
    return jnp.swapaxes(out, 0, 1).reshape(b, t, h, -1)

def to_chunks(x, chunk):
    b, t = x.shape[:2]
    return jnp.swapaxes(x.reshape(b, t // chunk, chunk, *x.shape[2:]), 0, 1)

def from_chunks(x):
    x = jnp.swapaxes(x, 0, 1)
    return x.reshape(x.shape[0], x.shape[1] * x.shape[2], *x.shape[3:])

def gla_chunked(q, k, v, log_f, s0, chunk):
    mask = jnp.tril(jnp.ones((chunk, chunk), dtype=bool))

    def step(s, inp):
        qc, kc, vc, gc = inp
        g = jnp.cumsum(gc, axis=1)
        o_inter = jnp.einsum('bthk,bhkv->bthv', qc * jnp.exp(g), s)
        diff = jnp.where(mask[None, :, :, None, None], g[:, :, None] - g[:, None, :], -jnp.inf)
        att = jnp.einsum('bthk,bshk,btshk->bhts', qc, kc, jnp.exp(diff))
        o_intra = jnp.einsum('bhts,bshv->bthv', att, vc)
        g_last = g[:, -1]
        s_new = jnp.exp(g_last)[..., None] * s + jnp.einsum('bshk,bshv->bhkv', kc * jnp.exp(g_last[:, None] - g), vc)
        return s_new, o_inter + o_intra

    xs = (to_chunks(q.astype(jnp.float32), chunk), to_chunks(k.astype(jnp.float32), chunk),
          to_chunks(v.astype(jnp.float32), chunk), to_chunks(log_f.astype(jnp.float32), chunk))
    s_fin, o = lax.scan(step, s0.astype(jnp.float32), xs)
    return from_chunks(o).astype(v.dtype), s_fin

def ssd_chunked(xdt, a, bh, ch, s0, chunk):
    mask = jnp.tril(jnp.ones((chunk, chunk), dtype=bool))

    def step(s, inp):
        xc, ac, bc, cc = inp
        acum = jnp.cumsum(ac, axis=1)
        o_inter = jnp.einsum('bthn,bhpn->bthp', cc * jnp.exp(acum)[..., None], s)
        decay = jnp.exp(jnp.where(mask[None, :, :, None], acum[:, :, None] - acum[:, None], -jnp.inf))
        scores = jnp.einsum('bthn,bshn->btsh', cc, bc) * decay
        o_intra = jnp.einsum('btsh,bshp->bthp', scores, xc)
        a_last = acum[:, -1]
        s_new = jnp.exp(a_last)[..., None, None] * s + jnp.einsum(
            'bshn,bshp->bhpn', bc * jnp.exp(a_last[:, None] - acum)[..., None], xc)
        return s_new, o_inter + o_intra

    xs = (to_chunks(xdt.astype(jnp.float32), chunk), to_chunks(a.astype(jnp.float32), chunk),
          to_chunks(bh.astype(jnp.float32), chunk), to_chunks(ch.astype(jnp.float32), chunk))
    s_fin, o = lax.scan(step, s0.astype(jnp.float32), xs)
    return from_chunks(o).astype(xdt.dtype), s_fin

def causal_conv(xbc, conv_buf, conv_w, conv_b):
    t = xbc.shape[1]
    xp = jnp.concatenate([conv_buf.astype(xbc.dtype), xbc], axis=1)
    out = conv_b.astype(xbc.dtype)
    for j in range(CONV_W):
        out = out + xp[:, j:j + t] * conv_w[j].astype(xbc.dtype)
    return jax.nn.silu(out), xp[:, t:]

def odd_mixer(xn, w_in, w_out, lb, hgrn_gain, conv_w, conv_b, dt_bias, a_log, d_skip, ssm_gain,
              s_hgrn0, s_ssm0, conv_buf, chunk):
    b, t, _ = xn.shape
    kd, vd = H_C * DK_C, H_C * DV_C
    cuts = (kd, 2 * kd, 2 * kd + vd, 2 * kd + 2 * vd, 2 * kd + 2 * vd + D_INNER_D,
            2 * kd + 2 * vd + D_INNER_D + CONV_DIM)
    proj = jnp.einsum('btd,de->bte', xn, w_in)
    q_raw, f_raw, i_raw, g_raw, z, xbc, dt_raw = jnp.split(proj, cuts, axis=-1)
    f_raw = f_raw.astype(jnp.float32)
    log_f = jnp.log(lb + (1.0 - lb) * jax.nn.sigmoid(f_raw))
    k = (1.0 - lb) * jax.nn.sigmoid(-f_raw)
    o_c, s_hgrn = gla_chunked(jax.nn.silu(q_raw).reshape(b, t, H_C, DK_C), k.reshape(b, t, H_C, DK_C),
                              i_raw.reshape(b, t, H_C, DV_C), log_f.reshape(b, t, H_C, DK_C), s_hgrn0, chunk)
    o_c = rms_normalize(o_c).reshape(b, t, vd) * hgrn_gain.astype(xn.dtype) * jax.nn.silu(g_raw)
    xbc_c, conv_new = causal_conv(xbc, conv_buf, conv_w, conv_b)
    xs, bm, cm = jnp.split(xbc_c, (D_INNER_D, D_INNER_D + G_D * N_D), axis=-1)
    dt = jax.nn.softplus(dt_raw.astype(jnp.float32) + dt_bias.astype(jnp.float32))
    a = -jnp.exp(a_log.astype(jnp.float32)) * dt
    xh = xs.reshape(b, t, H_D, P_D)
    rep = H_D // G_D
    bh = jnp.repeat(bm.reshape(b, t, G_D, N_D), rep, axis=2)
    ch = jnp.repeat(cm.reshape(b, t, G_D, N_D), rep, axis=2)
    y, s_ssm = ssd_chunked(xh * dt[..., None].astype(xh.dtype), a, bh, ch, s_ssm0, chunk)
    y = y + d_skip[:, None].astype(xh.dtype) * xh
    y = y.reshape(b, t, D_INNER_D) * jax.nn.silu(z)
    y = rms_normalize(y.reshape(b, t, G_D, D_INNER_D // G_D)).reshape(b, t, D_INNER_D) * ssm_gain.astype(xn.dtype)
    out = jnp.einsum('bte,ed->btd', jnp.concatenate([o_c, y], axis=-1), w_out)
    return out, s_hgrn, s_ssm, conv_new

def swiglu(xn, w1, w3, w2):
    return jnp.einsum('btf,fd->btd', jax.nn.silu(xn @ w1) * (xn @ w3), w2)

def moe_swiglu(xn, w_router, we1, we3, we2):
    logits = jnp.einsum('btd,de->bte', xn, w_router).astype(jnp.float32)
    top_val, top_idx = lax.top_k(logits, TOP_K)
    top_w = jax.nn.softmax(top_val, axis=-1)
    gate = jnp.sum(jax.nn.one_hot(top_idx, N_EXPERTS, dtype=jnp.float32) * top_w[..., None], axis=-2)
    out = jnp.zeros_like(xn)
    for e in range(N_EXPERTS):
        out = out + gate[..., e:e + 1].astype(xn.dtype) * swiglu(xn, we1[e], we3[e], we2[e])
    return out

def setup_inputs(seed: int = 0) -> dict:
    key = jax.random.key(seed)
    ks = iter(jax.random.split(key, 48))
    f32 = jnp.float32

    def nrm(shape, scale):
        return jax.random.normal(next(ks), shape, f32) * scale

    def gain(shape):
        return 1.0 + nrm(shape, 0.02)

    n_pages = PAST_LEN // PAGE_SIZE
    n_used = DEC_BATCH * n_pages
    n_phys = n_used + max(1, n_used // 4)
    buf_rows = min(WINDOW_MAX, PAST_LEN)
    page_table = jax.random.permutation(next(ks), n_phys)[:n_used].reshape(DEC_BATCH, n_pages).astype(jnp.int32)
    dt0 = jnp.exp(jax.random.uniform(next(ks), (N_ODD, H_D), f32, math.log(1e-3), math.log(1e-1)))
    dt_bias = dt0 + jnp.log(-jnp.expm1(-dt0))
    a_log = jnp.log(jax.random.uniform(next(ks), (N_ODD, H_D), f32, 1.0, 16.0))
    return {
        'x_prompt': nrm((BATCH, SEQ, D_MODEL), 1.0),
        'x_sample': nrm((DEC_BATCH, DEC_SEQ, D_MODEL), 1.0),
        'cache_win_k': nrm((DEC_BATCH, N_EVEN, buf_rows, H_A, HEAD_DIM), 1.0),
        'cache_win_v': nrm((DEC_BATCH, N_EVEN, buf_rows, H_A, HEAD_DIM), 1.0),
        'cache_sb_k': nrm((n_phys, N_EVEN, PAGE_SIZE, H_B, HEAD_DIM), 1.0),
        'cache_sb_v': nrm((n_phys, N_EVEN, PAGE_SIZE, H_B, HEAD_DIM), 1.0),
        'page_table': page_table,
        'state_hgrn': nrm((DEC_BATCH, N_ODD, H_C, DK_C, DV_C), 0.5),
        'state_ssm': nrm((DEC_BATCH, N_ODD, H_D, P_D, N_D), 0.1),
        'state_conv': nrm((DEC_BATCH, N_ODD, CONV_W - 1, CONV_DIM), 1.0),
        'norm_mix_even': gain((N_EVEN, D_MODEL)),
        'w_in_even': nrm((N_EVEN, D_MODEL, 3 * MIX_W_EVEN), D_MODEL ** -0.5),
        'w_out_even': nrm((N_EVEN, MIX_W_EVEN, D_MODEL), MIX_W_EVEN ** -0.5),
        'sb_bias': SB_BIAS_INIT + nrm((N_EVEN, H_B), 0.2),
        'norm_ffn_even': gain((N_EVEN, D_MODEL)),
        'w1_ffn': nrm((N_EVEN, D_MODEL, D_FF), D_MODEL ** -0.5),
        'w3_ffn': nrm((N_EVEN, D_MODEL, D_FF), D_MODEL ** -0.5),
        'w2_ffn': nrm((N_EVEN, D_FF, D_MODEL), D_FF ** -0.5),
        'norm_mix_odd': gain((N_ODD, D_MODEL)),
        'w_in_odd': nrm((N_ODD, D_MODEL, IN_W_ODD), D_MODEL ** -0.5),
        'hgrn_lb_logits': nrm((DEPTH, H_C * DK_C), 0.1),
        'hgrn_gain': gain((N_ODD, H_C * DV_C)),
        'conv_w': nrm((N_ODD, CONV_W, CONV_DIM), CONV_W ** -0.5),
        'conv_b': nrm((N_ODD, CONV_DIM), 0.01),
        'dt_bias': dt_bias,
        'a_log': a_log,
        'd_skip': gain((N_ODD, H_D)),
        'ssm_gain': gain((N_ODD, D_INNER_D)),
        'w_out_odd': nrm((N_ODD, MIX_W_ODD, D_MODEL), MIX_W_ODD ** -0.5),
        'norm_ffn_odd': gain((N_ODD, D_MODEL)),
        'w_router': nrm((N_ODD, D_MODEL, N_EXPERTS), D_MODEL ** -0.5),
        'we1': nrm((N_ODD, N_EXPERTS, D_MODEL, D_FF_E), D_MODEL ** -0.5),
        'we3': nrm((N_ODD, N_EXPERTS, D_MODEL, D_FF_E), D_MODEL ** -0.5),
        'we2': nrm((N_ODD, N_EXPERTS, D_FF_E, D_MODEL), D_FF_E ** -0.5),
        'norm_final': gain((D_MODEL,)),
    }

def reference(x_prompt, x_sample, cache_win_k, cache_win_v, cache_sb_k, cache_sb_v, page_table,
              state_hgrn, state_ssm, state_conv,
              norm_mix_even, w_in_even, w_out_even, sb_bias, norm_ffn_even, w1_ffn, w3_ffn, w2_ffn,
              norm_mix_odd, w_in_odd, hgrn_lb_logits, hgrn_gain, conv_w, conv_b, dt_bias, a_log, d_skip,
              ssm_gain, w_out_odd, norm_ffn_odd, w_router, we1, we3, we2, norm_final):
    lb_all = jnp.cumsum(jax.nn.softmax(hgrn_lb_logits.astype(jnp.float32), axis=0), axis=0)
    lb_all = lb_all - lb_all[0]
    hp, hs = x_prompt, x_sample
    bp, tp = hp.shape[:2]
    bs, ts = hs.shape[:2]
    wk_p, wv_p, wk_s, wv_s = [], [], [], []
    sk_p, sv_p, sk_s, sv_s = [], [], [], []
    hg_p, hg_s, ss_p, ss_s, cv_p, cv_s = [], [], [], [], [], []
    for layer in range(DEPTH):
        if layer % 2 == 0:
            e = layer // 2
            bias_e = sb_bias[e]
            xn = rms_norm(hp, norm_mix_even[e])
            (qa, ka, va), (qb, kb, vb) = split_even(xn, w_in_even[e])
            o_a = map_query_blocks(lambda qq, rr: dilated_attention(qq, ka, va, rr), qa, DIL_Q_BLOCK)
            o_b = map_query_blocks(lambda qq, rr: stick_breaking(qq, kb, vb, rr, bias_e), qb, SB_Q_BLOCK)
            hp = hp + merge_even(o_a, o_b, w_out_even[e])
            w_rows = min(WINDOW_MAX, tp)
            wk_p.append(ka[:, tp - w_rows:])
            wv_p.append(va[:, tp - w_rows:])
            sk_p.append(kb)
            sv_p.append(vb)
            xn = rms_norm(hs, norm_mix_even[e])
            (qa, ka, va), (qb, kb, vb) = split_even(xn, w_in_even[e])
            buf_rows = cache_win_k.shape[2]
            k_buf = jnp.concatenate([cache_win_k[:, e].astype(ka.dtype), ka], axis=1)
            v_buf = jnp.concatenate([cache_win_v[:, e].astype(va.dtype), va], axis=1)
            o_a = dilated_attention(qa, k_buf, v_buf, buf_rows + jnp.arange(ts, dtype=jnp.int32))
            past_len = page_table.shape[1] * PAGE_SIZE
            k_past = cache_sb_k[page_table, e].reshape(bs, past_len, H_B, HEAD_DIM).astype(kb.dtype)
            v_past = cache_sb_v[page_table, e].reshape(bs, past_len, H_B, HEAD_DIM).astype(vb.dtype)
            k_all = jnp.concatenate([k_past, kb], axis=1)
            v_all = jnp.concatenate([v_past, vb], axis=1)
            o_b = stick_breaking(qb, k_all, v_all, past_len + jnp.arange(ts, dtype=jnp.int32), bias_e)
            hs = hs + merge_even(o_a, o_b, w_out_even[e])
            wk_s.append(ka)
            wv_s.append(va)
            sk_s.append(kb)
            sv_s.append(vb)
            hp = hp + swiglu(rms_norm(hp, norm_ffn_even[e]), w1_ffn[e], w3_ffn[e], w2_ffn[e])
            hs = hs + swiglu(rms_norm(hs, norm_ffn_even[e]), w1_ffn[e], w3_ffn[e], w2_ffn[e])
        else:
            o = layer // 2
            lb = lb_all[layer]
            y, s1, s2, cb = odd_mixer(rms_norm(hp, norm_mix_odd[o]), w_in_odd[o], w_out_odd[o], lb, hgrn_gain[o],
                                      conv_w[o], conv_b[o], dt_bias[o], a_log[o], d_skip[o], ssm_gain[o],
                                      jnp.zeros((bp, H_C, DK_C, DV_C), jnp.float32),
                                      jnp.zeros((bp, H_D, P_D, N_D), jnp.float32),
                                      jnp.zeros((bp, CONV_W - 1, CONV_DIM), hp.dtype), CHUNK)
            hp = hp + y
            hg_p.append(s1)
            ss_p.append(s2)
            cv_p.append(cb)
            y, s1, s2, cb = odd_mixer(rms_norm(hs, norm_mix_odd[o]), w_in_odd[o], w_out_odd[o], lb, hgrn_gain[o],
                                      conv_w[o], conv_b[o], dt_bias[o], a_log[o], d_skip[o], ssm_gain[o],
                                      state_hgrn[:, o], state_ssm[:, o], state_conv[:, o], ts)
            hs = hs + y
            hg_s.append(s1)
            ss_s.append(s2)
            cv_s.append(cb)
            hp = hp + moe_swiglu(rms_norm(hp, norm_ffn_odd[o]), w_router[o], we1[o], we3[o], we2[o])
            hs = hs + moe_swiglu(rms_norm(hs, norm_ffn_odd[o]), w_router[o], we1[o], we3[o], we2[o])
    y_prompt = rms_norm(hp, norm_final)
    y_sample = rms_norm(hs, norm_final)
    return (y_prompt, y_sample,
            jnp.stack(wk_p, axis=1), jnp.stack(wv_p, axis=1), jnp.stack(wk_s, axis=1), jnp.stack(wv_s, axis=1),
            jnp.stack(sk_p, axis=1), jnp.stack(sv_p, axis=1), jnp.stack(sk_s, axis=1), jnp.stack(sv_s, axis=1),
            jnp.stack(hg_p, axis=1), jnp.stack(hg_s, axis=1), jnp.stack(ss_p, axis=1), jnp.stack(ss_s, axis=1),
            jnp.stack(cv_p, axis=1), jnp.stack(cv_s, axis=1))


_drawn_inputs = setup_inputs


def setup_inputs(seed=0):
    import zlib

    import numpy as np

    out = dict(_drawn_inputs(seed))
    spreads = {}
    factors = {'sb_bias': 24.392,
     'hgrn_gain': 26.915,
     'd_skip': 147.717,
     'ssm_gain': 13.445,
     'norm_final': 22.995,
     'cache_sb_k': 8.0,
     'cache_sb_v': 8.0,
     'norm_mix_even': 2.855,
     'conv_b': 2.959,
     'norm_ffn_odd': 6.437}
    for name, (base, spread) in spreads.items():
        noise = np.random.default_rng([zlib.crc32(name.encode()), seed]).standard_normal(out[name].shape)
        drawn = base * np.exp(spread * noise) if base else spread * noise
        out[name] = jnp.asarray(drawn.astype(out[name].dtype))
    for name, factor in factors.items():
        out[name] = (out[name] * factor).astype(out[name].dtype)
    return out
```

```python
from contextlib import ExitStack

import concourse.bass as bass
import numpy as np
from concourse import mybir

F32 = mybir.dt.float32
I32 = mybir.dt.int32
ALU = mybir.AluOpType
ACT = mybir.ActivationFunctionType
AX = mybir.AxisListType.X

P = 128
D = 1024
DC = D // P
TP = 256
NB, NT = 8, 4
TS = NB * NT
T = TP + TS
TILES = ((0, P), (P, P), (TP, TS))
HD = 64
PAST = 256
PAGE = 128
SCALE = HD ** -0.5
NEG = -1.0e30
FF = 2816
FC = FF // P
HC = 4
HM = 16
NE = 8
FE = 3584
FEC = FE // P
EPS = 1e-6
WCOLS = 512
SLOT = DC * WCOLS
EARLY_SLOTS = 3
MOE_SLOTS = 7
MAX_ITEMS = NE + 2 * T // P
DIL_PATTERNS = ((128, 1), (512, 4), (2048, 16))

VEC = {"norm_mix_even": 0, "norm_ffn_even": 8, "norm_mix_odd": 16, "norm_ffn_odd": 24, "norm_final": 32,
       "hgrn_lb_logits": 40, "hgrn_gain": 48, "ssm_gain": 52, "conv_w": 60, "conv_b": 108}
NVEC = 120
CC = 12


def shape_constants():
    p = np.arange(P)
    c = {}
    c["ident"] = np.eye(P)
    c["ones"] = np.ones((P, P))
    run = np.ones(T)
    run[[0] + [TP + NT * b for b in range(NB)]] = 0
    c["running"] = np.tile(run, (P, 1))
    c["before"] = (p[:, None] < p[None, :]) * 1.0
    c["slots"] = np.tile(p, (P, 1))
    c["items"] = np.tile(np.arange(MAX_ITEMS + 1), (P, 1))
    c["valid"] = np.repeat(np.stack([p < n for _, n in TILES], 1), NE, 1) * 1.0
    e = np.arange(NE)
    c["earlier_expert"] = np.tile(((e[None, :] < e[:, None]) * 1.0).reshape(1, -1), (P, 1))
    c["expert_ids"] = np.tile(e, (P, 1))
    c["batch_of"] = (p[:, None] // NT == np.arange(NB)[None, :]) * 1.0
    pair = np.zeros((P, 8, P))
    for h in range(HM):
        pair[h, h // 2, 64 * (h % 2):64 * (h % 2) + 64] = 1
    c["head_pair"] = pair.reshape(P, -1)
    future = np.where(p[:, None] <= p[None, :], 0.0, NEG)
    c["ssd_future"] = np.concatenate([future, np.zeros((P, P))], 1)
    t = np.arange(TS)
    fs = np.full((P, TS), NEG)
    fs[:TS] = np.where((t[:, None] // NT == t[None, :] // NT) & (t[:, None] <= t[None, :]), 0.0, NEG)
    c["ssd_future_s"] = fs
    lv = []
    for l in range(7):
        h = 1 << l
        s, q = p[:, None], p[None, :]
        lv.append((s // (2 * h) == q // (2 * h)) & (s % (2 * h) < h) & (q % (2 * h) >= h))
    c["level"] = np.stack(lv, 1).reshape(P, -1)
    core = {k: np.asarray(v, np.float32) for k, v in c.items()}

    def log_count(dist):
        n = np.zeros(dist.shape)
        for window, dil in DIL_PATTERNS:
            n += (dist >= 0) & (dist <= window) & (dist % dil == 0)
        return np.where(n > 0, np.log(np.maximum(n, 1)), NEG)

    a = {}
    slope = 2.0 ** (-8.0 * np.arange(1, 9) / 8)
    d = p[:, None] + P - np.arange(2 * P)[None, :]
    lc = log_count(d)
    order = [0, 2, 1, 3, 4, 6, 5, 7]
    a["alibi"] = np.stack([np.where(lc > NEG, lc - slope[h] * d, NEG) for h in order], 1).reshape(P, -1)
    a["stick_on"] = (d > 0) * 1.0
    a["stick_off"] = np.where(d > 0, 0.0, NEG)
    key = np.arange(PAST + TS)
    al, on = [], []
    for g in range(2):
        b, h, t = 4 * g + p // 32, (p % 32) // NT, p % NT
        new = key >= PAST
        kb, kt = (key - PAST) // NT, (key - PAST) % NT
        pos = np.where(new, PAST + kt, key)
        dist = PAST + t[:, None] - pos[None, :]
        mine = ~new[None, :] | (kb[None, :] == b[:, None])
        lc = np.where(mine, log_count(dist), NEG)
        al.append(np.where(lc > NEG, lc - slope[h][:, None] * dist, NEG))
        on.append(mine & (dist > 0))
    a["alibi_s"] = np.concatenate(al, 1)
    a["stick_on_s"] = np.concatenate(on, 1) * 1.0
    a["stick_off_s"] = np.where(np.concatenate(on, 1), 0.0, NEG)
    rh = np.zeros((P, P))
    rh[(p % 32) // NT, p] = 1
    a["row_head"] = rh
    attn = {k: np.asarray(v, np.float32) for k, v in a.items()}
    return core, attn


def columns(tables):
    at, out = 0, {}
    for k, v in tables.items():
        out[k] = (at, at + v.shape[1])
        at += v.shape[1]
    return out, at


class Count:

    def __init__(self, sem):
        self.sem, self.total, self.base = sem, 0, 0

    def up(self, by=1):
        self.total += by
        return self.sem, by

    def at(self, n):
        assert self.base + n > 0
        return self.sem, self.base + n

    def all(self):
        return self.sem, self.total


class Kernel:

    def __init__(self, nc, ctx, ins, outs, core, attn):
        self.nc, self.ins, self.outs = nc, ins, outs
        self.ctx = ctx
        self.counts = {}
        self.core_at, self.core_n = columns(core)
        self.attn_at, self.attn_n = columns(attn)
        self.ps = ctx.enter_context(nc.psum_tensor("ps", [P, 8, 512], F32))
        self.residual = self.sb(ctx, "residual", [P, DC, T])
        self.act = self.sb(ctx, "act", [P, DC, T])
        self.core = self.sb(ctx, "core", [P, self.core_n])
        self.vec = self.sb(ctx, "vec", [P, NVEC])
        self.ones_wide = self.sb(ctx, "ones_wide", [P, T])
        self.blocks = self.weight_blocks()
        self.issued, self.landed, self.freed = 0, {}, {}

    def sb(self, ctx, name, shape, dt=F32):
        return ctx.enter_context(self.nc.sbuf_tensor(name, shape, dt))

    def count(self, name):
        if name not in self.counts:
            self.counts[name] = Count(self.ctx.enter_context(self.nc.semaphore(name)))
        return self.counts[name]

    def stage(self):
        for c in self.counts.values():
            c.base = c.total
        return self.nc.Block()

    def const(self, name):
        a, b = self.core_at[name]
        return self.core[:, a:b]

    def table(self, name):
        a, b = self.attn_at[name]
        return self.attn[:, a:b]

    def weight_blocks(self):
        i = self.ins
        cols = lambda w, a, n: (w[0].rearrange("(k p) n -> p k n", p=P)[:, :, a:a + n], "cols", n)
        rows = lambda w, a, n: (w[0].rearrange("(k p) n -> p k n", p=P)[:, a:a + n, :], "rows", n)
        blocks = [cols(i["w_in_even"], WCOLS * n, WCOLS) for n in range(6)]
        blocks += [cols(i["w_out_even"], WCOLS * n, WCOLS) for n in range(2)]
        for n in range(FF // 256):
            blocks.append((n, "pair", 256))
        blocks += [rows(i["w2_ffn"], 4 * n, min(4, FC - 4 * n)) for n in range(-(-FC // 4))]
        blocks += [cols(i["w_in_odd"], WCOLS * n, min(WCOLS, 4624 - WCOLS * n)) for n in range(10)]
        blocks += [rows(i["w_out_odd"], 4 * n, 4) for n in range(3)]
        return blocks

    def slot(self, n, how, width):
        flat = self.ring[:, n % EARLY_SLOTS, :]
        if how == "cols":
            return flat[:, 0:DC * width].rearrange("p (k n) -> p k n", k=DC)
        if how == "rows":
            return flat[:, 0:width * D].rearrange("p (k n) -> p k n", k=width)
        return flat.rearrange("p (k w n) -> p k w n", k=DC, w=2)

    def stream(self, sp, upto):
        for n in range(self.issued, min(upto, len(self.blocks))):
            src, how, width = self.blocks[n]
            if n >= EARLY_SLOTS:
                sp.wait_ge(*self.freed[n - EARLY_SLOTS])
            loaded = self.count(f"block_loaded{n % EARLY_SLOTS}")
            dst = self.slot(n, how, width)
            if how == "pair":
                for w, name in enumerate(("w1_ffn", "w3_ffn")):
                    part = self.ins[name][0].rearrange("(k p) n -> p k n", p=P)[:, :, 256 * src:256 * src + 256]
                    sp.dma_start(dst[:, :, w, :], part).then_inc(*loaded.up(16))
            else:
                sp.dma_start(dst, src).then_inc(*loaded.up(16))
            self.landed[n] = loaded.sem, loaded.total
            self.issued = n + 1

    def arrived(self, n):
        return self.landed[n]


def stage_load(k):
    nc, ins = k.nc, k.ins
    with ExitStack() as s:
        tok = k.sb(s, "tok", [P, 3, D])
        rows = k.sb(s, "rows", [P, P])
        const_in, vec_in, x_in = k.count("const_in"), k.count("vec_in"), k.count("x_in")
        turned, copied = k.count("turned"), k.count("copied")
        with k.stage() as block:
            @block.sync
            def _(sp):
                sp.dma_start(k.core[:, :], ins["core_tables"]).then_inc(*const_in.up(16))
                k.stream(sp, EARLY_SLOTS)

            @block.gpsimd
            def _(pool):
                pool.dma_start(tok[:, 0:2, :], ins["x_prompt"][0].rearrange("(t p) d -> p t d", p=P)).then_inc(*x_in.up(16))
                pool.dma_start(tok[0:TS, 2, :], ins["x_sample"].rearrange("b t d -> (b t) d")).then_inc(*x_in.up(16))
                for name in ("norm_mix_even", "norm_ffn_even", "norm_mix_odd", "norm_ffn_odd", "norm_final",
                             "hgrn_lb_logits", "hgrn_gain", "ssm_gain", "conv_w", "conv_b"):
                    v = ins[name]
                    n = int(np.prod(v.shape)) // P
                    if name == "norm_final":
                        src = v.rearrange("(c q) -> c q", q=P)
                    elif name == "conv_w":
                        src = v[0].rearrange("j (c q) -> (j c) q", q=P)
                    else:
                        src = v.rearrange("a (c q) -> (a c) q", q=P)
                    pool.dma_start(rows[VEC[name]:VEC[name] + n, :], src).then_inc(*vec_in.up(16))

            @block.tensor
            def _(pe):
                pe.wait_ge(*const_in.at(16))
                ident = k.const("ident")
                pe.wait_ge(*x_in.at(32))
                for c in range(DC):
                    if c >= 4:
                        pe.wait_ge(*copied.at(c - 3))
                    for i, (a, n) in enumerate(TILES):
                        mm = pe.transpose(k.ps[:, c % 4, a:a + n], tok[0:n, i, P * c:P * c + P], ident[0:n, 0:n])
                    mm.then_inc(*turned.up())
                pe.wait_ge(*vec_in.at(160))
                pe.transpose(k.ps[:, 4, 0:NVEC], rows[0:NVEC, :], ident[0:NVEC, 0:NVEC]).then_inc(*turned.up())

            @block.vector
            def _(dve):
                dve.memset(k.ones_wide[:, :], 1.0).then_inc(*k.count("ones_set").up())
                for c in range(DC):
                    dve.wait_ge(*turned.at(c + 1))
                    dve.tensor_copy(k.residual[:, c, :], k.ps[:, c % 4, 0:T]).then_inc(*copied.up())
                dve.wait_ge(*turned.at(DC + 1))
                dve.tensor_copy(k.vec[:, :], k.ps[:, 4, 0:NVEC]).then_inc(*copied.up())


def stage_norm(k, gain):
    with ExitStack() as s:
        sq = k.sb(s, f"sq_{gain}", [P, DC, T])
        rstd = k.sb(s, f"rstd_{gain}", [P, T])
        squared, summed, mean, root = (k.count(n) for n in ("squared", "summed", "mean", "root"))
        normed = k.count("normed")
        with k.stage() as block:
            @block.scalar
            def _(act):
                for c in range(DC):
                    act.activation(sq[:, c, :], k.residual[:, c, :], ACT.Square).then_inc(*squared.up())
                act.wait_ge(*mean.at(1))
                act.activation(rstd[:, :], rstd[:, :], ACT.Ln).then_inc(*root.up())
                act.wait_ge(*root.at(1))
                act.activation(rstd[:, :], rstd[:, :], ACT.Exp, scale=-0.5).then_inc(*root.up())

            @block.tensor
            def _(pe):
                for c in range(DC):
                    pe.wait_ge(*squared.at(c + 1))
                    mm = pe.matmul(k.ps[:, 0, 0:T], k.const("ones"), sq[:, c, :], start=c == 0, stop=c == DC - 1)
                mm.then_inc(*summed.up())

            @block.vector
            def _(dve):
                dve.wait_ge(*summed.at(1))
                dve.tensor_scalar(rstd[:, :], k.ps[:, 0, 0:T], 1.0 / D, EPS, ALU.mult, ALU.add).then_inc(*mean.up())
                dve.wait_ge(*root.at(2))
                for c in range(DC):
                    g = VEC[gain] + c
                    dve.scalar_tensor_tensor(k.act[:, c, :], k.residual[:, c, :], k.vec[:, g:g + 1], rstd[:, :],
                                             ALU.mult, ALU.mult).then_inc(*normed.up())


def gemm(k, first, widths, copy_out, by_vector=False):
    done, out = k.count("product_done"), (k.count("even_out"), k.count("odd_out"))
    chunks = [(first + n, j, w) for n, w in enumerate(widths) for j in range(-(-w // P))]
    with k.stage() as block:
        for m, (n, j, w) in enumerate(chunks):
            k.freed[n] = done.at(m + 1)

        @block.sync
        def _(sp):
            k.stream(sp, first + len(widths) + EARLY_SLOTS)

        @block.tensor
        def _(pe):
            for m, (n, j, width) in enumerate(chunks):
                w = min(P, width - P * j)
                if j == 0:
                    pe.wait_ge(*k.arrived(n))
                if m >= 8:
                    pe.wait_ge(*out[m % 2].at(m // 2 - 3))
                slot = k.slot(n, "cols", width)
                for c in range(DC):
                    mm = pe.matmul(k.ps[0:w, m % 8, 0:T], slot[:, c, P * j:P * j + w], k.act[:, c, :],
                                   start=c == 0, stop=c == DC - 1)
                mm.then_inc(*done.up())

        @block.scalar
        def _(act):
            for m in range(0, 0 if by_vector else len(chunks), 2):
                act.wait_ge(*done.at(m + 1))
                copy_out(act, m).then_inc(*out[0].up())

        @block.vector
        def _(dve):
            for m in range(0 if by_vector else 1, len(chunks), 1 if by_vector else 2):
                dve.wait_ge(*done.at(m + 1))
                copy_out(dve, m).then_inc(*out[m % 2].up())


def gemm_rows(k, first, total, source):
    block_done, added = k.count("row_block_done"), k.count("residual_added")
    nblocks = -(-total // 4)
    with k.stage() as block:
        for n in range(nblocks):
            k.freed[first + n] = block_done.at(n + 1)

        @block.sync
        def _(sp):
            k.stream(sp, first + nblocks + EARLY_SLOTS)

        @block.tensor
        def _(pe):
            for n in range(nblocks):
                width = min(4, total - 4 * n)
                pe.wait_ge(*k.arrived(first + n))
                slot = k.slot(first + n, "rows", width)
                for j in range(width):
                    c = 4 * n + j
                    for m in range(DC):
                        mm = pe.matmul(k.ps[:, m, 0:T], slot[:, j, P * m:P * m + P], source[:, c, :],
                                       start=c == 0, stop=c == total - 1)
                mm.then_inc(*block_done.up())

        @block.vector
        def _(dve):
            dve.wait_ge(*block_done.at(nblocks))
            for m in range(DC):
                dve.tensor_tensor(k.residual[:, m, :], k.residual[:, m, :], k.ps[:, m, 0:T],
                                  ALU.add).then_inc(*added.up())


def copy(eng, out, in_):
    return eng.copy(out, in_) if eng.engine == mybir.EngineType.Activation else eng.tensor_copy(out, in_)



def stage_qkv(k, qkv):
    def copy_out(eng, m):
        return copy(eng, qkv[:, m, :], k.ps[:, m % 8, 0:T])
    gemm(k, 0, [WCOLS] * 6, copy_out)


def stage_kv_tokens(k, qkv, kv):
    ins, outs = k.ins, k.outs
    jobs = []
    for i, (a, n) in enumerate(TILES):
        for c0 in range(0, 16, 4):
            parts = [(qkv[:, 8 + c0 + c, a:a + n], None) for c in range(4)]
            jobs.append((i, n, c0, parts))
    turned, copied = k.count("turned"), (k.count("copied"), k.count("copied_odd"))
    stored = k.count("stored")
    with k.stage() as block:
        @block.sync
        def _(sp):
            sp.dma_start(k.attn[:, :], ins["attn_tables"]).then_inc(*k.count("tables_in").up(16))
            sp.wait_ge(*k.count("tables_in").at(16))

        @block.tensor
        def _(pe):
            for j, (i, n, c0, parts) in enumerate(jobs):
                if j >= 8:
                    pe.wait_ge(*copied[j % 2].at((j - 8) // 2 + 1))
                for c, (in_, _) in enumerate(parts):
                    mm = pe.transpose(k.ps[0:n, j % 8, P * c:P * c + P], in_, k.const("ident"))
                mm.then_inc(*turned.up())

        def copier(eng, odd):
            for j, (i, n, c0, parts) in enumerate(jobs):
                if j % 2 == odd:
                    eng.wait_ge(*turned.at(j + 1))
                    copy(eng, kv[0:n, i, P * c0:P * c0 + 4 * P], k.ps[0:n, j % 8, :]).then_inc(*copied[odd].up())

        @block.scalar
        def _(act):
            copier(act, 0)

        @block.vector
        def _(dve):
            copier(dve, 1)

        @block.gpsimd
        def _(pool):
            pool.wait_ge(*copied[0].at(len(jobs) // 2))
            pool.wait_ge(*copied[1].at(len(jobs) // 2))
            for n, (out_p, out_s, col) in enumerate(((2, 4, 0), (3, 5, 1024), (6, 8, 512), (7, 9, 1536))):
                pool.dma_start(outs[out_p][0, 0].rearrange("(i p) h d -> p i (h d)", p=P),
                               kv[:, 0:2, col:col + 512]).then_inc(*stored.up(16))
                pool.dma_start(outs[out_s].rearrange("b a t h d -> (b a t) (h d)"),
                               kv[0:TS, 2, col:col + 512]).then_inc(*stored.up(16))
            pool.wait_ge(*stored.all())


def stage_prompt_attention(k, mixer, qkv, kv):
    A = mixer == "A"
    off = 0 if A else 4
    steps = [(t, g) for t in range(2) for g in range(2)]
    with ExitStack() as s:
        z = k.sb(s, f"z{mixer}", [P, 4, 2 * P])
        prob = k.sb(s, f"prob{mixer}", [P, 4, 2 * P])
        probT = k.sb(s, f"probT{mixer}", [P, 2, 4, P])
        stat = k.sb(s, f"stat{mixer}", [P, 12])
        if not A:
            soft = k.sb(s, "soft", [P, 4, 2 * P])
            run = k.sb(s, "run", [P, 4, 2 * P])
            bias = k.sb(s, "stick_bias", [P, 8])
            bias_in = k.count("bias_in")
        scored, taken, peaked, exped, weighed, turned, copied, mixed, out = (k.count(n) for n in (
            "scored", "scores_taken", "peaked", "exped", "weighed", "turned", "copied", "mixed", "mixed_out"))
        z_ready, softened, shifted = (k.count(n) for n in ("z_ready", "softened", "shifted"))
        act_step, dve_step = k.count("act_step"), k.count("dve_step")
        with k.stage() as block:
            if not A:
                @block.gpsimd
                def _(pool):
                    pool.dma_start(bias[:, :], k.ins["sb_bias"].broadcast_to([P, 8])).then_inc(*bias_in.up(16))

            @block.tensor
            def _(pe):
                def scores(i):
                    t, g = steps[i]
                    if i >= 2:
                        pe.wait_ge(*taken.at(i - 1))
                    for j in range(4):
                        c, r = off + 2 * g + j % 2, HD * (j // 2)
                        mm = pe.matmul(k.ps[:, 2 * (i % 2) + j // 2, 256 * (j % 2):256 * (j % 2) + P * (t + 1)],
                                       qkv[r:r + HD, c, P * t:P * t + P], qkv[r:r + HD, 8 + c, 0:P * (t + 1)],
                                       start=True, stop=True)
                    mm.then_inc(*scored.up())

                scores(0)
                for i, (t, g) in enumerate(steps):
                    if i + 1 < len(steps):
                        scores(i + 1)
                    pe.wait_ge(*weighed.at(i + 1))
                    for kt in range(t + 1):
                        for j in range(4):
                            mm = pe.transpose(k.ps[:, 4 + kt, P * j:P * j + P], prob[:, j, P * kt:P * kt + P],
                                              k.const("ident"))
                    mm.then_inc(*turned.up())
                    pe.wait_ge(*copied.at(i + 1))
                    if i >= 2:
                        pe.wait_ge(*out.at(i - 1))
                    for j in range(4):
                        h, r = 2 * (off + 2 * g + j % 2) + j // 2, HD * (j // 2)
                        for kt in range(t + 1):
                            mm = pe.matmul(k.ps[r:r + HD, 6 + i % 2, P * (j % 2):P * (j % 2) + P],
                                           kv[:, kt, 1024 + HD * h:1024 + HD * h + HD], probT[:, kt, j, :],
                                           start=kt == 0, stop=kt == t)
                    mm.then_inc(*mixed.up())

            @block.vector
            def _(dve):
                def then(ins, sig=dve_step):
                    ins.then_inc(*sig.up())
                    dve.wait_ge(*sig.all())

                for i, (t, g) in enumerate(steps):
                    W, x0 = P * (t + 1), P * (1 - t)
                    zz, pp = z[:, :, 0:W], prob[:, :, 0:W]
                    raw = k.ps[:, 2 * (i % 2):2 * (i % 2) + 2, :].rearrange("p a (b n) -> p (a b) n", b=2)[:, :, 0:W]
                    dve.wait_ge(*scored.at(i + 1))
                    if A:
                        tab = k.table("alibi").rearrange("p (h n) -> p h n", h=8)[:, 4 * g:4 * g + 4, x0:2 * P]
                        then(dve.scalar_tensor_tensor(zz, raw, SCALE, tab, ALU.mult, ALU.add), taken)
                        dve.tensor_reduce(stat[:, 0:4], zz, AX, ALU.max, negate=True).then_inc(*peaked.up())
                        dve.wait_ge(*exped.at(i + 1))
                        then(dve.reciprocal(stat[:, 8:12], stat[:, 4:8]))
                        dve.tensor_tensor(pp, pp, stat[:, 8:12].unsqueeze(2).broadcast_to([P, 4, W]),
                                          ALU.mult).then_inc(*weighed.up())
                    else:
                        if i == 0:
                            dve.wait_ge(*bias_in.at(16))
                        else:
                            dve.wait_ge(*weighed.at(i))
                        ss = soft[:, :, 0:W]
                        on = k.table("stick_on")[:, x0:2 * P].unsqueeze(1).broadcast_to([P, 4, W])
                        offm = k.table("stick_off")[:, x0:2 * P].unsqueeze(1).broadcast_to([P, 4, W])
                        b = bias[:, 4 * g:4 * g + 4].rearrange("p (q a) -> p a q", a=2).unsqueeze(3).broadcast_to([P, 2, 2, W])
                        z4 = z[:, :, :].rearrange("p (a q) n -> p a q n", a=2)[:, :, :, 0:W]
                        then(dve.tensor_scalar(zz, raw, SCALE, None, ALU.mult), taken)
                        dve.tensor_tensor(z4, z4, b, ALU.add).then_inc(*z_ready.up())
                        dve.wait_ge(*softened.at(i + 1))
                        then(dve.scalar_tensor_tensor(ss, zz, 0.0, ss, ALU.max, ALU.add))
                        then(dve.tensor_tensor(ss, ss, on, ALU.mult))
                        for j in range(4):
                            then(dve.tensor_tensor_scan(run[:, j, 0:W][:, ::-1], k.ones_wide[:, 0:W],
                                                        soft[:, j, 0:W][:, ::-1], 0.0, ALU.mult, ALU.add))
                        then(dve.tensor_tensor(zz, zz, run[:, :, 0:W], ALU.subtract))
                        dve.tensor_tensor(zz, zz, offm, ALU.add).then_inc(*shifted.up())
                    dve.wait_ge(*turned.at(i + 1))
                    if t:
                        then(dve.tensor_copy(probT[:, 1, :, :], k.ps[:, 5, :].rearrange("p (h n) -> p h n", h=4)))
                    dve.tensor_copy(probT[:, 0, :, :], k.ps[:, 4, :].rearrange("p (h n) -> p h n", h=4)).then_inc(*copied.up())
                    dve.wait_ge(*mixed.at(i + 1))
                    dve.tensor_copy(k.act[:, off + 2 * g:off + 2 * g + 2, P * t:P * t + P],
                                    k.ps[:, 6 + i % 2, 0:2 * P].rearrange("p (c n) -> p c n", c=2)).then_inc(*out.up())

            @block.scalar
            def _(act):
                def then(ins, sig=act_step):
                    ins.then_inc(*sig.up())
                    act.wait_ge(*sig.all())

                for i, (t, g) in enumerate(steps):
                    W = P * (t + 1)
                    if A:
                        act.wait_ge(*peaked.at(i + 1))
                        if i >= 1:
                            act.wait_ge(*turned.at(i))
                        for j in range(4):
                            ins = act.activation(prob[:, j, 0:W], z[:, j, 0:W], ACT.Exp, bias=stat[:, j:j + 1],
                                                 accum_out=stat[:, 4 + j:5 + j])
                        ins.then_inc(*exped.up())
                    else:
                        act.wait_ge(*z_ready.at(i + 1))
                        then(act.activation(soft[:, :, 0:W], z[:, :, 0:W], ACT.Abs))
                        then(act.activation(soft[:, :, 0:W], soft[:, :, 0:W], ACT.Exp, scale=-1.0))
                        act.activation(soft[:, :, 0:W], soft[:, :, 0:W], ACT.Ln, bias=1.0).then_inc(*softened.up())
                        act.wait_ge(*shifted.at(i + 1))
                        if i >= 1:
                            act.wait_ge(*turned.at(i))
                        act.activation(prob[:, :, 0:W], z[:, :, 0:W], ACT.Exp).then_inc(*weighed.up())


def stage_sample_attention(k, mixer, group, qkv, kv):
    A = mixer == "A"
    off = 0 if A else 4
    W = PAST + TS
    with ExitStack() as s:
        tag = f"{mixer}{group}"
        keys = k.sb(s, "keys" + tag, [P, 4, 2, 4 * P])
        vals = k.sb(s, "vals" + tag, [P, 4, 2, 4 * P])
        keysT = k.sb(s, "keysT" + tag, [P, 2, 4, PAST])
        qbd = k.sb(s, "qbd" + tag, [P, 4, 4, 32])
        z = k.sb(s, "zs" + tag, [P, W])
        prob = k.sb(s, "probs" + tag, [P, W])
        probT = k.sb(s, "probTs" + tag, [P, 3, P])
        stat = k.sb(s, "stats" + tag, [P, 4])
        keys_in, vals_in, pages_in, bias_in = (k.count(n) for n in ("keys_in", "vals_in", "pages_in", "row_bias_in"))
        placed, scored, peaked, exped, weighed, turned, copied, mixed, out = (k.count(n) for n in (
            "placed", "scored", "peaked", "exped", "weighed", "turned", "copied", "mixed", "mixed_out"))
        keys_turned, keys_copied = k.count("keys_turned"), (k.count("keys_copied_act"), k.count("keys_copied_dve"))
        z_ready, softened, shifted, zeroed = (k.count(n) for n in ("z_ready", "softened", "shifted", "zeroed"))
        act_step, dve_step = k.count("act_step"), k.count("dve_step")
        if not A:
            soft = k.sb(s, "softs" + tag, [P, W])
            run = k.sb(s, "runs" + tag, [P, W])
            bias8 = k.sb(s, "bias8" + tag, [8, 1])
            pages = k.sb(s, "pages" + tag, [1, NB * 2], I32)
            biased = k.count("row_bias")
        with k.stage() as block:
            @block.sync
            def _(sp):
                if A:
                    for name, dst, landed in (("cache_win_k", keys, keys_in), ("cache_win_v", vals, vals_in)):
                        for b in range(4):
                            sp.dma_start(dst[:, b, :, :], k.ins[name][4 * group + b, 0].rearrange(
                                "(j p) h d -> p j (h d)", p=P)).then_inc(*landed.up(16))
                else:
                    sp.dma_start(pages[:, :], k.ins["page_table"].rearrange("b j -> (b j)").unsqueeze(0)).then_inc(*pages_in.up(16))
                    sp.dma_start(bias8[:, :], k.ins["sb_bias"].rearrange("a h -> h a")).then_inc(*bias_in.up(16))
                    sp.wait_ge(*pages_in.at(16))
                    at = [sp.value_load(pages[0:1, n:n + 1], min_val=0, max_val=k.ins["cache_sb_k"].shape[0] - 1)
                          for n in range(8 * group, 8 * group + 8)]
                    for name, dst, landed in (("cache_sb_k", keys, keys_in), ("cache_sb_v", vals, vals_in)):
                        for n in range(8):
                            page = k.ins[name][bass.ds(at[n], 1), 0].rearrange("a p h d -> p (a h d)")
                            sp.dma_start(dst[:, n // 2, n % 2, :], page).then_inc(*landed.up(16))

            @block.tensor
            def _(pe):
                ident = k.const("ident")
                if not A:
                    pe.wait_ge(*bias_in.at(16))
                    pe.matmul(k.ps[:, 7, 0:1], k.table("row_head")[0:8, :], bias8[:, :], start=True, stop=True).then_inc(*biased.up())
                pe.wait_ge(*keys_in.all())
                pe.wait_ge(*placed.at(2))

                def turn_keys(b):
                    for u in range(2):
                        if b >= 2:
                            pe.wait_ge(*keys_copied[u].at(b - 1))
                        for j in range(2):
                            for c in range(2):
                                mm = pe.transpose(k.ps[:, 2 * (b % 2) + u, PAST * c + P * j:PAST * c + P * j + P],
                                                  keys[:, b, j, P * (2 * u + c):P * (2 * u + c) + P], ident)
                        mm.then_inc(*keys_turned.up())

                turn_keys(0)
                for b in range(4):
                    if b < 3:
                        turn_keys(b + 1)
                    for u in range(2):
                        pe.wait_ge(*keys_copied[u].at(b + 1))
                    for part in range(2):
                        for c in range(4):
                            rhs = keysT[:, b % 2, c, :] if part == 0 else qkv[:, 8 + off + c, TP:T]
                            mm = pe.matmul(k.ps[32 * b:32 * b + 32, 4, PAST * part:PAST * part + rhs.shape[1]],
                                           qbd[:, c, b, :], rhs, start=c == 0, stop=c == 3)
                    mm.then_inc(*scored.up())
                pe.wait_ge(*weighed.at(1))
                for j, (a, n) in enumerate(TILES):
                    mm = pe.transpose(k.ps[0:n, 5, P * j:P * j + P], prob[:, a:a + n], ident)
                mm.then_inc(*turned.up())
                pe.wait_ge(*vals_in.all())
                pe.wait_ge(*copied.at(1))
                for b in range(4):
                    for c in range(4):
                        for j in range(3):
                            lhs = vals[:, b, j, P * c:P * c + P] if j < 2 else \
                                kv[0:TS, 2, 1024 + P * (off + c):1024 + P * (off + c) + P]
                            rhs = probT[0:TILES[j][1], j, 32 * b + 8 * c:32 * b + 8 * c + 8]
                            mm = pe.matmul(k.ps[:, 6, 32 * c + 8 * b:32 * c + 8 * b + 8], lhs, rhs,
                                           start=j == 0, stop=j == 2)
                mm.then_inc(*mixed.up())

            @block.vector
            def _(dve):
                def then(ins, sig=dve_step):
                    ins.then_inc(*sig.up())
                    dve.wait_ge(*sig.all())

                then(dve.memset(qbd[:, :, :, :], 0.0), zeroed)
                for r in range(2):
                    for c in range(4):
                        dst = qbd[HD * r:HD * r + HD, c, :, 4 * (2 * c + r):4 * (2 * c + r) + 4]
                        src = qkv[HD * r:HD * r + HD, off + c, TP + 16 * group:TP + 16 * group + 16]
                        ins = dve.tensor_copy(dst, src.rearrange("p (b t) -> p b t", t=NT))
                    ins.then_inc(*placed.up())
                for b in range(4):
                    dve.wait_ge(*keys_turned.at(2 * b + 2))
                    if b >= 2:
                        dve.wait_ge(*scored.at(b - 1))
                    dve.tensor_copy(keysT[:, b % 2, 2:4, :], k.ps[:, 2 * (b % 2) + 1, :].rearrange("p (c n) -> p c n", c=2))\
                       .then_inc(*keys_copied[1].up())
                dve.wait_ge(*scored.at(4))
                raw = k.ps[:, 4, 0:W]
                part = lambda name: k.table(name)[:, W * group:W * group + W]
                if A:
                    then(dve.scalar_tensor_tensor(z[:, :], raw, SCALE, part("alibi_s"), ALU.mult, ALU.add))
                    dve.tensor_reduce(stat[:, 0:1], z[:, :], AX, ALU.max, negate=True).then_inc(*peaked.up())
                    dve.wait_ge(*exped.at(1))
                    then(dve.reciprocal(stat[:, 2:3], stat[:, 1:2]))
                    dve.tensor_scalar(prob[:, :], prob[:, :], stat[:, 2:3], None, ALU.mult).then_inc(*weighed.up())
                else:
                    dve.wait_ge(*biased.at(1))
                    then(dve.tensor_copy(stat[:, 3:4], k.ps[:, 7, 0:1]))
                    dve.tensor_scalar(z[:, :], raw, SCALE, stat[:, 3:4], ALU.mult, ALU.add).then_inc(*z_ready.up())
                    dve.wait_ge(*softened.at(1))
                    then(dve.scalar_tensor_tensor(soft[:, :], z[:, :], 0.0, soft[:, :], ALU.max, ALU.add))
                    then(dve.tensor_tensor(soft[:, :], soft[:, :], part("stick_on_s"), ALU.mult))
                    then(dve.tensor_tensor_scan(run[:, ::-1], k.ones_wide[:, :], soft[:, ::-1], 0.0, ALU.mult, ALU.add))
                    then(dve.tensor_tensor(z[:, :], z[:, :], run[:, :], ALU.subtract))
                    dve.tensor_tensor(z[:, :], z[:, :], part("stick_off_s"), ALU.add).then_inc(*shifted.up())
                dve.wait_ge(*turned.at(1))
                then(dve.tensor_copy(probT[:, 0:2, :], k.ps[:, 5, 0:2 * P].rearrange("p (j n) -> p j n", j=2)))
                dve.tensor_copy(probT[0:TS, 2, :], k.ps[0:TS, 5, 2 * P:3 * P]).then_inc(*copied.up())
                dve.wait_ge(*mixed.at(1))
                for r in range(2):
                    src = k.ps[HD * r:HD * r + HD, 6, 0:P].rearrange("p (c b u t) -> p c b u t", c=4, b=4, u=2)[:, :, :, r, :]
                    dst = k.act[HD * r:HD * r + HD, off:off + 4, TP + 16 * group:TP + 16 * group + 16]
                    dve.tensor_copy(dst.rearrange("p c (b t) -> p c b t", t=NT), src).then_inc(*out.up())

            @block.scalar
            def _(act):
                for b in range(4):
                    act.wait_ge(*keys_turned.at(2 * b + 1))
                    if b >= 2:
                        act.wait_ge(*scored.at(b - 1))
                    act.copy(keysT[:, b % 2, 0:2, :], k.ps[:, 2 * (b % 2), :].rearrange("p (c n) -> p c n", c=2))\
                       .then_inc(*keys_copied[0].up())
                if A:
                    act.wait_ge(*peaked.at(1))
                    act.activation(prob[:, :], z[:, :], ACT.Exp, bias=stat[:, 0:1], accum_out=stat[:, 1:2]).then_inc(*exped.up())
                else:
                    act.wait_ge(*z_ready.at(1))
                    act.activation(soft[:, :], z[:, :], ACT.Abs).then_inc(*act_step.up())
                    act.wait_ge(*act_step.all())
                    act.activation(soft[:, :], soft[:, :], ACT.Exp, scale=-1.0).then_inc(*act_step.up())
                    act.wait_ge(*act_step.all())
                    act.activation(soft[:, :], soft[:, :], ACT.Ln, bias=1.0).then_inc(*softened.up())
                    act.wait_ge(*shifted.at(1))
                    act.activation(prob[:, :], z[:, :], ACT.Exp).then_inc(*weighed.up())


def stage_out_even(k):
    def copy_out(eng, m):
        return eng.tensor_tensor(k.residual[:, m, :], k.residual[:, m, :], k.ps[:, m, 0:T], ALU.add)
    gemm(k, 6, [WCOLS] * 2, copy_out, by_vector=True)



def stage_ffn_up(k, hidden):
    first = 8
    pair_done, gated, taken = k.count("pair_done"), k.count("gated"), k.count("pair_taken")
    with ExitStack() as s:
        gate = [k.sb(s, f"gate{n}", [P, T]) for n in range(2)]
        with k.stage() as block:
            for m in range(FC):
                k.freed[first + m // 2] = pair_done.at(m + 1)

            @block.sync
            def _(sp):
                k.stream(sp, first + FC // 2 + EARLY_SLOTS)

            @block.tensor
            def _(pe):
                for m in range(FC):
                    if m % 2 == 0:
                        pe.wait_ge(*k.arrived(first + m // 2))
                    if m >= 4:
                        pe.wait_ge(*taken.at(m - 3))
                    slot = k.slot(first + m // 2, "pair", 256)
                    for w in range(2):
                        for c in range(DC):
                            mm = pe.matmul(k.ps[:, 2 * (m % 4) + w, 0:T], slot[:, c, w, P * (m % 2):P * (m % 2) + P],
                                           k.act[:, c, :], start=c == 0, stop=c == DC - 1)
                    mm.then_inc(*pair_done.up())

            @block.scalar
            def _(act):
                for m in range(FC):
                    act.wait_ge(*pair_done.at(m + 1))
                    if m >= 2:
                        act.wait_ge(*taken.at(m - 1))
                    act.activation(gate[m % 2][:, :], k.ps[:, 2 * (m % 4), 0:T], ACT.Silu).then_inc(*gated.up())

            @block.vector
            def _(dve):
                for m in range(FC):
                    dve.wait_ge(*gated.at(m + 1))
                    dve.tensor_tensor(hidden[:, m, :], gate[m % 2][:, :], k.ps[:, 2 * (m % 4) + 1, 0:T],
                                      ALU.mult).then_inc(*taken.up())



Q, F_, V, G, Z, X, DT = 0, 4, 8, 12, 16, 24, 36


def stage_in_odd(k, proj, conv_in, conv_in_s, dt):
    first = 25
    widths = [WCOLS] * 9 + [HM]
    done, out = k.count("product_done"), (k.count("even_out"), k.count("odd_out"))
    chunks = [(first + n, j, w) for n, w in enumerate(widths) for j in range(-(-w // P))]
    silus = set(range(Q, Q + 4)) | set(range(G, G + 4)) | set(range(Z, Z + 8))
    on_act = [m for m in range(37) if m in silus or m % 4 == 1 and m < 36]
    on_dve = [m for m in range(37) if m not in on_act]
    past_in, past_turned = k.count("past_in"), k.count("past_turned")
    past = k.count("past_placed")
    with ExitStack() as s:
        old = k.sb(s, "old_conv", [NB * 3, CC * P])
        with k.stage() as block:
            for m, (n, j, w) in enumerate(chunks):
                k.freed[n] = done.at(m + 1)

            def place(m):
                return out[0].at(on_act.index(m) + 1) if m in on_act else out[1].at(on_dve.index(m) + 1)

            @block.sync
            def _(sp):
                k.stream(sp, first + len(widths) + EARLY_SLOTS)

            @block.gpsimd
            def _(pool):
                pool.dma_start(old[:, :], k.ins["state_conv"].rearrange("b a r c -> (b a r) c")).then_inc(*past_in.up(16))
                pool.memset(conv_in[:, :, 0:3], 0.0).then_inc(*k.count("past_zeroed").up())

            @block.tensor
            def _(pe):
                pe.wait_ge(*past_in.at(16))
                for c in range(CC):
                    mm = pe.transpose(k.ps[:, 7, 24 * c:24 * c + 24], old[:, P * c:P * c + P], k.const("ident")[0:24, 0:24])
                mm.then_inc(*past_turned.up())
                for m, (n, j, width) in enumerate(chunks):
                    w = min(P, width - P * j)
                    if j == 0:
                        pe.wait_ge(*k.arrived(n))
                    if m >= 7:
                        pe.wait_ge(*place(m - 7))
                    slot = k.slot(n, "cols", width)
                    for c in range(DC):
                        mm = pe.matmul(k.ps[0:w, m % 7, 0:T], slot[:, c, P * j:P * j + w], k.act[:, c, :],
                                       start=c == 0, stop=c == DC - 1)
                    mm.then_inc(*done.up())

            def leave(eng, m):
                bank = k.ps[:, m % 7, :]
                if m in silus:
                    dst = proj[:, m, :]
                    return eng.activation(dst, bank[:, 0:T], ACT.Silu)
                if m < X:
                    return copy(eng, proj[:, m, :], bank[:, 0:T])
                if m < DT:
                    copy(eng, conv_in_s[:, m - X, :, 3:3 + NT], bank[:, TP:T].rearrange("p (b t) -> p b t", t=NT))\
                        .then_inc(*k.count("new_placed").up())
                    return copy(eng, conv_in[:, m - X, 3:3 + TP], bank[:, 0:TP])
                return copy(eng, dt[:, :], bank[0:HM, 0:T])

            @block.scalar
            def _(act):
                for m in on_act:
                    act.wait_ge(*done.at(m + 1))
                    leave(act, m).then_inc(*out[0].up())

            @block.vector
            def _(dve):
                dve.wait_ge(*past_turned.at(1))
                dve.tensor_copy(conv_in_s[:, :, :, 0:3],
                                k.ps[:, 7, 0:24 * CC].rearrange("p (c b r) -> p c b r", c=CC, r=3)).then_inc(*past.up())
                for m in on_dve:
                    dve.wait_ge(*done.at(m + 1))
                    leave(dve, m).then_inc(*out[1].up())


def stage_hgrn_gates(k, proj, hg):
    act_step, dve_step = k.count("act_step"), k.count("dve_step")
    with ExitStack() as s:
        lb = k.sb(s, "lb", [P, 20])
        sig = k.sb(s, "sig", [P, 4, T])
        neg = k.sb(s, "neg", [P, 4, T])
        f = proj[:, F_:F_ + 4, :]
        lm, le, lr = k.count("lb_max"), k.count("lb_exp"), k.count("lb_done")
        expn, expp, gated, logged = (k.count(n) for n in ("exp_minus_f", "exp_f", "forget", "log_forget"))
        with k.stage() as block:
            @block.vector
            def _(dve):
                def then(ins, sig_=dve_step):
                    ins.then_inc(*sig_.up())
                    dve.wait_ge(*sig_.all())
                l0, l1 = k.vec[:, 40:44], k.vec[:, 44:48]
                then(dve.tensor_tensor(lb[:, 0:4], l0, l1, ALU.max))
                then(dve.tensor_tensor(lb[:, 4:8], l0, lb[:, 0:4], ALU.subtract))
                dve.tensor_tensor(lb[:, 8:12], l1, lb[:, 0:4], ALU.subtract).then_inc(*lm.up())
                dve.wait_ge(*le.at(1))
                then(dve.tensor_tensor(lb[:, 12:16], lb[:, 4:8], lb[:, 8:12], ALU.add))
                then(dve.reciprocal(lb[:, 12:16], lb[:, 12:16]))
                then(dve.tensor_tensor(lb[:, 0:4], lb[:, 8:12], lb[:, 12:16], ALU.mult))
                then(dve.tensor_tensor(lb[:, 16:20], lb[:, 4:8], lb[:, 12:16], ALU.mult))
                low, rest = lb[:, 0:4], lb[:, 16:20]
                wide = lambda v: v.unsqueeze(2).broadcast_to([P, 4, T])
                dve.wait_ge(*expn.at(1))
                then(dve.tensor_scalar(sig[:, :, :], sig[:, :, :], 1.0, None, ALU.add))
                then(dve.reciprocal(sig[:, :, :], sig[:, :, :]))
                then(dve.tensor_tensor(sig[:, :, :], sig[:, :, :], wide(rest), ALU.mult))
                dve.tensor_tensor(sig[:, :, :], sig[:, :, :], wide(low), ALU.add).then_inc(*gated.up())
                dve.wait_ge(*expp.at(1))
                then(dve.tensor_scalar(neg[:, :, :], neg[:, :, :], 1.0, None, ALU.add))
                then(dve.reciprocal(neg[:, :, :], neg[:, :, :]))
                then(dve.tensor_tensor(hg["k"][:, :, :], neg[:, :, :], wide(rest), ALU.mult))
                dve.wait_ge(*logged.at(1))
                for c in range(4):
                    then(dve.tensor_tensor_scan(hg["g"][:, c, :], k.const("running"), sig[:, c, :], 0.0, ALU.mult, ALU.add))

            @block.scalar
            def _(act):
                act.wait_ge(*lm.at(1))
                act.activation(lb[:, 4:12], lb[:, 4:12], ACT.Exp).then_inc(*le.up())
                act.activation(sig[:, :, :], f, ACT.Exp, scale=-1.0).then_inc(*expn.up())
                act.activation(neg[:, :, :], f, ACT.Exp).then_inc(*expp.up())
                act.wait_ge(*gated.at(1))
                act.activation(sig[:, :, :], sig[:, :, :], ACT.Ln).then_inc(*logged.up())


def stage_hgrn(k, proj, hg, mixed_out):
    q, v, gate = proj[:, Q:Q + 4, :], proj[:, V:V + 4, :], proj[:, G:G + 4, :]
    kk, g = hg["k"], hg["g"]
    levels = [1 << l for l in range(8)]
    act_step, dve_step = k.count("act_step"), k.count("dve_step")
    with ExitStack() as s:
        X2 = [k.act[:, 4 * n:4 * n + 4, :] for n in range(2)]
        att = k.sb(s, "att", [P, 2, 4, P])
        attx = k.sb(s, "attx", [P, 4, P])
        atts = k.sb(s, "atts", [TS, 4, TS])
        vt = k.sb(s, "v_tokens", [P, 3, 4 * P])
        kd = k.sb(s, "k_decayed", [P, 4, T])
        kdt = k.sb(s, "kd_tokens", [P, 3, 4 * P])
        qe = k.sb(s, "q_decayed", [P, 4, TS])
        vbd = k.sb(s, "v_by_sample", [TS, NB, 4 * P])
        eg = k.sb(s, "state_decay", [P, 4, TS])
        state = k.sb(s, "hgrn_state", [P, NB, 4, P])
        statep = k.sb(s, "hgrn_state_p", [P, 4, P])
        names = ("diff", "level_exp", "level_x", "level_dot", "level_in", "diag_dot", "state_in", "v_turned", "v_copied",
                 "kd_diff", "exp", "kd_done", "kd_turned", "kd_copied", "by_sample", "decays", "qe_done",
                 "state_dot", "state_new", "o_dot", "sq", "sum", "mean", "root", "o_out", "stored", "statep")
        n_ = {x: k.count(x) for x in names}

        def halves(x, H, n):
            b = x[:, :, 0:n]
            if n == T:
                b = b.rearrange("p c (b u) -> p (c b) u", u=2 * H)
                return b[:, :, 0:H], b[:, :, H:2 * H], b[:, :, H - 1:H].broadcast_to([P, 4 * n // (2 * H), H])
            b = b.rearrange("p c (b u) -> p c b u", u=2 * H)
            return b[:, :, :, 0:H], b[:, :, :, H:2 * H], b[:, :, :, H - 1:H].broadcast_to([P, 4, n // (2 * H), H])

        span = lambda H: T if H <= 2 else TP
        with k.stage() as block:
            @block.gpsimd
            def _(pool):
                pool.dma_start(state[:, :, :, :].rearrange("p b c v -> p (b c) v"),
                               k.ins["state_hgrn"].rearrange("b a c k v -> k (b a c) v")).then_inc(*n_["state_in"].up(16))
                pool.wait_ge(*n_["statep"].at(1))
                pool.dma_start(k.outs[10][0, 0].rearrange("c k v -> k c v"), statep[:, :, :]).then_inc(*n_["stored"].up(16))
                pool.wait_ge(*n_["state_new"].at(8))
                pool.dma_start(k.outs[11].rearrange("b a c k v -> k (b a c) v"),
                               state[:, :, :, :].rearrange("p b c v -> p (b c) v")).then_inc(*n_["stored"].up(16))
                pool.wait_ge(*n_["stored"].at(32))

            @block.vector
            def _(dve):
                def then(ins, sig=dve_step):
                    ins.then_inc(*sig.up())
                    dve.wait_ge(*sig.all())

                def diff(l):
                    H, x = levels[l], X2[l % 2]
                    n = span(H)
                    if l >= 2:
                        dve.wait_ge(*n_["level_dot"].at(l - 1))
                    g1, g2, ref = halves(g, H, n)
                    x1, x2, _ = halves(x, H, n)
                    then(dve.tensor_tensor(x1, ref, g1, ALU.subtract))
                    dve.tensor_tensor(x2, g2, ref, ALU.subtract).then_inc(*n_["diff"].up())

                def scale(l):
                    H, x = levels[l], X2[l % 2]
                    n = span(H)
                    dve.wait_ge(*n_["level_exp"].at(l + 1))
                    x1, x2, _ = halves(x, H, n)
                    k1 = halves(kk, H, n)[0]
                    q2 = halves(q, H, n)[1]
                    then(dve.tensor_tensor(x1, x1, k1, ALU.mult))
                    dve.tensor_tensor(x2, x2, q2, ALU.mult).then_inc(*n_["level_x"].up())

                def gather(l):
                    H = levels[l]
                    dve.wait_ge(*n_["level_dot"].at(l + 1))
                    bank = 3 * (l % 2)
                    if H == P:
                        then(dve.tensor_copy(attx[:, :, :], k.ps[:, bank, :].rearrange("p (c n) -> p c n", c=4)), n_["level_in"])
                        return
                    m0, _ = k.core_at["level"]
                    mask = k.core[:, m0 + P * l:m0 + P * l + P].bitcast(I32)
                    if H <= 2:
                        then(dve.copy_predicated(atts[:, :, :], mask[0:TS, 0:TS].unsqueeze(1).broadcast_to([TS, 4, TS]),
                                                 k.ps[0:TS, bank + 2, 0:4 * TS].rearrange("p (c n) -> p c n", c=4)))
                    then(dve.copy_predicated(att[:, :, :, :].rearrange("p i c n -> p (i c) n"), mask.unsqueeze(1).broadcast_to([P, 8, P]),
                                             k.ps[:, bank:bank + 2, :].rearrange("p i (c n) -> p (i c) n", c=4)), n_["level_in"])

                diff(0)
                diff(1)
                dve.wait_ge(*n_["diag_dot"].at(1))
                eye = k.const("ident")
                then(dve.tensor_tensor(att[:, :, :, :].rearrange("p i c n -> p (i c) n"),
                                       k.ps[:, 6:8, :].rearrange("p i (c n) -> p (i c) n", c=4),
                                       eye.unsqueeze(1).broadcast_to([P, 8, P]), ALU.mult))
                then(dve.tensor_tensor(atts[:, :, :], k.ps[0:TS, 5, 0:4 * TS].rearrange("p (c n) -> p c n", c=4),
                                       eye[0:TS, 0:TS].unsqueeze(1).broadcast_to([TS, 4, TS]), ALU.mult), n_["level_in"])
                for l in range(8):
                    scale(l)
                    if l + 2 < 8:
                        diff(l + 2)
                    gather(l)
                wide = lambda ap, n: ap.broadcast_to([P, 4, n])
                then(dve.tensor_tensor(kd[:, :, 0:TP], wide(g[:, :, TP - 1:TP], TP), g[:, :, 0:TP], ALU.subtract))
                kds = kd[:, :, TP:T].rearrange("p c (b t) -> p c b t", t=NT)
                gs4 = g[:, :, TP:T].rearrange("p c (b t) -> p c b t", t=NT)
                dve.tensor_tensor(kds, gs4[:, :, :, NT - 1:NT].broadcast_to([P, 4, NB, NT]), gs4, ALU.subtract).then_inc(*n_["kd_diff"].up())
                for i, (a, n) in enumerate(TILES):
                    dve.wait_ge(*n_["v_turned"].at(i + 1))
                    then(dve.tensor_copy(vt[0:n, i, :], k.ps[0:n, i, :]), n_["v_copied"])
                dve.wait_ge(*n_["exp"].at(1))
                then(dve.tensor_tensor(kd[:, :, :], kd[:, :, :], kk[:, :, :], ALU.mult), n_["kd_done"])
                for i, (a, n) in enumerate(TILES):
                    dve.wait_ge(*n_["kd_turned"].at(i + 1))
                    then(dve.tensor_copy(kdt[0:n, i, :], k.ps[0:n, 3 + i, :]), n_["kd_copied"])
                then(dve.tensor_tensor(vbd[:, :, :], vt[0:TS, 2, :].unsqueeze(1).broadcast_to([TS, NB, 4 * P]),
                                       k.const("batch_of")[0:TS, :].unsqueeze(2).broadcast_to([TS, NB, 4 * P]), ALU.mult), n_["by_sample"])
                dve.wait_ge(*n_["decays"].at(1))
                dve.tensor_tensor(qe[:, :, :], eg[:, :, :], q[:, :, TP:T], ALU.mult).then_inc(*n_["qe_done"].up())
                sq = X2[0]
                for c in range(4):
                    dve.wait_ge(*n_["o_dot"].at(c + 1))
                    then(dve.tensor_copy(mixed_out[:, c, :], k.ps[:, c, 0:T]))
                    dve.tensor_tensor(sq[:, c, :], mixed_out[:, c, :], mixed_out[:, c, :], ALU.mult).then_inc(*n_["sq"].up())
                dve.wait_ge(*n_["state_dot"].at(1))
                dve.tensor_copy(statep[:, :, :], k.ps[:, 4, :].rearrange("p (c v) -> p c v", c=4)).then_inc(*n_["statep"].up())
                for c in range(4):
                    for hf in range(2):
                        i = 2 * c + hf
                        dve.wait_ge(*n_["state_dot"].at(i + 2))
                        for b in range(4 * hf, 4 * hf + 4):
                            last = NT * b + NT - 1
                            ins = dve.scalar_tensor_tensor(state[:, b, c, :], state[:, b, c, :], eg[:, c, last:last + 1],
                                                           k.ps[:, 5 + i % 3, P * (b % 4):P * (b % 4) + P], ALU.mult, ALU.add)
                        ins.then_inc(*n_["state_new"].up())
                rs = X2[1]
                for c in range(4):
                    dve.wait_ge(*n_["sum"].at(c + 1))
                    then(dve.tensor_scalar(rs[:, c, :], k.ps[:, c, 0:T], 1.0 / P, EPS, ALU.mult, ALU.add), n_["mean"])
                dve.wait_ge(*n_["root"].at(2))
                for c in range(4):
                    then(dve.scalar_tensor_tensor(rs[:, c, :], rs[:, c, :], k.vec[:, 48 + c:49 + c], gate[:, c, :], ALU.mult, ALU.mult))
                    then(dve.tensor_tensor(mixed_out[:, c, :], mixed_out[:, c, :], rs[:, c, :], ALU.mult), n_["o_out"])

            @block.scalar
            def _(act):
                for l in range(8):
                    act.wait_ge(*n_["diff"].at(l + 1))
                    x = X2[l % 2][:, :, 0:span(levels[l])]
                    act.activation(x, x, ACT.Exp).then_inc(*n_["level_exp"].up())
                act.activation(eg[:, :, :], g[:, :, TP:T], ACT.Exp).then_inc(*n_["decays"].up())
                act.wait_ge(*n_["kd_diff"].at(1))
                act.activation(kd[:, :, :], kd[:, :, :], ACT.Exp).then_inc(*n_["exp"].up())
                rs = X2[1]
                act.wait_ge(*n_["mean"].at(4))
                act.activation(rs[:, :, :], rs[:, :, :], ACT.Ln).then_inc(*n_["root"].up())
                act.wait_ge(*n_["root"].at(1))
                act.activation(rs[:, :, :], rs[:, :, :], ACT.Exp, scale=-0.5).then_inc(*n_["root"].up())

            @block.tensor
            def _(pe):
                ident = k.const("ident")
                for i in range(2):
                    for c in range(4):
                        mm = pe.matmul(k.ps[:, 6 + i, P * c:P * c + P], kk[:, c, P * i:P * i + P], q[:, c, P * i:P * i + P], start=True, stop=True)
                for c in range(4):
                    mm = pe.matmul(k.ps[0:TS, 5, TS * c:TS * c + TS], kk[:, c, TP:T], q[:, c, TP:T], start=True, stop=True)
                mm.then_inc(*n_["diag_dot"].up())
                for l, H in enumerate(levels):
                    x, bank = X2[l % 2], 3 * (l % 2)
                    pe.wait_ge(*n_["level_x"].at(l + 1))
                    if l >= 1:
                        pe.wait_ge(*n_["level_in"].at(max(l, 1)))
                    if H == P:
                        for c in range(4):
                            mm = pe.matmul(k.ps[:, bank, P * c:P * c + P], x[:, c, 0:P], x[:, c, P:2 * P], start=True, stop=True)
                    else:
                        for i in range(2):
                            for c in range(4):
                                tile = x[:, c, P * i:P * i + P]
                                mm = pe.matmul(k.ps[:, bank + i, P * c:P * c + P], tile, tile, start=True, stop=True)
                        if H <= 2:
                            for c in range(4):
                                mm = pe.matmul(k.ps[0:TS, bank + 2, TS * c:TS * c + TS], x[:, c, TP:T], x[:, c, TP:T], start=True, stop=True)
                    mm.then_inc(*n_["level_dot"].up())
                pe.wait_ge(*n_["level_in"].at(9))
                for i, (a, n) in enumerate(TILES):
                    for c in range(4):
                        mm = pe.transpose(k.ps[0:n, i, P * c:P * c + P], v[:, c, a:a + n], ident)
                    mm.then_inc(*n_["v_turned"].up())
                pe.wait_ge(*n_["kd_done"].at(1))
                for i, (a, n) in enumerate(TILES):
                    for c in range(4):
                        mm = pe.transpose(k.ps[0:n, 3 + i, P * c:P * c + P], kd[:, c, a:a + n], ident)
                    mm.then_inc(*n_["kd_turned"].up())
                pe.wait_ge(*n_["state_in"].at(16))
                pe.wait_ge(*n_["qe_done"].at(1))
                for c in range(4):
                    cols = slice(P * c, P * c + P)
                    pe.matmul(k.ps[:, c, 0:P], vt[:, 0, cols], att[:, 0, c, :], start=True, stop=True)
                    pe.matmul(k.ps[:, c, P:TP], vt[:, 1, cols], att[:, 1, c, :], start=True, stop=False)
                    pe.matmul(k.ps[:, c, P:TP], vt[:, 0, cols], attx[:, c, :], start=False, stop=True)
                    pe.matmul(k.ps[:, c, TP:T], vt[0:TS, 2, cols], atts[:, c, :], start=True, stop=False, skip_group_check=True)
                    for b in range(NB):
                        mm = pe.matmul(k.ps[:, c, TP + NT * b:TP + NT * b + NT], state[:, b, c, :],
                                       qe[:, c, NT * b:NT * b + NT], start=False, stop=b == NB - 1, skip_group_check=True)
                    mm.then_inc(*n_["o_dot"].up())
                pe.wait_ge(*n_["kd_copied"].at(3))
                for c in range(4):
                    for i in range(2):
                        mm = pe.matmul(k.ps[:, 4, P * c:P * c + P], kdt[:, i, P * c:P * c + P], vt[:, i, P * c:P * c + P],
                                       start=i == 0, stop=i == 1)
                mm.then_inc(*n_["state_dot"].up())
                pe.wait_ge(*n_["by_sample"].at(1))
                for i in range(8):
                    c, hf = i // 2, i % 2
                    if i >= 3:
                        pe.wait_ge(*n_["state_new"].at(i - 2))
                    pe.matmul(k.ps[:, 5 + i % 3, :], kdt[0:TS, 2, P * c:P * c + P], vbd[:, 4 * hf:4 * hf + 4, P * c:P * c + P],
                              start=True, stop=True).then_inc(*n_["state_dot"].up())
                sq = X2[0]
                for c in range(4):
                    pe.wait_ge(*n_["sq"].at(c + 1))
                    pe.matmul(k.ps[:, c, 0:T], k.const("ones"), sq[:, c, :], start=True, stop=True).then_inc(*n_["sum"].up())


def stage_conv(k, conv_in, conv_in_s, xc):
    with ExitStack() as s:
        rows_p = k.sb(s, "conv_rows_p", [3, CC * P])
        rows_s = k.sb(s, "conv_rows_s", [3 * NB, CC * P])
        last3 = k.sb(s, "conv_last3", [P, CC, 3 * NB])
        packed = k.count("conv_packed")
        first, tapped, silued, dve_step = (k.count(n) for n in ("tap_first", "taps", "conv_silu", "dve_step"))
        turned, copied, stored = (k.count(n) for n in ("rows_turned", "rows_copied", "rows_stored"))
        w = lambda j, c: k.vec[:, 60 + CC * j + c:61 + CC * j + c]
        bias = lambda c: k.vec[:, 108 + c:109 + c]
        outp = lambda c: xc[:, c, 0:TP]
        outs = lambda c: xc[:, c, TP:T].rearrange("p (b t) -> p b t", t=NT)
        with k.stage() as block:
            @block.scalar
            def _(act):
                for c in range(CC):
                    act.activation(outs(c), conv_in_s[:, c, :, 0:NT], ACT.Identity, scale=w(0, c), bias=bias(c)).then_inc(*first.up())
                    act.activation(outp(c), conv_in[:, c, 0:TP], ACT.Identity, scale=w(0, c), bias=bias(c)).then_inc(*first.up())
                    if c >= 2:
                        act.wait_ge(*tapped.at(c - 1))
                        act.activation(xc[:, c - 2, :], xc[:, c - 2, :], ACT.Silu).then_inc(*silued.up())
                for c in (CC - 2, CC - 1):
                    act.wait_ge(*tapped.at(c + 1))
                    act.activation(xc[:, c, :], xc[:, c, :], ACT.Silu).then_inc(*silued.up())

            @block.vector
            def _(dve):
                dve.tensor_copy(last3[:, :, :].rearrange("p c (b r) -> p c b r", r=3), conv_in_s[:, :, :, NT:NT + 3]).then_inc(*packed.up())
                for c in range(CC):
                    dve.wait_ge(*first.at(2 * c + 2))
                    for j in range(1, 4):
                        if j > 1:
                            dve.wait_ge(*dve_step.all())
                        dve.scalar_tensor_tensor(outs(c), conv_in_s[:, c, :, j:j + NT], w(j, c), outs(c), ALU.mult, ALU.add)\
                           .then_inc(*dve_step.up())
                        dve.scalar_tensor_tensor(outp(c), conv_in[:, c, j:j + TP], w(j, c), outp(c), ALU.mult, ALU.add)\
                           .then_inc(*(tapped if j == 3 else dve_step).up())
                for n, (dst, rows) in enumerate(((rows_p, 3), (rows_s, 24))):
                    dve.wait_ge(*turned.at(n + 1))
                    dve.tensor_copy(dst[:, :].rearrange("r (b n) -> r b n", b=3), k.ps[0:rows, 3 * n:3 * n + 3, :]).then_inc(*copied.up())

            @block.tensor
            def _(pe):
                pe.wait_ge(*packed.at(1))
                for n in range(2):
                    for c in range(CC):
                        in_ = last3[:, c, :] if n else conv_in[:, c, TP:TP + 3]
                        mm = pe.transpose(k.ps[0:24 if n else 3, 3 * n + c // 4, P * (c % 4):P * (c % 4) + P], in_, k.const("ident"))
                    mm.then_inc(*turned.up())

            @block.gpsimd
            def _(pool):
                pool.wait_ge(*copied.at(1))
                pool.dma_start(k.outs[14][0, 0], rows_p[:, :]).then_inc(*stored.up(16))
                pool.wait_ge(*copied.at(2))
                pool.dma_start(k.outs[15].rearrange("b a r c -> (b a r) c"), rows_s[:, :]).then_inc(*stored.up(16))
                pool.wait_ge(*stored.at(32))


def stage_dt(k, dt, dta):
    acum, wend, dtt = dta["acum"], dta["wend"], dta["tok"]
    with ExitStack() as s:
        par = k.sb(s, "dt_params", [HM, 4])
        u = k.sb(s, "dt_u", [HM, T])
        par_in, raw_ready, log_ready, a_ready, dt_done, sums, ended = (k.count("d_" + n) for n in (
            "par_in", "raw", "log", "a", "dt", "sums", "ended"))
        diffed, turned, copied = k.count("d_diff"), k.count("turned"), k.count("copied")
        act_step, dve_step = k.count("act_step"), k.count("dve_step")
        with k.stage() as block:
            @block.sync
            def _(sp):
                for n, name in enumerate(("dt_bias", "a_log", "d_skip")):
                    sp.dma_start(par[:, n:n + 1], k.ins[name].rearrange("a h -> h a")).then_inc(*par_in.up(16))

            @block.vector
            def _(dve):
                def then(ins, sig=dve_step):
                    ins.then_inc(*sig.up())
                    dve.wait_ge(*sig.all())
                dve.wait_ge(*par_in.at(48))
                then(dve.tensor_scalar(dt[:, :], dt[:, :], par[:, 0:1], None, ALU.add), raw_ready)
                dve.wait_ge(*log_ready.at(1))
                then(dve.scalar_tensor_tensor(dt[:, :], dt[:, :], 0.0, u[:, :], ALU.max, ALU.add), dt_done)
                dve.wait_ge(*a_ready.at(1))
                then(dve.tensor_scalar(u[:, :], dt[:, :], par[:, 3:4], -1.0, ALU.mult, ALU.mult))
                then(dve.tensor_tensor_scan(acum[:, :], k.const("running")[0:HM, :], u[:, :], 0.0, ALU.mult, ALU.add), sums)
                dve.tensor_tensor(wend[:, 0:TP], acum[:, TP - 1:TP].broadcast_to([HM, TP]), acum[:, 0:TP], ALU.subtract).then_inc(*dve_step.up())
                ac = acum[:, TP:T].rearrange("p (b t) -> p b t", t=NT)
                dve.tensor_tensor(wend[:, TP:T].rearrange("p (b t) -> p b t", t=NT), ac[:, :, NT - 1:NT].broadcast_to([HM, NB, NT]), ac,
                                  ALU.subtract).then_inc(*diffed.up())
                dve.wait_ge(*ended.at(1))
                then(dve.tensor_tensor(wend[:, :], wend[:, :], dt[:, :], ALU.mult), ended)
                dve.wait_ge(*turned.at(1))
                dve.tensor_copy(dtt[:, 0:2, :], k.ps[:, 0, 0:96].rearrange("p (i n) -> p i n", i=2)).then_inc(*copied.up())
                dve.tensor_copy(dtt[0:TS, 2, :], k.ps[0:TS, 0, 96:144]).then_inc(*copied.up())
                dve.tensor_copy(dta["skip"][:, :], k.ps[:, 1, 0:8]).then_inc(*copied.up())

            @block.scalar
            def _(act):
                def then(ins, sig=act_step):
                    ins.then_inc(*sig.up())
                    act.wait_ge(*sig.all())
                act.wait_ge(*par_in.at(48))
                act.activation(par[:, 3:4], par[:, 1:2], ACT.Exp).then_inc(*a_ready.up())
                act.wait_ge(*raw_ready.at(1))
                then(act.activation(u[:, :], dt[:, :], ACT.Abs))
                then(act.activation(u[:, :], u[:, :], ACT.Exp, scale=-1.0))
                act.activation(u[:, :], u[:, :], ACT.Ln, bias=1.0).then_inc(*log_ready.up())
                act.wait_ge(*diffed.at(1))
                act.wait_ge(*dve_step.all())
                act.activation(wend[:, :], wend[:, :], ACT.Exp).then_inc(*ended.up())

            @block.tensor
            def _(pe):
                pe.wait_ge(*par_in.at(48))
                pairs = k.const("head_pair")
                for j in range(8):
                    pe.matmul(k.ps[:, 1, j:j + 1], pairs[0:HM, P * j:P * j + P], par[:, 2:3], start=True, stop=True)
                pe.wait_ge(*ended.at(2))
                for i, (a, n) in enumerate(TILES):
                    for m, src in enumerate((acum, dt, wend)):
                        mm = pe.transpose(k.ps[0:n, 0, 48 * i + 16 * m:48 * i + 16 * m + 16], src[:, a:a + n], k.const("ident")[0:HM, 0:HM])
                mm.then_inc(*turned.up())


SUM_BANKS = (2, 3, 4, 6)


def stage_ssd(k, proj, xc, dt, dta, mixed_out):
    acum, dtt = dta["acum"], dta["tok"]
    first_out = 4
    act_step, dve_step = k.count("act_step"), k.count("dve_step")
    with ExitStack() as s:
        xt = k.sb(s, "x_tokens", [P, 3, D])
        bt = k.sb(s, "b_tokens", [P, 3, 256])
        gm = k.sb(s, "cb", [P, 4, 416])
        dec = [k.sb(s, f"decay{n}", [P, 416]) for n in range(2)]
        sc = [k.sb(s, f"scores{n}", [P, 416]) for n in range(2)]
        state = k.sb(s, "ssm_state", [P, NB, 8, 64])
        stT = k.sb(s, "ssm_state_t", [P, NB, 4, P])
        statep = k.sb(s, "ssm_state_p", [P, 8, 64])
        ebc = k.sb(s, "ebc", [P, 8, TS])
        inter = k.sb(s, "inter", [P, 8, TS])
        bbd = proj[0:TS, 0:NB, 0:256]
        names = ("state_in", "xt_turned", "xt_copied", "cb_dot", "cb_copied", "row", "diff", "exp", "scores", "y_dot", "y_taken",
                 "st_turned", "st_copied", "ebc_dot", "ebc_exp", "inter_dot", "inter_done", "xw", "by_sample", "state_dot", "state_new",
                 "statep", "stored", "scaled", "sq", "sum", "mean", "root", "out")
        n_ = {x: k.count(x) for x in names}
        xtiles = [(i, q) for i in range(3) for q in range(2)]

        def slot(j):
            return 4 * (j // 4) + 2 * (j % 2) + (j // 2) % 2

        def parts(x):
            y = x[:, :, :, :].rearrange("p b (J w v) n -> p (b J) w v n", w=2, v=2)
            return [y[:, :, w, v, :] for v in range(2) for w in range(2)]

        def dram_parts(x):
            y = x.rearrange("b a (J v w u) p n -> v w (u p) (b a J) n", v=2, w=2, u=2)
            return [y[v, w] for v in range(2) for w in range(2)]

        def brow(g):
            return slice(64 * (g % 2), 64 * (g % 2) + 64)

        with k.stage() as block:
            @block.gpsimd
            def _(pool):
                for dst, src in zip(parts(state), dram_parts(k.ins["state_ssm"])):
                    pool.dma_start(dst, src).then_inc(*n_["state_in"].up(16))
                pool.wait_ge(*n_["statep"].at(1))
                pool.dma_start(k.outs[12][0, 0].rearrange("(j u) p n -> (u p) j n", u=2), statep[:, :, :]).then_inc(*n_["stored"].up(16))
                pool.wait_ge(*n_["state_new"].at(9))
                for src, dst in zip(parts(state), dram_parts(k.outs[13])):
                    pool.dma_start(dst, src).then_inc(*n_["stored"].up(16))
                pool.wait_ge(*n_["stored"].at(80))

            @block.tensor
            def _(pe):
                ident = k.const("ident")
                n = 0
                for i, (a, m) in enumerate(TILES):
                    for u in range(3):
                        if n >= 2:
                            pe.wait_ge(*n_["xt_copied"].at(n - 1))
                        for c in range(4 if u < 2 else 2):
                            mm = pe.transpose(k.ps[0:m, n % 2, P * c:P * c + P], xc[:, 4 * u + c, a:a + m], ident)
                        mm.then_inc(*n_["xt_turned"].up())
                        n += 1
                for g in range(4):
                    b, c, r = xc[:, 8 + g // 2, :], xc[:, 10 + g // 2, :], brow(g)
                    if g >= 1:
                        pe.wait_ge(*n_["cb_copied"].at(g))
                    pe.matmul(k.ps[:, 2, 0:TP], b[r, 0:P], c[r, 0:TP], start=True, stop=True)
                    pe.matmul(k.ps[:, 2, TP:TP + P], b[r, P:TP], c[r, P:TP], start=True, stop=True)
                    pe.matmul(k.ps[0:TS, 2, 384:416], b[r, TP:T], c[r, TP:T], start=True, stop=True).then_inc(*n_["cb_dot"].up())
                pe.wait_ge(*n_["state_in"].at(64))
                pe.wait_ge(*n_["xt_copied"].at(9))
                for b in range(NB):
                    if b >= 2:
                        pe.wait_ge(*n_["st_copied"].at(b - 1))
                    for q in range(4):
                        mm = pe.transpose(k.ps[:, b % 2, P * q:P * q + P], state[:, b, 2 * q:2 * q + 2, :].rearrange("p v n -> p (v n)"), ident)
                    mm.then_inc(*n_["st_turned"].up())
                pe.wait_ge(*n_["cb_copied"].at(4))
                pairs = k.const("head_pair")
                for j in range(8):
                    mm = pe.matmul(k.ps[:, 2, TS * slot(j):TS * slot(j) + TS], pairs[0:HM, P * j:P * j + P], acum[:, TP:T], start=True, stop=True)
                mm.then_inc(*n_["ebc_dot"].up())
                pe.wait_ge(*n_["st_copied"].at(NB))
                for par in range(2):
                    for b in range(NB):
                        for j in range(8):
                            g = j // 2
                            if g % 2 != par:
                                continue
                            r = brow(g)
                            mm = pe.matmul(k.ps[:, 3 + par, TS * j + NT * b:TS * j + NT * b + NT], stT[r, b, 2 * (j // 4) + j % 2, :],
                                           xc[r, 10 + g // 2, TP + NT * b:TP + NT * b + NT], start=True, stop=True)
                mm.then_inc(*n_["inter_dot"].up())

                def row(h):
                    if h >= 2:
                        pe.wait_ge(*n_["diff"].at(3 * (h - 1)))
                    pe.matmul(k.ps[:, h % 2, 0:T], ident[0:HM, h:h + 1].broadcast_to([HM, P]), acum[:, :], start=True, stop=True)\
                      .then_inc(*n_["row"].up())
                row(0)
                row(1)
                for h in range(HM):
                    pe.wait_ge(*n_["scores"].at(3 * h + 3))
                    if h % 2 == 0 and h >= 4:
                        pe.wait_ge(*n_["y_taken"].at(h // 2 - 1))
                    r, bank, x = slice(64 * (h % 2), 64 * (h % 2) + 64), 6 + (h // 2) % 2, slice(64 * h, 64 * h + 64)
                    m = sc[h % 2]
                    pe.matmul(k.ps[r, bank, 0:TP], xt[:, 0, x], m[:, 0:TP], start=True, stop=False, skip_group_check=True)
                    pe.matmul(k.ps[r, bank, P:TP], xt[:, 1, x], m[:, TP:TP + P], start=False, stop=True, skip_group_check=True)
                    pe.matmul(k.ps[r, bank, TP:T], xt[0:TS, 2, x], m[0:TS, 384:416], start=True, stop=True).then_inc(*n_["y_dot"].up())
                    if h + 2 < HM:
                        row(h + 2)
                pe.wait_ge(*n_["xw"].at(3))
                for j in range(8):
                    for i in range(2):
                        mm = pe.matmul(k.ps[:, 5, 64 * j:64 * j + 64], xt[:, i, P * j:P * j + P], bt[:, i, 64 * (j // 2):64 * (j // 2) + 64],
                                       start=i == 0, stop=i == 1)
                mm.then_inc(*n_["state_dot"].up())
                pe.wait_ge(*n_["by_sample"].at(1))
                for j in range(8):
                    if j >= 2:
                        pe.wait_ge(*n_["state_new"].at(j))
                    g = j // 2
                    pe.matmul(k.ps[:, j % 2, :], xt[0:TS, 2, P * j:P * j + P], bbd[:, :, 64 * g:64 * g + 64],
                              start=True, stop=True).then_inc(*n_["state_dot"].up())
                for g in range(4):
                    pe.wait_ge(*n_["sq"].at(2 * g + 2))
                    for u in range(2):
                        mm = pe.matmul(k.ps[:, SUM_BANKS[g], 0:T], k.const("ones"),
                                       dta["sq"][:, 2 * g + u, :], start=u == 0, stop=u == 1)
                    mm.then_inc(*n_["sum"].up())

            @block.vector
            def _(dve):
                def then(ins, sig=dve_step):
                    ins.then_inc(*sig.up())
                    dve.wait_ge(*sig.all())
                n = 0
                for i, (a, m) in enumerate(TILES):
                    for u in range(3):
                        dve.wait_ge(*n_["xt_turned"].at(n + 1))
                        dst = xt[0:m, i, 512 * u:512 * u + 512] if u < 2 else bt[0:m, i, :]
                        dve.tensor_copy(dst, k.ps[0:m, n % 2, 0:dst.shape[1]]).then_inc(*n_["xt_copied"].up())
                        n += 1
                for g in range(4):
                    dve.wait_ge(*n_["cb_dot"].at(g + 1))
                    dve.tensor_copy(gm[0:TS, g, 384:416], k.ps[0:TS, 2, 384:416]).then_inc(*dve_step.up())
                    dve.tensor_copy(gm[:, g, 0:384], k.ps[:, 2, 0:384]).then_inc(*n_["cb_copied"].up())
                for b in range(NB):
                    dve.wait_ge(*n_["st_turned"].at(b + 1))
                    dve.tensor_copy(stT[:, b, :, :], k.ps[:, b % 2, :].rearrange("p (q n) -> p q n", q=4)).then_inc(*n_["st_copied"].up())
                dve.wait_ge(*n_["cb_copied"].at(4))

                def diff(h):
                    bank, d = k.ps[:, h % 2, :], dec[h % 2]
                    dve.wait_ge(*n_["row"].at(h + 1))
                    if h >= 2:
                        dve.wait_ge(*n_["scores"].at(3 * (h - 1)))
                    fut = k.const("ssd_future")
                    for rows, dcol, bcol, w, i, mask in ((P, 0, 0, TP, 0, fut[:, 0:TP]), (P, TP, P, P, 1, fut[:, 0:P]),
                                                         (TS, 384, TP, TS, 2, k.const("ssd_future_s")[0:TS, :])):
                        dve.scalar_tensor_tensor(d[0:rows, dcol:dcol + w], bank[0:rows, bcol:bcol + w], dtt[0:rows, i, h:h + 1], mask,
                                                 ALU.subtract, ALU.add).then_inc(*n_["diff"].up())

                def score(h):
                    d, m, g = dec[h % 2], sc[h % 2], h // 4
                    dve.wait_ge(*n_["exp"].at(2 * h + 2))
                    if h >= 2:
                        dve.wait_ge(*n_["y_dot"].at(h - 1))
                    for rows, col, w, i in ((P, 0, TP, 0), (P, TP, P, 1), (TS, 384, TS, 2)):
                        dve.scalar_tensor_tensor(m[0:rows, col:col + w], d[0:rows, col:col + w], dtt[0:rows, i, 16 + h:17 + h],
                                                 gm[0:rows, g, col:col + w], ALU.mult, ALU.mult).then_inc(*n_["scores"].up())

                def take(j):
                    bank = k.ps[:, 6 + j % 2, :]
                    y = mixed_out[:, first_out + j, :]
                    dve.wait_ge(*n_["y_dot"].at(2 * j + 2))
                    then(dve.scalar_tensor_tensor(y, xc[:, j, :], dta["skip"][:, j:j + 1], bank[:, 0:T], ALU.mult, ALU.add), n_["y_taken"])
                    if j == 0:
                        dve.wait_ge(*n_["ebc_exp"].at(1))
                        dve.wait_ge(*n_["inter_dot"].at(1))
                        for par in range(2):
                            pv = k.ps[:, 3 + par, 0:TP].rearrange("p (j t) -> p j t", t=TS)
                            for jj in (0, 1, 4, 5) if par == 0 else (2, 3, 6, 7):
                                then(dve.tensor_tensor(inter[:, jj, :], pv[:, jj, :], ebc[:, slot(jj), :], ALU.mult))
                    then(dve.tensor_tensor(y[:, TP:T], y[:, TP:T], inter[:, j, :], ALU.add))
                    then(dve.tensor_tensor(y, y, proj[:, Z + j, :], ALU.mult), n_["scaled"])

                diff(0)
                for h in range(HM):
                    if h + 1 < HM:
                        diff(h + 1)
                    score(h)
                    if h >= 2 and h % 2 == 1:
                        take(h // 2 - 1)
                take(7)
                for i, (a, m) in enumerate(TILES):
                    v = xt[0:m, i, :].rearrange("p (h n) -> p h n", h=HM)
                    then(dve.tensor_tensor(v, v, dtt[0:m, i, 32:48].unsqueeze(2).broadcast_to([m, HM, 64]), ALU.mult), n_["xw"])
                then(dve.tensor_tensor(bbd, bt[0:TS, 2, :].unsqueeze(1).broadcast_to([TS, NB, 256]),
                                       k.const("batch_of")[0:TS, :].unsqueeze(2).broadcast_to([TS, NB, 256]), ALU.mult), n_["by_sample"])
                dve.wait_ge(*n_["state_dot"].at(1))
                dve.tensor_copy(statep[:, :, :], k.ps[:, 5, :].rearrange("p (j n) -> p j n", j=8)).then_inc(*n_["statep"].up())
                last = ebc[:, :, :].rearrange("p j (b t) -> p b j t", t=NT)[:, :, :, NT - 1:NT]
                then(dve.tensor_tensor(state[:, :, :, :], state[:, :, :, :], last.broadcast_to([P, NB, 8, 64]), ALU.mult), n_["state_new"])
                for j in range(8):
                    dve.wait_ge(*n_["state_dot"].at(j + 2))
                    dve.tensor_tensor(state[:, :, slot(j), :], state[:, :, slot(j), :], k.ps[:, j % 2, :].rearrange("p (b n) -> p b n", b=NB),
                                      ALU.add).then_inc(*n_["state_new"].up())
                rs = dta["rs"]
                for g in range(4):
                    dve.wait_ge(*n_["sum"].at(g + 1))
                    dve.tensor_scalar(rs[:, g, :], k.ps[:, SUM_BANKS[g], 0:T], 1.0 / 256, EPS, ALU.mult, ALU.add).then_inc(*n_["mean"].up())
                dve.wait_ge(*n_["root"].at(2))
                for j in range(8):
                    y = mixed_out[:, first_out + j, :]
                    dve.scalar_tensor_tensor(y, y, k.vec[:, 52 + j:53 + j], rs[:, j // 2, :], ALU.mult, ALU.mult).then_inc(*n_["out"].up())

            @block.scalar
            def _(act):
                act.wait_ge(*n_["ebc_dot"].at(1))
                act.activation(ebc[:, :, :], k.ps[:, 2, 0:TP].rearrange("p (j t) -> p j t", t=TS), ACT.Exp).then_inc(*n_["ebc_exp"].up())

                def square(j):
                    act.wait_ge(*n_["scaled"].at(j + 1))
                    act.activation(dta["sq"][:, j, :], mixed_out[:, first_out + j, :], ACT.Square).then_inc(*n_["sq"].up())

                for h in range(HM):
                    act.wait_ge(*n_["diff"].at(3 * h + 3))
                    d = dec[h % 2]
                    act.activation(d[:, 0:384], d[:, 0:384], ACT.Exp).then_inc(*n_["exp"].up())
                    act.activation(d[0:TS, 384:416], d[0:TS, 384:416], ACT.Exp).then_inc(*n_["exp"].up())
                    if h >= 4 and h % 2 == 0:
                        square(h // 2 - 2)
                square(6)
                square(7)
                rs = dta["rs"]
                act.wait_ge(*n_["mean"].at(4))
                act.activation(rs[:, :, :], rs[:, :, :], ACT.Ln).then_inc(*n_["root"].up())
                act.wait_ge(*n_["root"].at(1))
                act.activation(rs[:, :, :], rs[:, :, :], ACT.Exp, scale=-0.5).then_inc(*n_["root"].up())



def stage_route(k, moe):
    nc = k.nc
    I = MAX_ITEMS + 1
    with ExitStack() as s:
        wr = k.sb(s, "w_router", [P, DC, NE])
        lg = k.sb(s, "logits", [P, 3, NE])
        gt = k.sb(s, "greater", [P, 3, NE, NE])
        eq = k.sb(s, "equal", [P, 3, NE, NE])
        chosen = k.sb(s, "chosen", [P, 3, NE])
        gate = k.sb(s, "gate", [P, 3, NE])
        place = k.sb(s, "place", [P, 3, NE])
        cnt = k.sb(s, "cnt", [P, 4, NE])
        one = k.sb(s, "item_expert", [P, I, NE])
        blk = k.sb(s, "item_block", [P, I, NE])
        tmp = k.sb(s, "item_tmp", [P, I, NE])
        tmp2 = k.sb(s, "item_tmp2", [P, I, NE])
        ids = k.sb(s, "item_ids", [P, I + 1])
        small = k.sb(s, "small", [P, 3, 2])
        wr_in, logit, turned, copied, exp_in, exped, chose, ranked = (k.count(n) for n in (
            "router_in", "scored", "turned", "copied", "diff", "exped", "chosen", "ranked"))
        dve_step = k.count("dve_step")
        with k.stage() as block:
            @block.sync
            def _(sp):
                sp.dma_start(wr[:, :, :], k.ins["w_router"][0].rearrange("(c p) e -> p c e", p=P)).then_inc(*wr_in.up(16))

            @block.tensor
            def _(pe):
                pe.wait_ge(*wr_in.at(16))
                for i, (a, n) in enumerate(TILES):
                    for c in range(DC):
                        mm = pe.matmul(k.ps[0:n, 0, NE * i:NE * i + NE], k.act[:, c, a:a + n], wr[:, c, :], start=c == 0, stop=c == DC - 1)
                mm.then_inc(*logit.up())
                for i, (a, n) in enumerate(TILES):
                    for u in range(2):
                        for c in range(4):
                            mm = pe.transpose(k.ps[0:n, 2 + 2 * i + u, P * c:P * c + P], k.act[:, 4 * u + c, a:a + n], k.const("ident"))
                        mm.then_inc(*turned.up())
                pe.wait_ge(*chose.at(1))
                for i in range(3):
                    for e in range(i + 1):
                        pe.matmul(k.ps[:, 1, NE * i:NE * i + NE], k.const("ones") if e < i else k.const("before"), chosen[:, e, :],
                                  start=e == 0, stop=e == i)
                for i in range(3):
                    mm = pe.matmul(k.ps[:, 1, 32:32 + NE], k.const("ones"), chosen[:, i, :], start=i == 0, stop=i == 2)
                mm.then_inc(*ranked.up())

            @block.scalar
            def _(act):
                for n in range(6):
                    act.wait_ge(*turned.at(n + 1))
                    rows = TILES[n // 2][1]
                    act.copy(moe["tokens"][0:rows, n // 2, 512 * (n % 2):512 * (n % 2) + 512], k.ps[0:rows, 2 + n, :]).then_inc(*copied.up())
                act.wait_ge(*exp_in.at(1))
                act.activation(gate[:, :, :], gate[:, :, :], ACT.Exp).then_inc(*exped.up())

            @block.vector
            def _(dve):
                def then(ins, sig=dve_step):
                    ins.then_inc(*sig.up())
                    dve.wait_ge(*sig.all())
                then(dve.memset(lg[:, :, :], 0.0))
                dve.wait_ge(*logit.at(1))
                dve.tensor_copy(lg[0:TS, 2, :], k.ps[0:TS, 0, 16:24]).then_inc(*dve_step.up())
                then(dve.tensor_copy(lg[:, 0:2, :], k.ps[:, 0, 0:16].rearrange("p (i e) -> p i e", i=2)))
                other = lg[:, :, :].unsqueeze(2).broadcast_to([P, 3, NE, NE])
                mine = lg[:, :, :].unsqueeze(3).broadcast_to([P, 3, NE, NE])
                then(dve.tensor_tensor(gt[:, :, :, :], other, mine, ALU.is_gt))
                then(dve.tensor_tensor(eq[:, :, :, :], other, mine, ALU.is_equal))
                earlier = k.const("earlier_expert").rearrange("p (e f) -> p e f", e=NE).unsqueeze(1).broadcast_to([P, 3, NE, NE])
                then(dve.tensor_tensor(eq[:, :, :, :], eq[:, :, :, :], earlier, ALU.mult))
                then(dve.tensor_tensor(gt[:, :, :, :], gt[:, :, :, :], eq[:, :, :, :], ALU.add))
                then(dve.tensor_reduce(chosen[:, :, :], gt[:, :, :, :], AX, ALU.add))
                then(dve.tensor_scalar(chosen[:, :, :], chosen[:, :, :], 2.0, None, ALU.is_lt))
                valid = k.const("valid").rearrange("p (i e) -> p i e", i=3)
                then(dve.tensor_tensor(chosen[:, :, :], chosen[:, :, :], valid, ALU.mult), chose)
                then(dve.tensor_reduce(small[:, :, 0:1], lg[:, :, :], AX, ALU.max))
                then(dve.tensor_tensor(gate[:, :, :], lg[:, :, :], small[:, :, 0:1].broadcast_to([P, 3, NE]), ALU.subtract), exp_in)
                dve.wait_ge(*exped.at(1))
                then(dve.tensor_tensor(gate[:, :, :], gate[:, :, :], chosen[:, :, :], ALU.mult))
                then(dve.tensor_reduce(small[:, :, 1:2], gate[:, :, :], AX, ALU.add))
                then(dve.tensor_scalar(small[:, :, 1:2], small[:, :, 1:2], 1e-30, None, ALU.max))
                then(dve.reciprocal(small[:, :, 1:2], small[:, :, 1:2]))
                then(dve.tensor_tensor(gate[:, :, :], gate[:, :, :], small[:, :, 1:2].broadcast_to([P, 3, NE]), ALU.mult))
                dve.wait_ge(*ranked.at(1))
                then(dve.tensor_copy(cnt[:, 0, :], k.ps[:, 1, 32:32 + NE]))
                then(dve.scalar_tensor_tensor(place[:, :, :], k.ps[:, 1, 0:24].rearrange("p (i e) -> p i e", i=3), 1.0, chosen[:, :, :],
                                              ALU.add, ALU.mult))
                then(dve.tensor_scalar(cnt[:, 1, :], cnt[:, 0, :], 0.0, None, ALU.is_gt))
                for edge in (128.0, 256.0):
                    then(dve.scalar_tensor_tensor(cnt[:, 1, :], cnt[:, 0, :], edge, cnt[:, 1, :], ALU.is_gt, ALU.add))
                then(dve.tensor_tensor_scan(cnt[:, 2, :], k.ones_wide[:, 0:NE], cnt[:, 1, :], 0.0, ALU.mult, ALU.add))
                then(dve.tensor_tensor(cnt[:, 3, :], cnt[:, 2, :], cnt[:, 1, :], ALU.subtract))
                item = k.const("items").unsqueeze(2).broadcast_to([P, I, NE])
                per = lambda ap: ap.unsqueeze(1).broadcast_to([P, I, NE])
                then(dve.tensor_tensor(blk[:, :, :], item, per(cnt[:, 3, :]), ALU.subtract))
                then(dve.tensor_tensor(tmp[:, :, :], item, per(cnt[:, 2, :]), ALU.is_lt))
                then(dve.scalar_tensor_tensor(one[:, :, :], blk[:, :, :], 0.0, tmp[:, :, :], ALU.is_ge, ALU.mult))
                then(dve.scalar_tensor_tensor(blk[:, :, :], blk[:, :, :], float(P), one[:, :, :], ALU.mult, ALU.mult))
                then(dve.tensor_tensor(tmp[:, :, :], one[:, :, :], per(k.const("expert_ids")), ALU.mult))
                then(dve.tensor_reduce(ids[:, 0:I], tmp[:, :, :], AX, ALU.add))
                then(dve.tensor_copy(ids[:, I:I + 1], cnt[:, 2, NE - 1:NE]))
                then(dve.tensor_copy(moe["table"][:, :], ids[0:1, :]))
                for i in range(3):
                    then(dve.tensor_tensor(tmp[:, :, :], one[:, :, :], per(place[:, i, :]), ALU.mult))
                    then(dve.tensor_tensor(tmp2[:, :, :], blk[:, :, :], per(chosen[:, i, :]), ALU.mult))
                    then(dve.tensor_tensor(tmp[:, :, :], tmp[:, :, :], tmp2[:, :, :], ALU.subtract))
                    then(dve.tensor_reduce(moe["slot"][:, i, :], tmp[:, :, :], AX, ALU.add))
                    then(dve.tensor_tensor(tmp[:, :, :], one[:, :, :], per(gate[:, i, :]), ALU.mult))
                    then(dve.tensor_reduce(moe["gate"][:, i, :], tmp[:, :, :], AX, ALU.add))
                then(dve.tensor_scalar(moe["slot"][:, :, :], moe["slot"][:, :, :], -1.0, None, ALU.add))


def stage_experts(k, moe):
    PAIRS = FE // WCOLS
    BLOCKS = 3 * PAIRS
    I = MAX_ITEMS + 1
    slot_of, gate_of, table, tokens = moe["slot"], moe["gate"], moe["table"], moe["tokens"]
    ins = k.ins
    with ExitStack() as s:
        ring = k.sb(s, "moe_ring", [P, MOE_SLOTS, SLOT])
        pick = k.sb(s, "pick", [P, 3, P])
        weigh = k.sb(s, "weigh", [P, 3, P])
        weighT = k.sb(s, "weigh_t", [P, T])
        xg = k.sb(s, "item_tokens", [P, DC, P])
        gated = k.sb(s, "gated", [P, 2, WCOLS])
        hid = k.sb(s, "hid", [P, 2, WCOLS])
        hidT = k.sb(s, "hid_t", [P, FEC, P])
        y = k.sb(s, "item_out", [P, D])
        names = ("free", "pick_ready", "gathered", "xg_low", "xg_high", "silu_done", "hid_done", "hid_turned", "hid_copied",
                 "weigh_turned", "weigh_copied", "y_low", "y_high", "spread", "added")
        n_ = {x: k.count("m_" + x).sem for x in names}
        loaded = [k.count(f"m_loaded{x}").sem for x in range(MOE_SLOTS)]

        def items(eng):
            n = eng.value_load(table[0:1, I:I + 1], min_val=1, max_val=MAX_ITEMS)
            return eng.Fori(0, n)

        with k.stage() as block:
            @block.sync
            def _(sp):
                with items(sp) as i:
                    e = sp.value_load(table[0:1, bass.ds(i, 1)], min_val=0, max_val=NE - 1)
                    for b in range(BLOCKS):
                        sp.wait_ge(n_["free"], i * BLOCKS + (b + 1))
                        if b < 2 * PAIRS:
                            w = ins["we3" if b % 2 else "we1"][0, bass.ds(e, 1)].rearrange("a (c p) f -> p (a c) f", p=P)
                            src = w[:, :, WCOLS * (b // 2):WCOLS * (b // 2) + WCOLS]
                            dst = ring[:, b % MOE_SLOTS, :].rearrange("p (c f) -> p c f", c=DC)
                        else:
                            w = ins["we2"][0, bass.ds(e, 1)].rearrange("a (f p) d -> p (a f) d", p=P)
                            r = b - 2 * PAIRS
                            src = w[:, 4 * r:4 * r + 4, :]
                            dst = ring[:, b % MOE_SLOTS, :].rearrange("p (f d) -> p f d", f=4)
                        sp.dma_start(dst, src).then_inc(loaded[b % MOE_SLOTS], 16)

            @block.tensor
            def _(pe):
                ident = k.const("ident")

                def gather():
                    for c in range(DC):
                        for t, (_, n) in enumerate(TILES):
                            mm = pe.matmul(k.ps[:, 6 + c // 4, P * (c % 4):P * (c % 4) + P], tokens[0:n, t, P * c:P * c + P],
                                           pick[0:n, t, :], start=t == 0, stop=t == 2)
                        if c % 4 == 3:
                            mm.then_inc(n_["gathered"], 1)

                def turn(i, n):
                    pe.wait_ge(n_["hid_done"], i * PAIRS + (n + 1))
                    if n >= 2:
                        pe.wait_ge(n_["hid_copied"], i * PAIRS + (n - 1))
                    for j in range(4):
                        mm = pe.transpose(k.ps[:, 6 + n % 2, P * j:P * j + P], hid[:, n % 2, P * j:P * j + P], ident)
                    mm.then_inc(n_["hid_turned"], 1)

                pe.wait_ge(n_["pick_ready"], 1)
                gather()
                with items(pe) as i:
                    pe.wait_ge(n_["xg_low"], i + 1)
                    pe.wait_ge(n_["xg_high"], i + 1)
                    pe.wait_ge(n_["added"], i * DC + 1)
                    for n in range(PAIRS):
                        if n >= 2:
                            pe.wait_ge(n_["hid_done"], i * PAIRS + (n - 1))
                        for w in range(2):
                            b = 2 * n + w
                            blk = ring[:, b % MOE_SLOTS, :].rearrange("p (c f) -> p c f", c=DC)
                            pe.wait_ge(loaded[b % MOE_SLOTS], i * 48 + 16 * (b // MOE_SLOTS + 1))
                            for c in range(DC):
                                mm = pe.matmul(k.ps[:, 2 * w + n % 2, :], xg[:, c, :], blk[:, c, :], start=c == 0, stop=c == DC - 1)
                            mm.then_inc(n_["free"], 1)
                        if n == 0:
                            for t, (a, m) in enumerate(TILES):
                                mm = pe.transpose(k.ps[:, 4, a:a + m], weigh[0:m, t, :], ident[0:m, 0:m])
                            mm.then_inc(n_["weigh_turned"], 1)
                        else:
                            turn(i, n - 1)
                    turn(i, PAIRS - 1)
                    pe.wait_ge(n_["weigh_copied"], i + 1)
                    for r in range(PAIRS):
                        b = 2 * PAIRS + r
                        blk = ring[:, b % MOE_SLOTS, :].rearrange("p (f d) -> p f d", f=4)
                        pe.wait_ge(n_["hid_copied"], i * PAIRS + (r + 1))
                        pe.wait_ge(loaded[b % MOE_SLOTS], i * 48 + 16 * (b // MOE_SLOTS + 1))
                        for j in range(4):
                            f = 4 * r + j
                            for u in range(2):
                                mm = pe.matmul(k.ps[:, 4 + u, :], hidT[:, f, :], blk[:, j, 512 * u:512 * u + 512],
                                               start=f == 0, stop=f == FEC - 1)
                        mm.then_inc(n_["free"], 1)
                    pe.wait_ge(n_["pick_ready"], i + 2)
                    gather()
                    pe.wait_ge(n_["y_low"], i + 1)
                    pe.wait_ge(n_["y_high"], i + 1)
                    for m in range(DC):
                        if m >= 4:
                            pe.wait_ge(n_["added"], i * DC + (m - 2))
                        pe.matmul(k.ps[:, m % 4, 0:T], y[:, P * m:P * m + P], weighT[:, :], start=True, stop=True)\
                          .then_inc(n_["spread"], 1)

            @block.vector
            def _(dve):
                def picks(col):
                    for t, (_, n) in enumerate(TILES):
                        at = slot_of[0:n, t, col]
                        dve.tensor_scalar(pick[0:n, t, :], k.const("slots")[0:n, :], at, None, ALU.is_equal)
                        ins_ = dve.tensor_scalar(weigh[0:n, t, :], k.const("slots")[0:n, :], at, gate_of[0:n, t, col],
                                                 ALU.is_equal, ALU.mult)
                    ins_.then_inc(n_["pick_ready"], 1)

                dve.sem_inc(n_["added"], 1)
                picks(slice(0, 1))
                dve.wait_ge(n_["gathered"], 2)
                dve.tensor_copy(xg[:, 4:8, :], k.ps[:, 7, :].rearrange("p (c n) -> p c n", c=4)).then_inc(n_["xg_high"], 1)
                with items(dve) as i:
                    for n in range(PAIRS):
                        dve.wait_ge(n_["silu_done"], i * PAIRS + (n + 1))
                        if n >= 2:
                            dve.wait_ge(n_["hid_turned"], i * PAIRS + (n - 1))
                        dve.tensor_tensor(hid[:, n % 2, :], gated[:, n % 2, :], k.ps[:, 2 + n % 2, :], ALU.mult).then_inc(n_["hid_done"], 1)
                        if n == 0:
                            dve.wait_ge(n_["weigh_turned"], i + 1)
                            dve.tensor_copy(weighT[:, :], k.ps[:, 4, 0:T]).then_inc(n_["weigh_copied"], 1)
                    picks(bass.ds(i + 1, 1))
                    dve.wait_ge(n_["free"], i * BLOCKS + (MOE_SLOTS + BLOCKS))
                    dve.tensor_copy(y[:, 512:1024], k.ps[:, 5, :]).then_inc(n_["y_high"], 1)
                    dve.wait_ge(n_["gathered"], i * 2 + 4)
                    dve.tensor_copy(xg[:, 4:8, :], k.ps[:, 7, :].rearrange("p (c n) -> p c n", c=4)).then_inc(n_["xg_high"], 1)
                    for m in range(DC):
                        dve.wait_ge(n_["spread"], i * DC + (m + 1))
                        dve.tensor_tensor(k.residual[:, m, :], k.residual[:, m, :], k.ps[:, m % 4, 0:T], ALU.add).then_inc(n_["added"], 1)

            @block.scalar
            def _(act):
                def take_low(n):
                    act.wait_ge(n_["gathered"], n)
                    act.copy(xg[:, 0:4, :], k.ps[:, 6, :].rearrange("p (c n) -> p c n", c=4)).then_inc(n_["xg_low"], 1)

                def take_hidden(i, n):
                    act.wait_ge(n_["hid_turned"], i * PAIRS + (n + 1))
                    act.copy(hidT[:, 4 * n:4 * n + 4, :], k.ps[:, 6 + n % 2, :].rearrange("p (f n) -> p f n", f=4)).then_inc(n_["hid_copied"], 1)

                take_low(1)
                with items(act) as i:
                    for n in range(PAIRS):
                        act.wait_ge(n_["free"], i * BLOCKS + (MOE_SLOTS + 2 * n + 2))
                        if n >= 2:
                            act.wait_ge(n_["hid_done"], i * PAIRS + (n - 1))
                        act.activation(gated[:, n % 2, :], k.ps[:, n % 2, :], ACT.Silu).then_inc(n_["silu_done"], 1)
                        if n >= 1:
                            take_hidden(i, n - 1)
                    take_hidden(i, PAIRS - 1)
                    act.wait_ge(n_["free"], i * BLOCKS + (MOE_SLOTS + BLOCKS))
                    act.copy(y[:, 0:512], k.ps[:, 4, :]).then_inc(n_["y_low"], 1)
                    take_low(i * 2 + 3)

            @block.gpsimd
            def _(pool):
                pool.sem_inc(n_["free"], MOE_SLOTS)


def stage_store_tokens(k):
    with ExitStack() as s:
        tok = k.sb(s, "out_tokens", [P, 3, D])
        turned, copied, stored = k.count("turned"), (k.count("copied"), k.count("copied_odd")), k.count("out_stored")
        with k.stage() as block:
            @block.tensor
            def _(pe):
                for n in range(6):
                    i, u = n // 2, n % 2
                    a, rows = TILES[i]
                    for c in range(4):
                        mm = pe.transpose(k.ps[0:rows, n, P * c:P * c + P], k.act[:, 4 * u + c, a:a + rows], k.const("ident"))
                    mm.then_inc(*turned.up())

            def copier(eng, u):
                for i in range(3):
                    rows = TILES[i][1]
                    eng.wait_ge(*turned.at(2 * i + u + 1))
                    copy(eng, tok[0:rows, i, 512 * u:512 * u + 512], k.ps[0:rows, 2 * i + u, :]).then_inc(*copied[u].up())

            @block.scalar
            def _(act):
                copier(act, 0)

            @block.vector
            def _(dve):
                copier(dve, 1)

            @block.sync
            def _(sp):
                for i, (a, rows) in enumerate(TILES):
                    for u in range(2):
                        sp.wait_ge(*copied[u].at(i + 1))
                    dst = k.outs[0][0, a:a + rows, :] if i < 2 else k.outs[1].rearrange("b t d -> (b t) d")
                    sp.dma_start(dst, tok[0:rows, i, :]).then_inc(*stored.up(16))
                sp.wait_ge(*stored.at(48))


def program(nc, ins, outs, core, attn):
    with ExitStack() as ctx:
        k = Kernel(nc, ctx, ins, outs, core, attn)
        with ExitStack() as early:
            k.ring = k.sb(early, "ring", [P, EARLY_SLOTS, SLOT])
            stage_load(k)
            stage_norm(k, "norm_mix_even")
            with ExitStack() as s:
                qkv = k.sb(s, "qkv", [P, 24, T])
                kv = k.sb(s, "kv", [P, 3, 2048])
                k.attn = k.sb(s, "attn", [P, k.attn_n])
                stage_qkv(k, qkv)
                stage_kv_tokens(k, qkv, kv)
                for mixer in "AB":
                    stage_prompt_attention(k, mixer, qkv, kv)
                    for group in range(2):
                        stage_sample_attention(k, mixer, group, qkv, kv)
            stage_out_even(k)
            stage_norm(k, "norm_ffn_even")
            with ExitStack() as s:
                hidden = k.sb(s, "hidden", [P, FC, T])
                stage_ffn_up(k, hidden)
                gemm_rows(k, 19, FC, hidden)
            stage_norm(k, "norm_mix_odd")
            with ExitStack() as s:
                mixed_out = k.sb(s, "mixed_out", [P, 12, T])
                proj = k.sb(s, "proj", [P, 24, T])
                xc = k.sb(s, "xc", [P, CC, T])
                dt = k.sb(s, "dt", [HM, T])
                with ExitStack() as c:
                    conv_in = k.sb(c, "conv_in", [P, CC, TP + 3])
                    conv_in_s = k.sb(c, "conv_in_s", [P, CC, NB, NT + 3])
                    stage_in_odd(k, proj, conv_in, conv_in_s, dt)
                    stage_conv(k, conv_in, conv_in_s, xc)
                with ExitStack() as c:
                    hg = {"k": k.sb(c, "one_minus_f", [P, 4, T]), "g": k.sb(c, "log_f_sums", [P, 4, T])}
                    stage_hgrn_gates(k, proj, hg)
                    stage_hgrn(k, proj, hg, mixed_out)
                with ExitStack() as c:
                    dta = {"acum": k.sb(c, "acum", [HM, T]), "wend": k.sb(c, "wend", [HM, T]), "tok": k.sb(c, "dt_tokens", [P, 3, 48]),
                           "skip": k.sb(c, "skip", [P, 8]), "sq": k.act, "rs": k.sb(c, "group_rstd", [P, 4, T])}
                    stage_dt(k, dt, dta)
                    stage_ssd(k, proj, xc, dt, dta, mixed_out)
                gemm_rows(k, 35, 12, mixed_out)
        stage_norm(k, "norm_ffn_odd")
        with ExitStack() as s:
            moe = {"tokens": k.sb(s, "tokens", [P, 3, D]), "slot": k.sb(s, "item_slot", [P, 3, MAX_ITEMS + 1]),
                   "gate": k.sb(s, "item_gate", [P, 3, MAX_ITEMS + 1]), "table": k.sb(s, "item_table", [1, MAX_ITEMS + 2], I32)}
            stage_route(k, moe)
            stage_experts(k, moe)
        stage_norm(k, "norm_final")
        stage_store_tokens(k)


_INS = ['x_prompt', 'x_sample', 'cache_win_k', 'cache_win_v', 'cache_sb_k', 'cache_sb_v', 'page_table',
        'state_hgrn', 'state_ssm', 'state_conv', 'norm_mix_even', 'w_in_even', 'w_out_even', 'sb_bias',
        'norm_ffn_even', 'w1_ffn', 'w3_ffn', 'w2_ffn', 'norm_mix_odd', 'w_in_odd', 'hgrn_lb_logits',
        'hgrn_gain', 'conv_w', 'conv_b', 'dt_bias', 'a_log', 'd_skip', 'ssm_gain', 'w_out_odd',
        'norm_ffn_odd', 'w_router', 'we1', 'we3', 'we2', 'norm_final']
_OUTS = [(1, TP, D), (NB, NT, D), (1, 1, TP, 8, HD), (1, 1, TP, 8, HD), (NB, 1, NT, 8, HD), (NB, 1, NT, 8, HD),
         (1, 1, TP, 8, HD), (1, 1, TP, 8, HD), (NB, 1, NT, 8, HD), (NB, 1, NT, 8, HD),
         (1, 1, HC, P, P), (NB, 1, HC, P, P), (1, 1, HM, 64, 64), (NB, 1, HM, 64, 64), (1, 1, 3, 1536), (NB, 1, 3, 1536)]


def kernel(**inputs):
    import numpy as _np
    import concourse.bacc as _bacc
    from concourse import mybir as _mybir
    from concourse.bass_utils import run_bass_kernel_spmd as _run

    nc = _bacc.Bacc("TRN2", target_bir_lowering=False, num_devices=1)
    core, attn = shape_constants()
    arrays, ins, outs = {}, {}, []
    given = {name: _np.ascontiguousarray(inputs[name]) for name in _INS}
    given["core_tables"] = _np.concatenate(list(core.values()), 1)
    given["attn_tables"] = _np.concatenate(list(attn.values()), 1)
    for name, a in given.items():
        arrays[f"in_{name}_dram"] = a
        ins[name] = nc.dram_tensor(f"in_{name}_dram", a.shape, _mybir.dt.from_np(a.dtype), kind="ExternalInput").ap()
    for i, shape in enumerate(_OUTS):
        outs.append(nc.dram_tensor(f"out_{i}_dram", shape, F32, kind="ExternalOutput").ap())
    program(nc, ins, outs, core, attn)
    r = _run(nc, [arrays], core_ids=[0])
    return tuple(r.results[0][f"out_{i}_dram"] for i in range(len(_OUTS)))
```

```python
from contextlib import ExitStack

import concourse.bass as bass
import numpy as np
from concourse import mybir

F32 = mybir.dt.float32
F32R = mybir.dt.float32r
I32 = mybir.dt.int32
ALU = mybir.AluOpType
ACT = mybir.ActivationFunctionType
AX = mybir.AxisListType.X

P = 128
D = 1024
DC = D // P
TP = 256
NB, NT = 8, 4
TS = NB * NT
T = TP + TS
TILES = ((0, P), (P, P), (TP, TS))
HD = 64
PAST = 256
PAGE = 128
SCALE = HD ** -0.5
NEG = -1.0e30
FF = 2816
FC = FF // P
HC = 4
HM = 16
NE = 8
FE = 3584
FEC = FE // P
EPS = 1e-6
WCOLS = 512
SLOT = DC * WCOLS
EARLY_SLOTS = 3
MOE_SLOTS = 7
MAX_ITEMS = NE + 2 * T // P
DIL_PATTERNS = ((128, 1), (512, 4), (2048, 16))

VEC = {"norm_mix_even": 0, "norm_ffn_even": 8, "norm_mix_odd": 16, "norm_ffn_odd": 24, "norm_final": 32,
       "hgrn_lb_logits": 40, "hgrn_gain": 48, "ssm_gain": 52, "conv_w": 60, "conv_b": 108}
NVEC = 120
CC = 12


def shape_constants():
    p = np.arange(P)
    c = {}
    c["ident"] = np.eye(P)
    c["ones"] = np.ones((P, P))
    run = np.ones(T)
    run[[0] + [TP + NT * b for b in range(NB)]] = 0
    c["running"] = np.tile(run, (P, 1))
    c["before"] = (p[:, None] < p[None, :]) * 1.0
    c["slots"] = np.tile(p, (P, 1))
    c["items"] = np.tile(np.arange(MAX_ITEMS + 1), (P, 1))
    c["valid"] = np.repeat(np.stack([p < n for _, n in TILES], 1), NE, 1) * 1.0
    e = np.arange(NE)
    c["earlier_expert"] = np.tile(((e[None, :] < e[:, None]) * 1.0).reshape(1, -1), (P, 1))
    c["expert_ids"] = np.tile(e, (P, 1))
    c["batch_of"] = (p[:, None] // NT == np.arange(NB)[None, :]) * 1.0
    pair = np.zeros((P, 8, P))
    for h in range(HM):
        pair[h, h // 2, 64 * (h % 2):64 * (h % 2) + 64] = 1
    c["head_pair"] = pair.reshape(P, -1)
    future = np.where(p[:, None] <= p[None, :], 0.0, NEG)
    c["ssd_future"] = np.concatenate([future, np.zeros((P, P))], 1)
    t = np.arange(TS)
    fs = np.full((P, TS), NEG)
    fs[:TS] = np.where((t[:, None] // NT == t[None, :] // NT) & (t[:, None] <= t[None, :]), 0.0, NEG)
    c["ssd_future_s"] = fs
    lv = []
    for l in range(7):
        h = 1 << l
        s, q = p[:, None], p[None, :]
        lv.append((s // (2 * h) == q // (2 * h)) & (s % (2 * h) < h) & (q % (2 * h) >= h))
    c["level"] = np.stack(lv, 1).reshape(P, -1)
    core = {k: np.asarray(v, np.float32) for k, v in c.items()}

    def log_count(dist):
        n = np.zeros(dist.shape)
        for window, dil in DIL_PATTERNS:
            n += (dist >= 0) & (dist <= window) & (dist % dil == 0)
        return np.where(n > 0, np.log(np.maximum(n, 1)), NEG)

    a = {}
    slope = 2.0 ** (-8.0 * np.arange(1, 9) / 8)
    d = p[:, None] + P - np.arange(2 * P)[None, :]
    lc = log_count(d)
    order = [0, 2, 1, 3, 4, 6, 5, 7]
    a["alibi"] = np.stack([np.where(lc > NEG, lc - slope[h] * d, NEG) for h in order], 1).reshape(P, -1)
    a["stick_on"] = (d > 0) * 1.0
    a["stick_off"] = np.where(d > 0, 0.0, NEG)
    key = np.arange(PAST + TS)
    al, on = [], []
    for g in range(2):
        b, h, t = 4 * g + p // 32, (p % 32) // NT, p % NT
        new = key >= PAST
        kb, kt = (key - PAST) // NT, (key - PAST) % NT
        pos = np.where(new, PAST + kt, key)
        dist = PAST + t[:, None] - pos[None, :]
        mine = ~new[None, :] | (kb[None, :] == b[:, None])
        lc = np.where(mine, log_count(dist), NEG)
        al.append(np.where(lc > NEG, lc - slope[h][:, None] * dist, NEG))
        on.append(mine & (dist > 0))
    a["alibi_s"] = np.concatenate(al, 1)
    a["stick_on_s"] = np.concatenate(on, 1) * 1.0
    a["stick_off_s"] = np.where(np.concatenate(on, 1), 0.0, NEG)
    rh = np.zeros((P, P))
    rh[(p % 32) // NT, p] = 1
    a["row_head"] = rh
    attn = {k: np.asarray(v, np.float32) for k, v in a.items()}
    return core, attn


def columns(tables):
    at, out = 0, {}
    for k, v in tables.items():
        out[k] = (at, at + v.shape[1])
        at += v.shape[1]
    return out, at


class Count:

    def __init__(self, sem):
        self.sem, self.total, self.base = sem, 0, 0

    def up(self, by=1):
        self.total += by
        return self.sem, by

    def at(self, n):
        assert self.base + n > 0
        return self.sem, self.base + n

    def all(self):
        return self.sem, self.total


class Kernel:

    def __init__(self, nc, ctx, ins, outs, core, attn):
        self.nc, self.ins, self.outs = nc, ins, outs
        self.ctx = ctx
        self.counts = {}
        self.core_at, self.core_n = columns(core)
        self.attn_at, self.attn_n = columns(attn)
        self.ps = ctx.enter_context(nc.psum_tensor("ps", [P, 8, 512], F32))
        self.residual = self.sb(ctx, "residual", [P, DC, T])
        self.act = self.sb(ctx, "act", [P, DC, T])
        self.core = self.sb(ctx, "core", [P, self.core_n])
        self.vec = self.sb(ctx, "vec", [P, NVEC])
        self.ones_wide = self.sb(ctx, "ones_wide", [P, T])
        self.blocks = self.weight_blocks()
        self.issued, self.landed, self.freed = 0, {}, {}

    def sb(self, ctx, name, shape, dt=F32):
        return ctx.enter_context(self.nc.sbuf_tensor(name, shape, dt))

    def count(self, name):
        if name not in self.counts:
            self.counts[name] = Count(self.ctx.enter_context(self.nc.semaphore(name)))
        return self.counts[name]

    def stage(self):
        for c in self.counts.values():
            c.base = c.total
        return self.nc.Block()

    def const(self, name):
        a, b = self.core_at[name]
        return self.core[:, a:b]

    def table(self, name):
        a, b = self.attn_at[name]
        return self.attn[:, a:b]

    def weight_blocks(self):
        i = self.ins
        cols = lambda w, a, n: (w[0].rearrange("(k p) n -> p k n", p=P)[:, :, a:a + n], "cols", n)
        rows = lambda w, a, n: (w[0].rearrange("(k p) n -> p k n", p=P)[:, a:a + n, :], "rows", n)
        blocks = [cols(i["w_in_even"], WCOLS * n, WCOLS) for n in range(6)]
        blocks += [cols(i["w_out_even"], WCOLS * n, WCOLS) for n in range(2)]
        for n in range(FF // 256):
            blocks.append((n, "pair", 256))
        blocks += [rows(i["w2_ffn"], 4 * n, min(4, FC - 4 * n)) for n in range(-(-FC // 4))]
        blocks += [cols(i["w_in_odd"], WCOLS * n, min(WCOLS, 4624 - WCOLS * n)) for n in range(10)]
        blocks += [rows(i["w_out_odd"], 4 * n, 4) for n in range(3)]
        return blocks

    def slot(self, n, how, width):
        flat = self.ring[:, n % EARLY_SLOTS, :]
        if how == "cols":
            return flat[:, 0:DC * width].rearrange("p (k n) -> p k n", k=DC)
        if how == "rows":
            return flat[:, 0:width * D].rearrange("p (k n) -> p k n", k=width)
        return flat.rearrange("p (k w n) -> p k w n", k=DC, w=2)

    def stream(self, sp, upto):
        for n in range(self.issued, min(upto, len(self.blocks))):
            src, how, width = self.blocks[n]
            if n >= EARLY_SLOTS:
                sp.wait_ge(*self.freed[n - EARLY_SLOTS])
            loaded = self.count(f"block_loaded{n % EARLY_SLOTS}")
            dst = self.slot(n, how, width)
            if how == "pair":
                for w, name in enumerate(("w1_ffn", "w3_ffn")):
                    part = self.ins[name][0].rearrange("(k p) n -> p k n", p=P)[:, :, 256 * src:256 * src + 256]
                    sp.dma_start(dst[:, :, w, :], part).then_inc(*loaded.up(16))
            else:
                sp.dma_start(dst, src).then_inc(*loaded.up(16))
            self.landed[n] = loaded.sem, loaded.total
            self.issued = n + 1

    def arrived(self, n):
        return self.landed[n]


def stage_load(k):
    nc, ins = k.nc, k.ins
    with ExitStack() as s:
        tok = k.sb(s, "tok", [P, 3, D])
        rows = k.sb(s, "rows", [P, P])
        const_in, vec_in, x_in = k.count("const_in"), k.count("vec_in"), k.count("x_in")
        turned, copied = k.count("turned"), k.count("copied")
        with k.stage() as block:
            @block.sync
            def _(sp):
                sp.dma_start(k.core[:, :], ins["core_tables"]).then_inc(*const_in.up(16))
                k.stream(sp, EARLY_SLOTS)

            @block.gpsimd
            def _(pool):
                pool.dma_start(tok[:, 0:2, :], ins["x_prompt"][0].rearrange("(t p) d -> p t d", p=P)).then_inc(*x_in.up(16))
                pool.dma_start(tok[0:TS, 2, :], ins["x_sample"].rearrange("b t d -> (b t) d")).then_inc(*x_in.up(16))
                for name in ("norm_mix_even", "norm_ffn_even", "norm_mix_odd", "norm_ffn_odd", "norm_final",
                             "hgrn_lb_logits", "hgrn_gain", "ssm_gain", "conv_w", "conv_b"):
                    v = ins[name]
                    n = int(np.prod(v.shape)) // P
                    if name == "norm_final":
                        src = v.rearrange("(c q) -> c q", q=P)
                    elif name == "conv_w":
                        src = v[0].rearrange("j (c q) -> (j c) q", q=P)
                    else:
                        src = v.rearrange("a (c q) -> (a c) q", q=P)
                    pool.dma_start(rows[VEC[name]:VEC[name] + n, :], src).then_inc(*vec_in.up(16))

            @block.tensor
            def _(pe):
                pe.wait_ge(*const_in.at(16))
                ident = k.const("ident")
                pe.wait_ge(*x_in.at(32))
                for c in range(DC):
                    if c >= 4:
                        pe.wait_ge(*copied.at(c - 3))
                    for i, (a, n) in enumerate(TILES):
                        mm = pe.transpose(k.ps[:, c % 4, a:a + n], tok[0:n, i, P * c:P * c + P], ident[0:n, 0:n])
                    mm.then_inc(*turned.up())
                pe.wait_ge(*vec_in.at(160))
                pe.transpose(k.ps[:, 4, 0:NVEC], rows[0:NVEC, :], ident[0:NVEC, 0:NVEC]).then_inc(*turned.up())

            @block.vector
            def _(dve):
                dve.memset(k.ones_wide[:, :], 1.0).then_inc(*k.count("ones_set").up())
                for c in range(DC):
                    dve.wait_ge(*turned.at(c + 1))
                    dve.tensor_copy(k.residual[:, c, :], k.ps[:, c % 4, 0:T]).then_inc(*copied.up())
                dve.wait_ge(*turned.at(DC + 1))
                dve.tensor_copy(k.vec[:, :], k.ps[:, 4, 0:NVEC]).then_inc(*copied.up())


def stage_norm(k, gain):
    with ExitStack() as s:
        sq = k.sb(s, f"sq_{gain}", [P, DC, T])
        rstd = k.sb(s, f"rstd_{gain}", [P, T])
        squared, summed, mean, root = (k.count(n) for n in ("squared", "summed", "mean", "root"))
        normed = k.count("normed")
        with k.stage() as block:
            @block.scalar
            def _(act):
                for c in range(DC):
                    act.activation(sq[:, c, :], k.residual[:, c, :], ACT.Square).then_inc(*squared.up())
                act.wait_ge(*mean.at(1))
                act.activation(rstd[:, :], rstd[:, :], ACT.Ln).then_inc(*root.up())
                act.wait_ge(*root.at(1))
                act.activation(rstd[:, :], rstd[:, :], ACT.Exp, scale=-0.5).then_inc(*root.up())

            @block.tensor
            def _(pe):
                for c in range(DC):
                    pe.wait_ge(*squared.at(c + 1))
                    mm = pe.matmul(k.ps[:, 0, 0:T], k.const("ones"), sq[:, c, :], start=c == 0, stop=c == DC - 1)
                mm.then_inc(*summed.up())

            @block.vector
            def _(dve):
                dve.wait_ge(*summed.at(1))
                dve.tensor_scalar(rstd[:, :], k.ps[:, 0, 0:T], 1.0 / D, EPS, ALU.mult, ALU.add).then_inc(*mean.up())
                dve.wait_ge(*root.at(2))
                for c in range(DC):
                    g = VEC[gain] + c
                    dve.scalar_tensor_tensor(k.act[:, c, :], k.residual[:, c, :], k.vec[:, g:g + 1], rstd[:, :],
                                             ALU.mult, ALU.mult).then_inc(*normed.up())


def split(k, s, tag, x, chunks):
    hi, lo = k.sb(s, "x_hi" + tag, [P, chunks, T], F32R), k.sb(s, "x_lo" + tag, [P, chunks, T], F32R)
    rounded, rest = k.count("rounded"), k.count("rest")
    with k.stage() as block:
        @block.scalar
        def _(act):
            for c in range(0, chunks, 2):
                act.copy(hi[:, c:c + 2, :], x[:, c:c + 2, :]).then_inc(*rounded.up())

        @block.vector
        def _(dve):
            for c in range(0, chunks, 2):
                dve.wait_ge(*rounded.at(c // 2 + 1))
                dve.tensor_tensor(lo[:, c:c + 2, :], x[:, c:c + 2, :], hi[:, c:c + 2, :].bitcast(F32), ALU.subtract).then_inc(*rest.up())
    return hi, lo


class Split:

    def __init__(self, k, s, tag, halves, used):
        self.k, self.halves, self.used = k, halves, used
        self.hi = [k.sb(s, f"w_hi{n}{tag}", [P, SLOT // 2], F32R) for n in range(2)]
        self.lo = [k.sb(s, f"w_lo{n}{tag}", [P, SLOT // 2], F32R) for n in range(2)]
        self.hi_done, self.lo_done = k.count("hi_done"), k.count("lo_done")

    def view(self, buf, h):
        a, b = self.halves[h][3]
        return buf[h % 2][:, 0:a * b].rearrange("p (a b) -> p a b", a=a)

    def start(self):
        for h, (n, _, _, _) in enumerate(self.halves):
            self.k.freed[n] = self.lo_done.at(h + 1)

    def round_hi(self, act, h):
        if h >= len(self.halves):
            return
        n, first, raw, _ = self.halves[h]
        if first:
            act.wait_ge(*self.k.arrived(n))
        if h >= 2:
            act.wait_ge(*self.used(h - 2))
        act.copy(self.view(self.hi, h), raw).then_inc(*self.hi_done.up())

    def take_lo(self, dve, h):
        if h >= len(self.halves):
            return
        dve.wait_ge(*self.hi_done.at(h + 1))
        dve.tensor_tensor(self.view(self.lo, h), self.halves[h][2], self.view(self.hi, h).bitcast(F32), ALU.subtract)\
           .then_inc(*self.lo_done.up())

    def products(self, pe, out, h, cols, rows, x, first, last):
        hi, lo = self.view(self.hi, h), self.view(self.lo, h)
        for c, r in enumerate(rows):
            pe.matmul(out, hi[:, c, cols], x[0][:, r, :], start=first and c == 0, stop=False)
            pe.matmul(out, hi[:, c, cols], x[1][:, r, :], start=False, stop=False)
        pe.wait_ge(*self.lo_done.at(h + 1))
        for c, r in enumerate(rows):
            mm = pe.matmul(out, lo[:, c, cols], x[0][:, r, :], start=False, stop=last and c == len(rows) - 1)
        return mm


def gemm(k, tag, first, widths, x, copy_out, by_vector=False):
    done, out = k.count("product_done"), (k.count("even_out"), k.count("odd_out"))
    halves = [(first + n, j == 0, k.slot(first + n, "cols", w)[:, :, 256 * j:256 * j + 256], (DC, 256))
              for n, w in enumerate(widths) for j in range(w // 256)]
    chunks = 2 * len(halves)
    with ExitStack() as s:
        sp_ = Split(k, s, tag, halves, lambda h: done.at(2 * h + 2))
        with k.stage() as block:
            sp_.start()

            @block.sync
            def _(sp):
                k.stream(sp, first + len(widths) + EARLY_SLOTS)

            @block.tensor
            def _(pe):
                for m in range(chunks):
                    h = m // 2
                    if m % 2 == 0:
                        pe.wait_ge(*sp_.hi_done.at(h + 1))
                    if m >= 8:
                        pe.wait_ge(*out[m % 2].at(m // 2 - 3))
                    sp_.products(pe, k.ps[:, m % 8, 0:T], h, slice(P * (m % 2), P * (m % 2) + P), range(DC), x, True, True)\
                       .then_inc(*done.up())

            @block.scalar
            def _(act):
                sp_.round_hi(act, 0)
                sp_.round_hi(act, 1)
                for h in range(len(halves)):
                    if not by_vector:
                        act.wait_ge(*done.at(2 * h + 1))
                        copy_out(act, 2 * h).then_inc(*out[0].up())
                    sp_.round_hi(act, h + 2)

            @block.vector
            def _(dve):
                sp_.take_lo(dve, 0)
                for h in range(len(halves)):
                    sp_.take_lo(dve, h + 1)
                    for m in range(2 * h + (not by_vector), 2 * h + 2):
                        dve.wait_ge(*done.at(m + 1))
                        copy_out(dve, m).then_inc(*out[m % 2].up())


def gemm_rows(k, tag, first, total, x):
    half_done, added = k.count("row_half_done"), k.count("residual_added")
    nblocks = -(-total // 4)
    halves = [(first + n, j == 0, k.slot(first + n, "rows", min(4, total - 4 * n))[:, 2 * j:2 * j + 2, :], (2, D))
              for n in range(nblocks) for j in range(min(4, total - 4 * n) // 2)]
    with ExitStack() as s:
        sp_ = Split(k, s, tag, halves, lambda h: half_done.at(h + 1))
        with k.stage() as block:
            sp_.start()

            @block.sync
            def _(sp):
                k.stream(sp, first + nblocks + EARLY_SLOTS)

            @block.tensor
            def _(pe):
                for h in range(len(halves)):
                    pe.wait_ge(*sp_.hi_done.at(h + 1))
                    for m in range(DC):
                        mm = sp_.products(pe, k.ps[:, m, 0:T], h, slice(P * m, P * m + P), range(2 * h, 2 * h + 2), x,
                                          h == 0, h == len(halves) - 1)
                    mm.then_inc(*half_done.up())

            @block.scalar
            def _(act):
                for h in range(len(halves)):
                    sp_.round_hi(act, h)

            @block.vector
            def _(dve):
                for h in range(len(halves)):
                    sp_.take_lo(dve, h)
                dve.wait_ge(*half_done.at(len(halves)))
                for m in range(DC):
                    dve.tensor_tensor(k.residual[:, m, :], k.residual[:, m, :], k.ps[:, m, 0:T],
                                      ALU.add).then_inc(*added.up())


def copy(eng, out, in_):
    return eng.copy(out, in_) if eng.engine == mybir.EngineType.Activation else eng.tensor_copy(out, in_)



def stage_qkv(k, qkv, x):
    def copy_out(eng, m):
        return copy(eng, qkv[:, m, :], k.ps[:, m % 8, 0:T])
    gemm(k, "_qkv", 0, [WCOLS] * 6, x, copy_out)


def stage_kv_tokens(k, qkv, kv):
    ins, outs = k.ins, k.outs
    jobs = []
    for i, (a, n) in enumerate(TILES):
        for c0 in range(0, 16, 4):
            parts = [(qkv[:, 8 + c0 + c, a:a + n], None) for c in range(4)]
            jobs.append((i, n, c0, parts))
    turned, copied = k.count("turned"), (k.count("copied"), k.count("copied_odd"))
    stored = k.count("stored")
    with k.stage() as block:
        @block.sync
        def _(sp):
            sp.dma_start(k.attn[:, :], ins["attn_tables"]).then_inc(*k.count("tables_in").up(16))
            sp.wait_ge(*k.count("tables_in").at(16))

        @block.tensor
        def _(pe):
            for j, (i, n, c0, parts) in enumerate(jobs):
                if j >= 8:
                    pe.wait_ge(*copied[j % 2].at((j - 8) // 2 + 1))
                for c, (in_, _) in enumerate(parts):
                    mm = pe.transpose(k.ps[0:n, j % 8, P * c:P * c + P], in_, k.const("ident"))
                mm.then_inc(*turned.up())

        def copier(eng, odd):
            for j, (i, n, c0, parts) in enumerate(jobs):
                if j % 2 == odd:
                    eng.wait_ge(*turned.at(j + 1))
                    copy(eng, kv[0:n, i, P * c0:P * c0 + 4 * P], k.ps[0:n, j % 8, :]).then_inc(*copied[odd].up())

        @block.scalar
        def _(act):
            copier(act, 0)

        @block.vector
        def _(dve):
            copier(dve, 1)

        @block.gpsimd
        def _(pool):
            pool.wait_ge(*copied[0].at(len(jobs) // 2))
            pool.wait_ge(*copied[1].at(len(jobs) // 2))
            for n, (out_p, out_s, col) in enumerate(((2, 4, 0), (3, 5, 1024), (6, 8, 512), (7, 9, 1536))):
                pool.dma_start(outs[out_p][0, 0].rearrange("(i p) h d -> p i (h d)", p=P),
                               kv[:, 0:2, col:col + 512]).then_inc(*stored.up(16))
                pool.dma_start(outs[out_s].rearrange("b a t h d -> (b a t) (h d)"),
                               kv[0:TS, 2, col:col + 512]).then_inc(*stored.up(16))
            pool.wait_ge(*stored.all())


def stage_prompt_attention(k, mixer, qkv, kv):
    A = mixer == "A"
    off = 0 if A else 4
    steps = [(t, g) for t in range(2) for g in range(2)]
    with ExitStack() as s:
        z = k.sb(s, f"z{mixer}", [P, 4, 2 * P])
        prob = k.sb(s, f"prob{mixer}", [P, 4, 2 * P])
        probT = k.sb(s, f"probT{mixer}", [P, 2, 4, P])
        stat = k.sb(s, f"stat{mixer}", [P, 12])
        if not A:
            soft = k.sb(s, "soft", [P, 4, 2 * P])
            run = k.sb(s, "run", [P, 4, 2 * P])
            bias = k.sb(s, "stick_bias", [P, 8])
            bias_in = k.count("bias_in")
        scored, taken, peaked, exped, weighed, turned, copied, mixed, out = (k.count(n) for n in (
            "scored", "scores_taken", "peaked", "exped", "weighed", "turned", "copied", "mixed", "mixed_out"))
        z_ready, softened, shifted = (k.count(n) for n in ("z_ready", "softened", "shifted"))
        act_step, dve_step = k.count("act_step"), k.count("dve_step")
        with k.stage() as block:
            if not A:
                @block.gpsimd
                def _(pool):
                    pool.dma_start(bias[:, :], k.ins["sb_bias"].broadcast_to([P, 8])).then_inc(*bias_in.up(16))

            @block.tensor
            def _(pe):
                def scores(i):
                    t, g = steps[i]
                    if i >= 2:
                        pe.wait_ge(*taken.at(i - 1))
                    for j in range(4):
                        c, r = off + 2 * g + j % 2, HD * (j // 2)
                        mm = pe.matmul(k.ps[:, 2 * (i % 2) + j // 2, 256 * (j % 2):256 * (j % 2) + P * (t + 1)],
                                       qkv[r:r + HD, c, P * t:P * t + P], qkv[r:r + HD, 8 + c, 0:P * (t + 1)],
                                       start=True, stop=True)
                    mm.then_inc(*scored.up())

                scores(0)
                for i, (t, g) in enumerate(steps):
                    if i + 1 < len(steps):
                        scores(i + 1)
                    pe.wait_ge(*weighed.at(i + 1))
                    for kt in range(t + 1):
                        for j in range(4):
                            mm = pe.transpose(k.ps[:, 4 + kt, P * j:P * j + P], prob[:, j, P * kt:P * kt + P],
                                              k.const("ident"))
                    mm.then_inc(*turned.up())
                    pe.wait_ge(*copied.at(i + 1))
                    if i >= 2:
                        pe.wait_ge(*out.at(i - 1))
                    for j in range(4):
                        h, r = 2 * (off + 2 * g + j % 2) + j // 2, HD * (j // 2)
                        for kt in range(t + 1):
                            mm = pe.matmul(k.ps[r:r + HD, 6 + i % 2, P * (j % 2):P * (j % 2) + P],
                                           kv[:, kt, 1024 + HD * h:1024 + HD * h + HD], probT[:, kt, j, :],
                                           start=kt == 0, stop=kt == t)
                    mm.then_inc(*mixed.up())

            @block.vector
            def _(dve):
                def then(ins, sig=dve_step):
                    ins.then_inc(*sig.up())
                    dve.wait_ge(*sig.all())

                for i, (t, g) in enumerate(steps):
                    W, x0 = P * (t + 1), P * (1 - t)
                    zz, pp = z[:, :, 0:W], prob[:, :, 0:W]
                    raw = k.ps[:, 2 * (i % 2):2 * (i % 2) + 2, :].rearrange("p a (b n) -> p (a b) n", b=2)[:, :, 0:W]
                    dve.wait_ge(*scored.at(i + 1))
                    if A:
                        tab = k.table("alibi").rearrange("p (h n) -> p h n", h=8)[:, 4 * g:4 * g + 4, x0:2 * P]
                        then(dve.scalar_tensor_tensor(zz, raw, SCALE, tab, ALU.mult, ALU.add), taken)
                        dve.tensor_reduce(stat[:, 0:4], zz, AX, ALU.max, negate=True).then_inc(*peaked.up())
                        dve.wait_ge(*exped.at(i + 1))
                        then(dve.reciprocal(stat[:, 8:12], stat[:, 4:8]))
                        dve.tensor_tensor(pp, pp, stat[:, 8:12].unsqueeze(2).broadcast_to([P, 4, W]),
                                          ALU.mult).then_inc(*weighed.up())
                    else:
                        if i == 0:
                            dve.wait_ge(*bias_in.at(16))
                        else:
                            dve.wait_ge(*weighed.at(i))
                        ss = soft[:, :, 0:W]
                        on = k.table("stick_on")[:, x0:2 * P].unsqueeze(1).broadcast_to([P, 4, W])
                        offm = k.table("stick_off")[:, x0:2 * P].unsqueeze(1).broadcast_to([P, 4, W])
                        b = bias[:, 4 * g:4 * g + 4].rearrange("p (q a) -> p a q", a=2).unsqueeze(3).broadcast_to([P, 2, 2, W])
                        z4 = z[:, :, :].rearrange("p (a q) n -> p a q n", a=2)[:, :, :, 0:W]
                        then(dve.tensor_scalar(zz, raw, SCALE, None, ALU.mult), taken)
                        dve.tensor_tensor(z4, z4, b, ALU.add).then_inc(*z_ready.up())
                        dve.wait_ge(*softened.at(i + 1))
                        then(dve.scalar_tensor_tensor(ss, zz, 0.0, ss, ALU.max, ALU.add))
                        then(dve.tensor_tensor(ss, ss, on, ALU.mult))
                        for j in range(4):
                            then(dve.tensor_tensor_scan(run[:, j, 0:W][:, ::-1], k.ones_wide[:, 0:W],
                                                        soft[:, j, 0:W][:, ::-1], 0.0, ALU.mult, ALU.add))
                        then(dve.tensor_tensor(zz, zz, run[:, :, 0:W], ALU.subtract))
                        dve.tensor_tensor(zz, zz, offm, ALU.add).then_inc(*shifted.up())
                    dve.wait_ge(*turned.at(i + 1))
                    if t:
                        then(dve.tensor_copy(probT[:, 1, :, :], k.ps[:, 5, :].rearrange("p (h n) -> p h n", h=4)))
                    dve.tensor_copy(probT[:, 0, :, :], k.ps[:, 4, :].rearrange("p (h n) -> p h n", h=4)).then_inc(*copied.up())
                    dve.wait_ge(*mixed.at(i + 1))
                    dve.tensor_copy(k.act[:, off + 2 * g:off + 2 * g + 2, P * t:P * t + P],
                                    k.ps[:, 6 + i % 2, 0:2 * P].rearrange("p (c n) -> p c n", c=2)).then_inc(*out.up())

            @block.scalar
            def _(act):
                def then(ins, sig=act_step):
                    ins.then_inc(*sig.up())
                    act.wait_ge(*sig.all())

                for i, (t, g) in enumerate(steps):
                    W = P * (t + 1)
                    if A:
                        act.wait_ge(*peaked.at(i + 1))
                        if i >= 1:
                            act.wait_ge(*turned.at(i))
                        for j in range(4):
                            ins = act.activation(prob[:, j, 0:W], z[:, j, 0:W], ACT.Exp, bias=stat[:, j:j + 1],
                                                 accum_out=stat[:, 4 + j:5 + j])
                        ins.then_inc(*exped.up())
                    else:
                        act.wait_ge(*z_ready.at(i + 1))
                        then(act.activation(soft[:, :, 0:W], z[:, :, 0:W], ACT.Abs))
                        then(act.activation(soft[:, :, 0:W], soft[:, :, 0:W], ACT.Exp, scale=-1.0))
                        act.activation(soft[:, :, 0:W], soft[:, :, 0:W], ACT.Ln, bias=1.0).then_inc(*softened.up())
                        act.wait_ge(*shifted.at(i + 1))
                        if i >= 1:
                            act.wait_ge(*turned.at(i))
                        act.activation(prob[:, :, 0:W], z[:, :, 0:W], ACT.Exp).then_inc(*weighed.up())


def stage_sample_attention(k, mixer, group, qkv, kv):
    A = mixer == "A"
    off = 0 if A else 4
    W = PAST + TS
    with ExitStack() as s:
        tag = f"{mixer}{group}"
        keys = k.sb(s, "keys" + tag, [P, 4, 2, 4 * P])
        vals = k.sb(s, "vals" + tag, [P, 4, 2, 4 * P])
        keysT = k.sb(s, "keysT" + tag, [P, 2, 4, PAST])
        qbd = k.sb(s, "qbd" + tag, [P, 4, 4, 32])
        z = k.sb(s, "zs" + tag, [P, W])
        prob = k.sb(s, "probs" + tag, [P, W])
        probT = k.sb(s, "probTs" + tag, [P, 3, P])
        stat = k.sb(s, "stats" + tag, [P, 4])
        keys_in, vals_in, pages_in, bias_in = (k.count(n) for n in ("keys_in", "vals_in", "pages_in", "row_bias_in"))
        placed, scored, peaked, exped, weighed, turned, copied, mixed, out = (k.count(n) for n in (
            "placed", "scored", "peaked", "exped", "weighed", "turned", "copied", "mixed", "mixed_out"))
        keys_turned, keys_copied = k.count("keys_turned"), (k.count("keys_copied_act"), k.count("keys_copied_dve"))
        z_ready, softened, shifted, zeroed = (k.count(n) for n in ("z_ready", "softened", "shifted", "zeroed"))
        act_step, dve_step = k.count("act_step"), k.count("dve_step")
        if not A:
            soft = k.sb(s, "softs" + tag, [P, W])
            run = k.sb(s, "runs" + tag, [P, W])
            bias8 = k.sb(s, "bias8" + tag, [8, 1])
            pages = k.sb(s, "pages" + tag, [1, NB * 2], I32)
            biased = k.count("row_bias")
        with k.stage() as block:
            @block.sync
            def _(sp):
                if A:
                    for name, dst, landed in (("cache_win_k", keys, keys_in), ("cache_win_v", vals, vals_in)):
                        for b in range(4):
                            sp.dma_start(dst[:, b, :, :], k.ins[name][4 * group + b, 0].rearrange(
                                "(j p) h d -> p j (h d)", p=P)).then_inc(*landed.up(16))
                else:
                    sp.dma_start(pages[:, :], k.ins["page_table"].rearrange("b j -> (b j)").unsqueeze(0)).then_inc(*pages_in.up(16))
                    sp.dma_start(bias8[:, :], k.ins["sb_bias"].rearrange("a h -> h a")).then_inc(*bias_in.up(16))
                    sp.wait_ge(*pages_in.at(16))
                    at = [sp.value_load(pages[0:1, n:n + 1], min_val=0, max_val=k.ins["cache_sb_k"].shape[0] - 1)
                          for n in range(8 * group, 8 * group + 8)]
                    for name, dst, landed in (("cache_sb_k", keys, keys_in), ("cache_sb_v", vals, vals_in)):
                        for n in range(8):
                            page = k.ins[name][bass.ds(at[n], 1), 0].rearrange("a p h d -> p (a h d)")
                            sp.dma_start(dst[:, n // 2, n % 2, :], page).then_inc(*landed.up(16))

            @block.tensor
            def _(pe):
                ident = k.const("ident")
                if not A:
                    pe.wait_ge(*bias_in.at(16))
                    pe.matmul(k.ps[:, 7, 0:1], k.table("row_head")[0:8, :], bias8[:, :], start=True, stop=True).then_inc(*biased.up())
                pe.wait_ge(*keys_in.all())
                pe.wait_ge(*placed.at(2))

                def turn_keys(b):
                    for u in range(2):
                        if b >= 2:
                            pe.wait_ge(*keys_copied[u].at(b - 1))
                        for j in range(2):
                            for c in range(2):
                                mm = pe.transpose(k.ps[:, 2 * (b % 2) + u, PAST * c + P * j:PAST * c + P * j + P],
                                                  keys[:, b, j, P * (2 * u + c):P * (2 * u + c) + P], ident)
                        mm.then_inc(*keys_turned.up())

                turn_keys(0)
                for b in range(4):
                    if b < 3:
                        turn_keys(b + 1)
                    for u in range(2):
                        pe.wait_ge(*keys_copied[u].at(b + 1))
                    for part in range(2):
                        for c in range(4):
                            rhs = keysT[:, b % 2, c, :] if part == 0 else qkv[:, 8 + off + c, TP:T]
                            mm = pe.matmul(k.ps[32 * b:32 * b + 32, 4, PAST * part:PAST * part + rhs.shape[1]],
                                           qbd[:, c, b, :], rhs, start=c == 0, stop=c == 3)
                    mm.then_inc(*scored.up())
                pe.wait_ge(*weighed.at(1))
                for j, (a, n) in enumerate(TILES):
                    mm = pe.transpose(k.ps[0:n, 5, P * j:P * j + P], prob[:, a:a + n], ident)
                mm.then_inc(*turned.up())
                pe.wait_ge(*vals_in.all())
                pe.wait_ge(*copied.at(1))
                for b in range(4):
                    for c in range(4):
                        for j in range(3):
                            lhs = vals[:, b, j, P * c:P * c + P] if j < 2 else \
                                kv[0:TS, 2, 1024 + P * (off + c):1024 + P * (off + c) + P]
                            rhs = probT[0:TILES[j][1], j, 32 * b + 8 * c:32 * b + 8 * c + 8]
                            mm = pe.matmul(k.ps[:, 6, 32 * c + 8 * b:32 * c + 8 * b + 8], lhs, rhs,
                                           start=j == 0, stop=j == 2)
                mm.then_inc(*mixed.up())

            @block.vector
            def _(dve):
                def then(ins, sig=dve_step):
                    ins.then_inc(*sig.up())
                    dve.wait_ge(*sig.all())

                then(dve.memset(qbd[:, :, :, :], 0.0), zeroed)
                for r in range(2):
                    for c in range(4):
                        dst = qbd[HD * r:HD * r + HD, c, :, 4 * (2 * c + r):4 * (2 * c + r) + 4]
                        src = qkv[HD * r:HD * r + HD, off + c, TP + 16 * group:TP + 16 * group + 16]
                        ins = dve.tensor_copy(dst, src.rearrange("p (b t) -> p b t", t=NT))
                    ins.then_inc(*placed.up())
                for b in range(4):
                    dve.wait_ge(*keys_turned.at(2 * b + 2))
                    if b >= 2:
                        dve.wait_ge(*scored.at(b - 1))
                    dve.tensor_copy(keysT[:, b % 2, 2:4, :], k.ps[:, 2 * (b % 2) + 1, :].rearrange("p (c n) -> p c n", c=2))\
                       .then_inc(*keys_copied[1].up())
                dve.wait_ge(*scored.at(4))
                raw = k.ps[:, 4, 0:W]
                part = lambda name: k.table(name)[:, W * group:W * group + W]
                if A:
                    then(dve.scalar_tensor_tensor(z[:, :], raw, SCALE, part("alibi_s"), ALU.mult, ALU.add))
                    dve.tensor_reduce(stat[:, 0:1], z[:, :], AX, ALU.max, negate=True).then_inc(*peaked.up())
                    dve.wait_ge(*exped.at(1))
                    then(dve.reciprocal(stat[:, 2:3], stat[:, 1:2]))
                    dve.tensor_scalar(prob[:, :], prob[:, :], stat[:, 2:3], None, ALU.mult).then_inc(*weighed.up())
                else:
                    dve.wait_ge(*biased.at(1))
                    then(dve.tensor_copy(stat[:, 3:4], k.ps[:, 7, 0:1]))
                    dve.tensor_scalar(z[:, :], raw, SCALE, stat[:, 3:4], ALU.mult, ALU.add).then_inc(*z_ready.up())
                    dve.wait_ge(*softened.at(1))
                    then(dve.scalar_tensor_tensor(soft[:, :], z[:, :], 0.0, soft[:, :], ALU.max, ALU.add))
                    then(dve.tensor_tensor(soft[:, :], soft[:, :], part("stick_on_s"), ALU.mult))
                    then(dve.tensor_tensor_scan(run[:, ::-1], k.ones_wide[:, :], soft[:, ::-1], 0.0, ALU.mult, ALU.add))
                    then(dve.tensor_tensor(z[:, :], z[:, :], run[:, :], ALU.subtract))
                    dve.tensor_tensor(z[:, :], z[:, :], part("stick_off_s"), ALU.add).then_inc(*shifted.up())
                dve.wait_ge(*turned.at(1))
                then(dve.tensor_copy(probT[:, 0:2, :], k.ps[:, 5, 0:2 * P].rearrange("p (j n) -> p j n", j=2)))
                dve.tensor_copy(probT[0:TS, 2, :], k.ps[0:TS, 5, 2 * P:3 * P]).then_inc(*copied.up())
                dve.wait_ge(*mixed.at(1))
                for r in range(2):
                    src = k.ps[HD * r:HD * r + HD, 6, 0:P].rearrange("p (c b u t) -> p c b u t", c=4, b=4, u=2)[:, :, :, r, :]
                    dst = k.act[HD * r:HD * r + HD, off:off + 4, TP + 16 * group:TP + 16 * group + 16]
                    dve.tensor_copy(dst.rearrange("p c (b t) -> p c b t", t=NT), src).then_inc(*out.up())

            @block.scalar
            def _(act):
                for b in range(4):
                    act.wait_ge(*keys_turned.at(2 * b + 1))
                    if b >= 2:
                        act.wait_ge(*scored.at(b - 1))
                    act.copy(keysT[:, b % 2, 0:2, :], k.ps[:, 2 * (b % 2), :].rearrange("p (c n) -> p c n", c=2))\
                       .then_inc(*keys_copied[0].up())
                if A:
                    act.wait_ge(*peaked.at(1))
                    act.activation(prob[:, :], z[:, :], ACT.Exp, bias=stat[:, 0:1], accum_out=stat[:, 1:2]).then_inc(*exped.up())
                else:
                    act.wait_ge(*z_ready.at(1))
                    act.activation(soft[:, :], z[:, :], ACT.Abs).then_inc(*act_step.up())
                    act.wait_ge(*act_step.all())
                    act.activation(soft[:, :], soft[:, :], ACT.Exp, scale=-1.0).then_inc(*act_step.up())
                    act.wait_ge(*act_step.all())
                    act.activation(soft[:, :], soft[:, :], ACT.Ln, bias=1.0).then_inc(*softened.up())
                    act.wait_ge(*shifted.at(1))
                    act.activation(prob[:, :], z[:, :], ACT.Exp).then_inc(*weighed.up())


def stage_out_even(k, x):
    def copy_out(eng, m):
        return eng.tensor_tensor(k.residual[:, m, :], k.residual[:, m, :], k.ps[:, m, 0:T], ALU.add)
    gemm(k, "_out_even", 6, [WCOLS] * 2, x, copy_out, by_vector=True)



def stage_ffn_up(k, x, hidden_hi, hidden_lo):
    first = 8
    pair_done, gated, made, rounded, rest = (k.count(n) for n in ("pair_done", "gated", "hidden_made", "rounded", "rest"))
    halves = [(first + m // 2, m % 2 == 0, k.slot(first + m // 2, "pair", 256)[:, :, :, P * (m % 2):P * (m % 2) + P], (2 * DC, P))
              for m in range(FC)]
    halves = [(n, f, raw.rearrange("p k w n -> p (k w) n"), shape) for n, f, raw, shape in halves]
    with ExitStack() as s:
        gate = [k.sb(s, f"gate{n}", [P, T]) for n in range(2)]
        full = [k.sb(s, f"hidden_full{n}", [P, T]) for n in range(2)]
        sp_ = Split(k, s, "_up", halves, lambda h: pair_done.at(h + 1))
        with k.stage() as block:
            sp_.start()

            @block.sync
            def _(sp):
                k.stream(sp, first + FC // 2 + EARLY_SLOTS)

            @block.tensor
            def _(pe):
                for m in range(FC):
                    pe.wait_ge(*sp_.hi_done.at(m + 1))
                    if m >= 4:
                        pe.wait_ge(*made.at(m - 3))
                    hi, lo = (sp_.view(b, m).rearrange("p (c w) n -> p c w n", w=2) for b in (sp_.hi, sp_.lo))
                    outs = [k.ps[:, 2 * (m % 4) + w, 0:T] for w in range(2)]
                    for w in range(2):
                        for c in range(DC):
                            pe.matmul(outs[w], hi[:, c, w, :], x[0][:, c, :], start=c == 0, stop=False)
                            pe.matmul(outs[w], hi[:, c, w, :], x[1][:, c, :], start=False, stop=False)
                    pe.wait_ge(*sp_.lo_done.at(m + 1))
                    for w in range(2):
                        for c in range(DC):
                            mm = pe.matmul(outs[w], lo[:, c, w, :], x[0][:, c, :], start=False, stop=c == DC - 1)
                    mm.then_inc(*pair_done.up())

            @block.scalar
            def _(act):
                sp_.round_hi(act, 0)
                sp_.round_hi(act, 1)
                for m in range(FC):
                    act.wait_ge(*pair_done.at(m + 1))
                    if m >= 2:
                        act.wait_ge(*made.at(m - 1))
                    act.activation(gate[m % 2][:, :], k.ps[:, 2 * (m % 4), 0:T], ACT.Silu).then_inc(*gated.up())
                    sp_.round_hi(act, m + 2)
                    act.wait_ge(*made.at(m + 1))
                    act.copy(hidden_hi[:, m, :], full[m % 2][:, :]).then_inc(*rounded.up())

            @block.vector
            def _(dve):
                def take_rest(m):
                    dve.wait_ge(*rounded.at(m + 1))
                    dve.tensor_tensor(hidden_lo[:, m, :], full[m % 2][:, :], hidden_hi[:, m, :].bitcast(F32), ALU.subtract)\
                       .then_inc(*rest.up())
                sp_.take_lo(dve, 0)
                for m in range(FC):
                    sp_.take_lo(dve, m + 1)
                    if m >= 1:
                        take_rest(m - 1)
                    if m >= 2:
                        dve.wait_ge(*rest.at(m - 1))
                    dve.wait_ge(*gated.at(m + 1))
                    dve.tensor_tensor(full[m % 2][:, :], gate[m % 2][:, :], k.ps[:, 2 * (m % 4) + 1, 0:T],
                                      ALU.mult).then_inc(*made.up())
                take_rest(FC - 1)



Q, F_, V, G, Z, X, DT = 0, 4, 8, 12, 16, 24, 36


def stage_in_odd(k, x, proj, conv_in, conv_in_s, dt):
    first = 25
    done, out = k.count("product_done"), (k.count("even_out"), k.count("odd_out"))
    halves = [(first + n, j == 0, k.slot(first + n, "cols", WCOLS)[:, :, 256 * j:256 * j + 256], (DC, 256))
              for n in range(9) for j in range(2)]
    silus = set(range(Q, Q + 4)) | set(range(G, G + 4)) | set(range(Z, Z + 8))
    on_act = [m for m in range(37) if m in silus or m % 4 == 1 and m < 36]
    on_dve = [m for m in range(37) if m not in on_act]
    past_in, past_turned = k.count("past_in"), k.count("past_turned")
    past = k.count("past_placed")
    with ExitStack() as s:
        old = k.sb(s, "old_conv", [NB * 3, CC * P])
        sp_ = Split(k, s, "_in_odd", halves, lambda h: done.at(2 * h + 2))
        with k.stage() as block:
            sp_.start()
            k.freed[first + 9] = done.at(DT + 1)

            def place(m):
                return out[0].at(on_act.index(m) + 1) if m in on_act else out[1].at(on_dve.index(m) + 1)

            @block.sync
            def _(sp):
                k.stream(sp, first + 10 + EARLY_SLOTS)

            @block.gpsimd
            def _(pool):
                pool.dma_start(old[:, :], k.ins["state_conv"].rearrange("b a r c -> (b a r) c")).then_inc(*past_in.up(16))
                pool.memset(conv_in[:, :, 0:3], 0.0).then_inc(*k.count("past_zeroed").up())

            @block.tensor
            def _(pe):
                pe.wait_ge(*past_in.at(16))
                for c in range(CC):
                    mm = pe.transpose(k.ps[:, 7, 24 * c:24 * c + 24], old[:, P * c:P * c + P], k.const("ident")[0:24, 0:24])
                mm.then_inc(*past_turned.up())
                for m in range(DT + 1):
                    if m >= 7:
                        pe.wait_ge(*place(m - 7))
                    if m < DT:
                        if m % 2 == 0:
                            pe.wait_ge(*sp_.hi_done.at(m // 2 + 1))
                        mm = sp_.products(pe, k.ps[:, m % 7, 0:T], m // 2, slice(P * (m % 2), P * (m % 2) + P), range(DC), x, True, True)
                    else:
                        pe.wait_ge(*k.arrived(first + 9))
                        slot = k.slot(first + 9, "cols", HM)
                        for c in range(DC):
                            mm = pe.matmul(k.ps[0:HM, m % 7, 0:T], slot[:, c, :], k.act[:, c, :], start=c == 0, stop=c == DC - 1)
                    mm.then_inc(*done.up())

            def leave(eng, m):
                bank = k.ps[:, m % 7, :]
                if m in silus:
                    dst = proj[:, m, :]
                    return eng.activation(dst, bank[:, 0:T], ACT.Silu)
                if m < X:
                    return copy(eng, proj[:, m, :], bank[:, 0:T])
                if m < DT:
                    copy(eng, conv_in_s[:, m - X, :, 3:3 + NT], bank[:, TP:T].rearrange("p (b t) -> p b t", t=NT))\
                        .then_inc(*k.count("new_placed").up())
                    return copy(eng, conv_in[:, m - X, 3:3 + TP], bank[:, 0:TP])
                return copy(eng, dt[:, :], bank[0:HM, 0:T])

            @block.scalar
            def _(act):
                sp_.round_hi(act, 0)
                sp_.round_hi(act, 1)
                for h in range(19):
                    for m in (2 * h, 2 * h + 1):
                        if m in on_act:
                            act.wait_ge(*done.at(m + 1))
                            leave(act, m).then_inc(*out[0].up())
                    sp_.round_hi(act, h + 2)

            @block.vector
            def _(dve):
                dve.wait_ge(*past_turned.at(1))
                dve.tensor_copy(conv_in_s[:, :, :, 0:3],
                                k.ps[:, 7, 0:24 * CC].rearrange("p (c b r) -> p c b r", c=CC, r=3)).then_inc(*past.up())
                sp_.take_lo(dve, 0)
                for h in range(19):
                    sp_.take_lo(dve, h + 1)
                    for m in (2 * h, 2 * h + 1):
                        if m in on_dve:
                            dve.wait_ge(*done.at(m + 1))
                            leave(dve, m).then_inc(*out[1].up())


def stage_hgrn_gates(k, proj, hg):
    act_step, dve_step = k.count("act_step"), k.count("dve_step")
    with ExitStack() as s:
        lb = k.sb(s, "lb", [P, 20])
        sig = k.sb(s, "sig", [P, 4, T])
        neg = k.sb(s, "neg", [P, 4, T])
        f = proj[:, F_:F_ + 4, :]
        lm, le, lr = k.count("lb_max"), k.count("lb_exp"), k.count("lb_done")
        expn, expp, gated, logged = (k.count(n) for n in ("exp_minus_f", "exp_f", "forget", "log_forget"))
        with k.stage() as block:
            @block.vector
            def _(dve):
                def then(ins, sig_=dve_step):
                    ins.then_inc(*sig_.up())
                    dve.wait_ge(*sig_.all())
                l0, l1 = k.vec[:, 40:44], k.vec[:, 44:48]
                then(dve.tensor_tensor(lb[:, 0:4], l0, l1, ALU.max))
                then(dve.tensor_tensor(lb[:, 4:8], l0, lb[:, 0:4], ALU.subtract))
                dve.tensor_tensor(lb[:, 8:12], l1, lb[:, 0:4], ALU.subtract).then_inc(*lm.up())
                dve.wait_ge(*le.at(1))
                then(dve.tensor_tensor(lb[:, 12:16], lb[:, 4:8], lb[:, 8:12], ALU.add))
                then(dve.reciprocal(lb[:, 12:16], lb[:, 12:16]))
                then(dve.tensor_tensor(lb[:, 0:4], lb[:, 8:12], lb[:, 12:16], ALU.mult))
                then(dve.tensor_tensor(lb[:, 16:20], lb[:, 4:8], lb[:, 12:16], ALU.mult))
                low, rest = lb[:, 0:4], lb[:, 16:20]
                wide = lambda v: v.unsqueeze(2).broadcast_to([P, 4, T])
                dve.wait_ge(*expn.at(1))
                then(dve.tensor_scalar(sig[:, :, :], sig[:, :, :], 1.0, None, ALU.add))
                then(dve.reciprocal(sig[:, :, :], sig[:, :, :]))
                then(dve.tensor_tensor(sig[:, :, :], sig[:, :, :], wide(rest), ALU.mult))
                dve.tensor_tensor(sig[:, :, :], sig[:, :, :], wide(low), ALU.add).then_inc(*gated.up())
                dve.wait_ge(*expp.at(1))
                then(dve.tensor_scalar(neg[:, :, :], neg[:, :, :], 1.0, None, ALU.add))
                then(dve.reciprocal(neg[:, :, :], neg[:, :, :]))
                then(dve.tensor_tensor(hg["k"][:, :, :], neg[:, :, :], wide(rest), ALU.mult))
                dve.wait_ge(*logged.at(1))
                for c in range(4):
                    then(dve.tensor_tensor_scan(hg["g"][:, c, :], k.const("running"), sig[:, c, :], 0.0, ALU.mult, ALU.add))

            @block.scalar
            def _(act):
                act.wait_ge(*lm.at(1))
                act.activation(lb[:, 4:12], lb[:, 4:12], ACT.Exp).then_inc(*le.up())
                act.activation(sig[:, :, :], f, ACT.Exp, scale=-1.0).then_inc(*expn.up())
                act.activation(neg[:, :, :], f, ACT.Exp).then_inc(*expp.up())
                act.wait_ge(*gated.at(1))
                act.activation(sig[:, :, :], sig[:, :, :], ACT.Ln).then_inc(*logged.up())


def stage_hgrn(k, proj, hg, mixed_out):
    q, v, gate = proj[:, Q:Q + 4, :], proj[:, V:V + 4, :], proj[:, G:G + 4, :]
    kk, g = hg["k"], hg["g"]
    levels = [1 << l for l in range(8)]
    act_step, dve_step = k.count("act_step"), k.count("dve_step")
    with ExitStack() as s:
        X2 = [k.act[:, 4 * n:4 * n + 4, :] for n in range(2)]
        att = k.sb(s, "att", [P, 2, 4, P])
        attx = k.sb(s, "attx", [P, 4, P])
        atts = k.sb(s, "atts", [TS, 4, TS])
        vt = k.sb(s, "v_tokens", [P, 3, 4 * P])
        kd = k.sb(s, "k_decayed", [P, 4, T])
        kdt = k.sb(s, "kd_tokens", [P, 3, 4 * P])
        qe = k.sb(s, "q_decayed", [P, 4, TS])
        vbd = k.sb(s, "v_by_sample", [TS, NB, 4 * P])
        eg = k.sb(s, "state_decay", [P, 4, TS])
        state = k.sb(s, "hgrn_state", [P, NB, 4, P])
        statep = k.sb(s, "hgrn_state_p", [P, 4, P])
        names = ("diff", "level_exp", "level_x", "level_dot", "level_in", "diag_dot", "state_in", "v_turned", "v_copied",
                 "kd_diff", "exp", "kd_done", "kd_turned", "kd_copied", "by_sample", "decays", "qe_done",
                 "state_dot", "state_new", "o_dot", "sq", "sum", "mean", "root", "o_out", "stored", "statep")
        n_ = {x: k.count(x) for x in names}

        def halves(x, H, n):
            b = x[:, :, 0:n]
            if n == T:
                b = b.rearrange("p c (b u) -> p (c b) u", u=2 * H)
                return b[:, :, 0:H], b[:, :, H:2 * H], b[:, :, H - 1:H].broadcast_to([P, 4 * n // (2 * H), H])
            b = b.rearrange("p c (b u) -> p c b u", u=2 * H)
            return b[:, :, :, 0:H], b[:, :, :, H:2 * H], b[:, :, :, H - 1:H].broadcast_to([P, 4, n // (2 * H), H])

        span = lambda H: T if H <= 2 else TP
        with k.stage() as block:
            @block.gpsimd
            def _(pool):
                pool.dma_start(state[:, :, :, :].rearrange("p b c v -> p (b c) v"),
                               k.ins["state_hgrn"].rearrange("b a c k v -> k (b a c) v")).then_inc(*n_["state_in"].up(16))
                pool.wait_ge(*n_["statep"].at(1))
                pool.dma_start(k.outs[10][0, 0].rearrange("c k v -> k c v"), statep[:, :, :]).then_inc(*n_["stored"].up(16))
                pool.wait_ge(*n_["state_new"].at(8))
                pool.dma_start(k.outs[11].rearrange("b a c k v -> k (b a c) v"),
                               state[:, :, :, :].rearrange("p b c v -> p (b c) v")).then_inc(*n_["stored"].up(16))
                pool.wait_ge(*n_["stored"].at(32))

            @block.vector
            def _(dve):
                def then(ins, sig=dve_step):
                    ins.then_inc(*sig.up())
                    dve.wait_ge(*sig.all())

                def diff(l):
                    H, x = levels[l], X2[l % 2]
                    n = span(H)
                    if l >= 2:
                        dve.wait_ge(*n_["level_dot"].at(l - 1))
                    g1, g2, ref = halves(g, H, n)
                    x1, x2, _ = halves(x, H, n)
                    then(dve.tensor_tensor(x1, ref, g1, ALU.subtract))
                    dve.tensor_tensor(x2, g2, ref, ALU.subtract).then_inc(*n_["diff"].up())

                def scale(l):
                    H, x = levels[l], X2[l % 2]
                    n = span(H)
                    dve.wait_ge(*n_["level_exp"].at(l + 1))
                    x1, x2, _ = halves(x, H, n)
                    k1 = halves(kk, H, n)[0]
                    q2 = halves(q, H, n)[1]
                    then(dve.tensor_tensor(x1, x1, k1, ALU.mult))
                    dve.tensor_tensor(x2, x2, q2, ALU.mult).then_inc(*n_["level_x"].up())

                def gather(l):
                    H = levels[l]
                    dve.wait_ge(*n_["level_dot"].at(l + 1))
                    bank = 3 * (l % 2)
                    if H == P:
                        then(dve.tensor_copy(attx[:, :, :], k.ps[:, bank, :].rearrange("p (c n) -> p c n", c=4)), n_["level_in"])
                        return
                    m0, _ = k.core_at["level"]
                    mask = k.core[:, m0 + P * l:m0 + P * l + P].bitcast(I32)
                    if H <= 2:
                        then(dve.copy_predicated(atts[:, :, :], mask[0:TS, 0:TS].unsqueeze(1).broadcast_to([TS, 4, TS]),
                                                 k.ps[0:TS, bank + 2, 0:4 * TS].rearrange("p (c n) -> p c n", c=4)))
                    then(dve.copy_predicated(att[:, :, :, :].rearrange("p i c n -> p (i c) n"), mask.unsqueeze(1).broadcast_to([P, 8, P]),
                                             k.ps[:, bank:bank + 2, :].rearrange("p i (c n) -> p (i c) n", c=4)), n_["level_in"])

                diff(0)
                diff(1)
                dve.wait_ge(*n_["diag_dot"].at(1))
                eye = k.const("ident")
                then(dve.tensor_tensor(att[:, :, :, :].rearrange("p i c n -> p (i c) n"),
                                       k.ps[:, 6:8, :].rearrange("p i (c n) -> p (i c) n", c=4),
                                       eye.unsqueeze(1).broadcast_to([P, 8, P]), ALU.mult))
                then(dve.tensor_tensor(atts[:, :, :], k.ps[0:TS, 5, 0:4 * TS].rearrange("p (c n) -> p c n", c=4),
                                       eye[0:TS, 0:TS].unsqueeze(1).broadcast_to([TS, 4, TS]), ALU.mult), n_["level_in"])
                for l in range(8):
                    scale(l)
                    if l + 2 < 8:
                        diff(l + 2)
                    gather(l)
                wide = lambda ap, n: ap.broadcast_to([P, 4, n])
                then(dve.tensor_tensor(kd[:, :, 0:TP], wide(g[:, :, TP - 1:TP], TP), g[:, :, 0:TP], ALU.subtract))
                kds = kd[:, :, TP:T].rearrange("p c (b t) -> p c b t", t=NT)
                gs4 = g[:, :, TP:T].rearrange("p c (b t) -> p c b t", t=NT)
                dve.tensor_tensor(kds, gs4[:, :, :, NT - 1:NT].broadcast_to([P, 4, NB, NT]), gs4, ALU.subtract).then_inc(*n_["kd_diff"].up())
                for i, (a, n) in enumerate(TILES):
                    dve.wait_ge(*n_["v_turned"].at(i + 1))
                    then(dve.tensor_copy(vt[0:n, i, :], k.ps[0:n, i, :]), n_["v_copied"])
                dve.wait_ge(*n_["exp"].at(1))
                then(dve.tensor_tensor(kd[:, :, :], kd[:, :, :], kk[:, :, :], ALU.mult), n_["kd_done"])
                for i, (a, n) in enumerate(TILES):
                    dve.wait_ge(*n_["kd_turned"].at(i + 1))
                    then(dve.tensor_copy(kdt[0:n, i, :], k.ps[0:n, 3 + i, :]), n_["kd_copied"])
                then(dve.tensor_tensor(vbd[:, :, :], vt[0:TS, 2, :].unsqueeze(1).broadcast_to([TS, NB, 4 * P]),
                                       k.const("batch_of")[0:TS, :].unsqueeze(2).broadcast_to([TS, NB, 4 * P]), ALU.mult), n_["by_sample"])
                dve.wait_ge(*n_["decays"].at(1))
                dve.tensor_tensor(qe[:, :, :], eg[:, :, :], q[:, :, TP:T], ALU.mult).then_inc(*n_["qe_done"].up())
                sq = X2[0]
                for c in range(4):
                    dve.wait_ge(*n_["o_dot"].at(c + 1))
                    then(dve.tensor_copy(mixed_out[:, c, :], k.ps[:, c, 0:T]))
                    dve.tensor_tensor(sq[:, c, :], mixed_out[:, c, :], mixed_out[:, c, :], ALU.mult).then_inc(*n_["sq"].up())
                dve.wait_ge(*n_["state_dot"].at(1))
                dve.tensor_copy(statep[:, :, :], k.ps[:, 4, :].rearrange("p (c v) -> p c v", c=4)).then_inc(*n_["statep"].up())
                for c in range(4):
                    for hf in range(2):
                        i = 2 * c + hf
                        dve.wait_ge(*n_["state_dot"].at(i + 2))
                        for b in range(4 * hf, 4 * hf + 4):
                            last = NT * b + NT - 1
                            ins = dve.scalar_tensor_tensor(state[:, b, c, :], state[:, b, c, :], eg[:, c, last:last + 1],
                                                           k.ps[:, 5 + i % 3, P * (b % 4):P * (b % 4) + P], ALU.mult, ALU.add)
                        ins.then_inc(*n_["state_new"].up())
                rs = X2[1]
                for c in range(4):
                    dve.wait_ge(*n_["sum"].at(c + 1))
                    then(dve.tensor_scalar(rs[:, c, :], k.ps[:, c, 0:T], 1.0 / P, EPS, ALU.mult, ALU.add), n_["mean"])
                dve.wait_ge(*n_["root"].at(2))
                for c in range(4):
                    then(dve.scalar_tensor_tensor(rs[:, c, :], rs[:, c, :], k.vec[:, 48 + c:49 + c], gate[:, c, :], ALU.mult, ALU.mult))
                    then(dve.tensor_tensor(mixed_out[:, c, :], mixed_out[:, c, :], rs[:, c, :], ALU.mult), n_["o_out"])

            @block.scalar
            def _(act):
                for l in range(8):
                    act.wait_ge(*n_["diff"].at(l + 1))
                    x = X2[l % 2][:, :, 0:span(levels[l])]
                    act.activation(x, x, ACT.Exp).then_inc(*n_["level_exp"].up())
                act.activation(eg[:, :, :], g[:, :, TP:T], ACT.Exp).then_inc(*n_["decays"].up())
                act.wait_ge(*n_["kd_diff"].at(1))
                act.activation(kd[:, :, :], kd[:, :, :], ACT.Exp).then_inc(*n_["exp"].up())
                rs = X2[1]
                act.wait_ge(*n_["mean"].at(4))
                act.activation(rs[:, :, :], rs[:, :, :], ACT.Ln).then_inc(*n_["root"].up())
                act.wait_ge(*n_["root"].at(1))
                act.activation(rs[:, :, :], rs[:, :, :], ACT.Exp, scale=-0.5).then_inc(*n_["root"].up())

            @block.tensor
            def _(pe):
                ident = k.const("ident")
                for i in range(2):
                    for c in range(4):
                        mm = pe.matmul(k.ps[:, 6 + i, P * c:P * c + P], kk[:, c, P * i:P * i + P], q[:, c, P * i:P * i + P], start=True, stop=True)
                for c in range(4):
                    mm = pe.matmul(k.ps[0:TS, 5, TS * c:TS * c + TS], kk[:, c, TP:T], q[:, c, TP:T], start=True, stop=True)
                mm.then_inc(*n_["diag_dot"].up())
                for l, H in enumerate(levels):
                    x, bank = X2[l % 2], 3 * (l % 2)
                    pe.wait_ge(*n_["level_x"].at(l + 1))
                    if l >= 1:
                        pe.wait_ge(*n_["level_in"].at(max(l, 1)))
                    if H == P:
                        for c in range(4):
                            mm = pe.matmul(k.ps[:, bank, P * c:P * c + P], x[:, c, 0:P], x[:, c, P:2 * P], start=True, stop=True)
                    else:
                        for i in range(2):
                            for c in range(4):
                                tile = x[:, c, P * i:P * i + P]
                                mm = pe.matmul(k.ps[:, bank + i, P * c:P * c + P], tile, tile, start=True, stop=True)
                        if H <= 2:
                            for c in range(4):
                                mm = pe.matmul(k.ps[0:TS, bank + 2, TS * c:TS * c + TS], x[:, c, TP:T], x[:, c, TP:T], start=True, stop=True)
                    mm.then_inc(*n_["level_dot"].up())
                pe.wait_ge(*n_["level_in"].at(9))
                for i, (a, n) in enumerate(TILES):
                    for c in range(4):
                        mm = pe.transpose(k.ps[0:n, i, P * c:P * c + P], v[:, c, a:a + n], ident)
                    mm.then_inc(*n_["v_turned"].up())
                pe.wait_ge(*n_["kd_done"].at(1))
                for i, (a, n) in enumerate(TILES):
                    for c in range(4):
                        mm = pe.transpose(k.ps[0:n, 3 + i, P * c:P * c + P], kd[:, c, a:a + n], ident)
                    mm.then_inc(*n_["kd_turned"].up())
                pe.wait_ge(*n_["state_in"].at(16))
                pe.wait_ge(*n_["qe_done"].at(1))
                for c in range(4):
                    cols = slice(P * c, P * c + P)
                    pe.matmul(k.ps[:, c, 0:P], vt[:, 0, cols], att[:, 0, c, :], start=True, stop=True)
                    pe.matmul(k.ps[:, c, P:TP], vt[:, 1, cols], att[:, 1, c, :], start=True, stop=False)
                    pe.matmul(k.ps[:, c, P:TP], vt[:, 0, cols], attx[:, c, :], start=False, stop=True)
                    pe.matmul(k.ps[:, c, TP:T], vt[0:TS, 2, cols], atts[:, c, :], start=True, stop=False, skip_group_check=True)
                    for b in range(NB):
                        mm = pe.matmul(k.ps[:, c, TP + NT * b:TP + NT * b + NT], state[:, b, c, :],
                                       qe[:, c, NT * b:NT * b + NT], start=False, stop=b == NB - 1, skip_group_check=True)
                    mm.then_inc(*n_["o_dot"].up())
                pe.wait_ge(*n_["kd_copied"].at(3))
                for c in range(4):
                    for i in range(2):
                        mm = pe.matmul(k.ps[:, 4, P * c:P * c + P], kdt[:, i, P * c:P * c + P], vt[:, i, P * c:P * c + P],
                                       start=i == 0, stop=i == 1)
                mm.then_inc(*n_["state_dot"].up())
                pe.wait_ge(*n_["by_sample"].at(1))
                for i in range(8):
                    c, hf = i // 2, i % 2
                    if i >= 3:
                        pe.wait_ge(*n_["state_new"].at(i - 2))
                    pe.matmul(k.ps[:, 5 + i % 3, :], kdt[0:TS, 2, P * c:P * c + P], vbd[:, 4 * hf:4 * hf + 4, P * c:P * c + P],
                              start=True, stop=True).then_inc(*n_["state_dot"].up())
                sq = X2[0]
                for c in range(4):
                    pe.wait_ge(*n_["sq"].at(c + 1))
                    pe.matmul(k.ps[:, c, 0:T], k.const("ones"), sq[:, c, :], start=True, stop=True).then_inc(*n_["sum"].up())


def stage_conv(k, conv_in, conv_in_s, xc):
    with ExitStack() as s:
        rows_p = k.sb(s, "conv_rows_p", [3, CC * P])
        rows_s = k.sb(s, "conv_rows_s", [3 * NB, CC * P])
        last3 = k.sb(s, "conv_last3", [P, CC, 3 * NB])
        packed = k.count("conv_packed")
        first, tapped, silued, dve_step = (k.count(n) for n in ("tap_first", "taps", "conv_silu", "dve_step"))
        turned, copied, stored = (k.count(n) for n in ("rows_turned", "rows_copied", "rows_stored"))
        w = lambda j, c: k.vec[:, 60 + CC * j + c:61 + CC * j + c]
        bias = lambda c: k.vec[:, 108 + c:109 + c]
        outp = lambda c: xc[:, c, 0:TP]
        outs = lambda c: xc[:, c, TP:T].rearrange("p (b t) -> p b t", t=NT)
        with k.stage() as block:
            @block.scalar
            def _(act):
                for c in range(CC):
                    act.activation(outs(c), conv_in_s[:, c, :, 0:NT], ACT.Identity, scale=w(0, c), bias=bias(c)).then_inc(*first.up())
                    act.activation(outp(c), conv_in[:, c, 0:TP], ACT.Identity, scale=w(0, c), bias=bias(c)).then_inc(*first.up())
                    if c >= 2:
                        act.wait_ge(*tapped.at(c - 1))
                        act.activation(xc[:, c - 2, :], xc[:, c - 2, :], ACT.Silu).then_inc(*silued.up())
                for c in (CC - 2, CC - 1):
                    act.wait_ge(*tapped.at(c + 1))
                    act.activation(xc[:, c, :], xc[:, c, :], ACT.Silu).then_inc(*silued.up())

            @block.vector
            def _(dve):
                dve.tensor_copy(last3[:, :, :].rearrange("p c (b r) -> p c b r", r=3), conv_in_s[:, :, :, NT:NT + 3]).then_inc(*packed.up())
                for c in range(CC):
                    dve.wait_ge(*first.at(2 * c + 2))
                    for j in range(1, 4):
                        if j > 1:
                            dve.wait_ge(*dve_step.all())
                        dve.scalar_tensor_tensor(outs(c), conv_in_s[:, c, :, j:j + NT], w(j, c), outs(c), ALU.mult, ALU.add)\
                           .then_inc(*dve_step.up())
                        dve.scalar_tensor_tensor(outp(c), conv_in[:, c, j:j + TP], w(j, c), outp(c), ALU.mult, ALU.add)\
                           .then_inc(*(tapped if j == 3 else dve_step).up())
                for n, (dst, rows) in enumerate(((rows_p, 3), (rows_s, 24))):
                    dve.wait_ge(*turned.at(n + 1))
                    dve.tensor_copy(dst[:, :].rearrange("r (b n) -> r b n", b=3), k.ps[0:rows, 3 * n:3 * n + 3, :]).then_inc(*copied.up())

            @block.tensor
            def _(pe):
                pe.wait_ge(*packed.at(1))
                for n in range(2):
                    for c in range(CC):
                        in_ = last3[:, c, :] if n else conv_in[:, c, TP:TP + 3]
                        mm = pe.transpose(k.ps[0:24 if n else 3, 3 * n + c // 4, P * (c % 4):P * (c % 4) + P], in_, k.const("ident"))
                    mm.then_inc(*turned.up())

            @block.gpsimd
            def _(pool):
                pool.wait_ge(*copied.at(1))
                pool.dma_start(k.outs[14][0, 0], rows_p[:, :]).then_inc(*stored.up(16))
                pool.wait_ge(*copied.at(2))
                pool.dma_start(k.outs[15].rearrange("b a r c -> (b a r) c"), rows_s[:, :]).then_inc(*stored.up(16))
                pool.wait_ge(*stored.at(32))


def stage_dt(k, dt, dta):
    acum, wend, dtt = dta["acum"], dta["wend"], dta["tok"]
    with ExitStack() as s:
        par = k.sb(s, "dt_params", [HM, 4])
        u = k.sb(s, "dt_u", [HM, T])
        par_in, raw_ready, log_ready, a_ready, dt_done, sums, ended = (k.count("d_" + n) for n in (
            "par_in", "raw", "log", "a", "dt", "sums", "ended"))
        diffed, turned, copied = k.count("d_diff"), k.count("turned"), k.count("copied")
        act_step, dve_step = k.count("act_step"), k.count("dve_step")
        with k.stage() as block:
            @block.sync
            def _(sp):
                for n, name in enumerate(("dt_bias", "a_log", "d_skip")):
                    sp.dma_start(par[:, n:n + 1], k.ins[name].rearrange("a h -> h a")).then_inc(*par_in.up(16))

            @block.vector
            def _(dve):
                def then(ins, sig=dve_step):
                    ins.then_inc(*sig.up())
                    dve.wait_ge(*sig.all())
                dve.wait_ge(*par_in.at(48))
                then(dve.tensor_scalar(dt[:, :], dt[:, :], par[:, 0:1], None, ALU.add), raw_ready)
                dve.wait_ge(*log_ready.at(1))
                then(dve.scalar_tensor_tensor(dt[:, :], dt[:, :], 0.0, u[:, :], ALU.max, ALU.add), dt_done)
                dve.wait_ge(*a_ready.at(1))
                then(dve.tensor_scalar(u[:, :], dt[:, :], par[:, 3:4], -1.0, ALU.mult, ALU.mult))
                then(dve.tensor_tensor_scan(acum[:, :], k.const("running")[0:HM, :], u[:, :], 0.0, ALU.mult, ALU.add), sums)
                dve.tensor_tensor(wend[:, 0:TP], acum[:, TP - 1:TP].broadcast_to([HM, TP]), acum[:, 0:TP], ALU.subtract).then_inc(*dve_step.up())
                ac = acum[:, TP:T].rearrange("p (b t) -> p b t", t=NT)
                dve.tensor_tensor(wend[:, TP:T].rearrange("p (b t) -> p b t", t=NT), ac[:, :, NT - 1:NT].broadcast_to([HM, NB, NT]), ac,
                                  ALU.subtract).then_inc(*diffed.up())
                dve.wait_ge(*ended.at(1))
                then(dve.tensor_tensor(wend[:, :], wend[:, :], dt[:, :], ALU.mult), ended)
                dve.wait_ge(*turned.at(1))
                dve.tensor_copy(dtt[:, 0:2, :], k.ps[:, 0, 0:96].rearrange("p (i n) -> p i n", i=2)).then_inc(*copied.up())
                dve.tensor_copy(dtt[0:TS, 2, :], k.ps[0:TS, 0, 96:144]).then_inc(*copied.up())
                dve.tensor_copy(dta["skip"][:, :], k.ps[:, 1, 0:8]).then_inc(*copied.up())

            @block.scalar
            def _(act):
                def then(ins, sig=act_step):
                    ins.then_inc(*sig.up())
                    act.wait_ge(*sig.all())
                act.wait_ge(*par_in.at(48))
                act.activation(par[:, 3:4], par[:, 1:2], ACT.Exp).then_inc(*a_ready.up())
                act.wait_ge(*raw_ready.at(1))
                then(act.activation(u[:, :], dt[:, :], ACT.Abs))
                then(act.activation(u[:, :], u[:, :], ACT.Exp, scale=-1.0))
                act.activation(u[:, :], u[:, :], ACT.Ln, bias=1.0).then_inc(*log_ready.up())
                act.wait_ge(*diffed.at(1))
                act.wait_ge(*dve_step.all())
                act.activation(wend[:, :], wend[:, :], ACT.Exp).then_inc(*ended.up())

            @block.tensor
            def _(pe):
                pe.wait_ge(*par_in.at(48))
                pairs = k.const("head_pair")
                for j in range(8):
                    pe.matmul(k.ps[:, 1, j:j + 1], pairs[0:HM, P * j:P * j + P], par[:, 2:3], start=True, stop=True)
                pe.wait_ge(*ended.at(2))
                for i, (a, n) in enumerate(TILES):
                    for m, src in enumerate((acum, dt, wend)):
                        mm = pe.transpose(k.ps[0:n, 0, 48 * i + 16 * m:48 * i + 16 * m + 16], src[:, a:a + n], k.const("ident")[0:HM, 0:HM])
                mm.then_inc(*turned.up())


SUM_BANKS = (2, 3, 4, 6)


def stage_ssd(k, proj, xc, dt, dta, mixed_out):
    acum, dtt = dta["acum"], dta["tok"]
    first_out = 4
    act_step, dve_step = k.count("act_step"), k.count("dve_step")
    with ExitStack() as s:
        xt = k.sb(s, "x_tokens", [P, 3, D])
        bt = k.sb(s, "b_tokens", [P, 3, 256])
        gm = k.sb(s, "cb", [P, 4, 416])
        dec = [k.sb(s, f"decay{n}", [P, 416]) for n in range(2)]
        sc = [k.sb(s, f"scores{n}", [P, 416]) for n in range(2)]
        state = k.sb(s, "ssm_state", [P, NB, 8, 64])
        stT = k.sb(s, "ssm_state_t", [P, NB, 4, P])
        statep = k.sb(s, "ssm_state_p", [P, 8, 64])
        ebc = k.sb(s, "ebc", [P, 8, TS])
        inter = k.sb(s, "inter", [P, 8, TS])
        bbd = proj[0:TS, 0:NB, 0:256]
        names = ("state_in", "xt_turned", "xt_copied", "cb_dot", "cb_copied", "row", "diff", "exp", "scores", "y_dot", "y_taken",
                 "st_turned", "st_copied", "ebc_dot", "ebc_exp", "inter_dot", "inter_done", "xw", "by_sample", "state_dot", "state_new",
                 "statep", "stored", "scaled", "sq", "sum", "mean", "root", "out")
        n_ = {x: k.count(x) for x in names}
        xtiles = [(i, q) for i in range(3) for q in range(2)]

        def slot(j):
            return 4 * (j // 4) + 2 * (j % 2) + (j // 2) % 2

        def parts(x):
            y = x[:, :, :, :].rearrange("p b (J w v) n -> p (b J) w v n", w=2, v=2)
            return [y[:, :, w, v, :] for v in range(2) for w in range(2)]

        def dram_parts(x):
            y = x.rearrange("b a (J v w u) p n -> v w (u p) (b a J) n", v=2, w=2, u=2)
            return [y[v, w] for v in range(2) for w in range(2)]

        def brow(g):
            return slice(64 * (g % 2), 64 * (g % 2) + 64)

        with k.stage() as block:
            @block.gpsimd
            def _(pool):
                for dst, src in zip(parts(state), dram_parts(k.ins["state_ssm"])):
                    pool.dma_start(dst, src).then_inc(*n_["state_in"].up(16))
                pool.wait_ge(*n_["statep"].at(1))
                pool.dma_start(k.outs[12][0, 0].rearrange("(j u) p n -> (u p) j n", u=2), statep[:, :, :]).then_inc(*n_["stored"].up(16))
                pool.wait_ge(*n_["state_new"].at(9))
                for src, dst in zip(parts(state), dram_parts(k.outs[13])):
                    pool.dma_start(dst, src).then_inc(*n_["stored"].up(16))
                pool.wait_ge(*n_["stored"].at(80))

            @block.tensor
            def _(pe):
                ident = k.const("ident")
                n = 0
                for i, (a, m) in enumerate(TILES):
                    for u in range(3):
                        if n >= 2:
                            pe.wait_ge(*n_["xt_copied"].at(n - 1))
                        for c in range(4 if u < 2 else 2):
                            mm = pe.transpose(k.ps[0:m, n % 2, P * c:P * c + P], xc[:, 4 * u + c, a:a + m], ident)
                        mm.then_inc(*n_["xt_turned"].up())
                        n += 1
                for g in range(4):
                    b, c, r = xc[:, 8 + g // 2, :], xc[:, 10 + g // 2, :], brow(g)
                    if g >= 1:
                        pe.wait_ge(*n_["cb_copied"].at(g))
                    pe.matmul(k.ps[:, 2, 0:TP], b[r, 0:P], c[r, 0:TP], start=True, stop=True)
                    pe.matmul(k.ps[:, 2, TP:TP + P], b[r, P:TP], c[r, P:TP], start=True, stop=True)
                    pe.matmul(k.ps[0:TS, 2, 384:416], b[r, TP:T], c[r, TP:T], start=True, stop=True).then_inc(*n_["cb_dot"].up())
                pe.wait_ge(*n_["state_in"].at(64))
                pe.wait_ge(*n_["xt_copied"].at(9))
                for b in range(NB):
                    if b >= 2:
                        pe.wait_ge(*n_["st_copied"].at(b - 1))
                    for q in range(4):
                        mm = pe.transpose(k.ps[:, b % 2, P * q:P * q + P], state[:, b, 2 * q:2 * q + 2, :].rearrange("p v n -> p (v n)"), ident)
                    mm.then_inc(*n_["st_turned"].up())
                pe.wait_ge(*n_["cb_copied"].at(4))
                pairs = k.const("head_pair")
                for j in range(8):
                    mm = pe.matmul(k.ps[:, 2, TS * slot(j):TS * slot(j) + TS], pairs[0:HM, P * j:P * j + P], acum[:, TP:T], start=True, stop=True)
                mm.then_inc(*n_["ebc_dot"].up())
                pe.wait_ge(*n_["st_copied"].at(NB))
                for par in range(2):
                    for b in range(NB):
                        for j in range(8):
                            g = j // 2
                            if g % 2 != par:
                                continue
                            r = brow(g)
                            mm = pe.matmul(k.ps[:, 3 + par, TS * j + NT * b:TS * j + NT * b + NT], stT[r, b, 2 * (j // 4) + j % 2, :],
                                           xc[r, 10 + g // 2, TP + NT * b:TP + NT * b + NT], start=True, stop=True)
                mm.then_inc(*n_["inter_dot"].up())

                def row(h):
                    if h >= 2:
                        pe.wait_ge(*n_["diff"].at(3 * (h - 1)))
                    pe.matmul(k.ps[:, h % 2, 0:T], ident[0:HM, h:h + 1].broadcast_to([HM, P]), acum[:, :], start=True, stop=True)\
                      .then_inc(*n_["row"].up())
                row(0)
                row(1)
                for h in range(HM):
                    pe.wait_ge(*n_["scores"].at(3 * h + 3))
                    if h % 2 == 0 and h >= 4:
                        pe.wait_ge(*n_["y_taken"].at(h // 2 - 1))
                    r, bank, x = slice(64 * (h % 2), 64 * (h % 2) + 64), 6 + (h // 2) % 2, slice(64 * h, 64 * h + 64)
                    m = sc[h % 2]
                    pe.matmul(k.ps[r, bank, 0:TP], xt[:, 0, x], m[:, 0:TP], start=True, stop=False, skip_group_check=True)
                    pe.matmul(k.ps[r, bank, P:TP], xt[:, 1, x], m[:, TP:TP + P], start=False, stop=True, skip_group_check=True)
                    pe.matmul(k.ps[r, bank, TP:T], xt[0:TS, 2, x], m[0:TS, 384:416], start=True, stop=True).then_inc(*n_["y_dot"].up())
                    if h + 2 < HM:
                        row(h + 2)
                pe.wait_ge(*n_["xw"].at(3))
                for j in range(8):
                    for i in range(2):
                        mm = pe.matmul(k.ps[:, 5, 64 * j:64 * j + 64], xt[:, i, P * j:P * j + P], bt[:, i, 64 * (j // 2):64 * (j // 2) + 64],
                                       start=i == 0, stop=i == 1)
                mm.then_inc(*n_["state_dot"].up())
                pe.wait_ge(*n_["by_sample"].at(1))
                for j in range(8):
                    if j >= 2:
                        pe.wait_ge(*n_["state_new"].at(j))
                    g = j // 2
                    pe.matmul(k.ps[:, j % 2, :], xt[0:TS, 2, P * j:P * j + P], bbd[:, :, 64 * g:64 * g + 64],
                              start=True, stop=True).then_inc(*n_["state_dot"].up())
                for g in range(4):
                    pe.wait_ge(*n_["sq"].at(2 * g + 2))
                    for u in range(2):
                        mm = pe.matmul(k.ps[:, SUM_BANKS[g], 0:T], k.const("ones"),
                                       dta["sq"][:, 2 * g + u, :], start=u == 0, stop=u == 1)
                    mm.then_inc(*n_["sum"].up())

            @block.vector
            def _(dve):
                def then(ins, sig=dve_step):
                    ins.then_inc(*sig.up())
                    dve.wait_ge(*sig.all())
                n = 0
                for i, (a, m) in enumerate(TILES):
                    for u in range(3):
                        dve.wait_ge(*n_["xt_turned"].at(n + 1))
                        dst = xt[0:m, i, 512 * u:512 * u + 512] if u < 2 else bt[0:m, i, :]
                        dve.tensor_copy(dst, k.ps[0:m, n % 2, 0:dst.shape[1]]).then_inc(*n_["xt_copied"].up())
                        n += 1
                for g in range(4):
                    dve.wait_ge(*n_["cb_dot"].at(g + 1))
                    dve.tensor_copy(gm[0:TS, g, 384:416], k.ps[0:TS, 2, 384:416]).then_inc(*dve_step.up())
                    dve.tensor_copy(gm[:, g, 0:384], k.ps[:, 2, 0:384]).then_inc(*n_["cb_copied"].up())
                for b in range(NB):
                    dve.wait_ge(*n_["st_turned"].at(b + 1))
                    dve.tensor_copy(stT[:, b, :, :], k.ps[:, b % 2, :].rearrange("p (q n) -> p q n", q=4)).then_inc(*n_["st_copied"].up())
                dve.wait_ge(*n_["cb_copied"].at(4))

                def diff(h):
                    bank, d = k.ps[:, h % 2, :], dec[h % 2]
                    dve.wait_ge(*n_["row"].at(h + 1))
                    if h >= 2:
                        dve.wait_ge(*n_["scores"].at(3 * (h - 1)))
                    fut = k.const("ssd_future")
                    for rows, dcol, bcol, w, i, mask in ((P, 0, 0, TP, 0, fut[:, 0:TP]), (P, TP, P, P, 1, fut[:, 0:P]),
                                                         (TS, 384, TP, TS, 2, k.const("ssd_future_s")[0:TS, :])):
                        dve.scalar_tensor_tensor(d[0:rows, dcol:dcol + w], bank[0:rows, bcol:bcol + w], dtt[0:rows, i, h:h + 1], mask,
                                                 ALU.subtract, ALU.add).then_inc(*n_["diff"].up())

                def score(h):
                    d, m, g = dec[h % 2], sc[h % 2], h // 4
                    dve.wait_ge(*n_["exp"].at(2 * h + 2))
                    if h >= 2:
                        dve.wait_ge(*n_["y_dot"].at(h - 1))
                    for rows, col, w, i in ((P, 0, TP, 0), (P, TP, P, 1), (TS, 384, TS, 2)):
                        dve.scalar_tensor_tensor(m[0:rows, col:col + w], d[0:rows, col:col + w], dtt[0:rows, i, 16 + h:17 + h],
                                                 gm[0:rows, g, col:col + w], ALU.mult, ALU.mult).then_inc(*n_["scores"].up())

                def take(j):
                    bank = k.ps[:, 6 + j % 2, :]
                    y = mixed_out[:, first_out + j, :]
                    dve.wait_ge(*n_["y_dot"].at(2 * j + 2))
                    then(dve.scalar_tensor_tensor(y, xc[:, j, :], dta["skip"][:, j:j + 1], bank[:, 0:T], ALU.mult, ALU.add), n_["y_taken"])
                    if j == 0:
                        dve.wait_ge(*n_["ebc_exp"].at(1))
                        dve.wait_ge(*n_["inter_dot"].at(1))
                        for par in range(2):
                            pv = k.ps[:, 3 + par, 0:TP].rearrange("p (j t) -> p j t", t=TS)
                            for jj in (0, 1, 4, 5) if par == 0 else (2, 3, 6, 7):
                                then(dve.tensor_tensor(inter[:, jj, :], pv[:, jj, :], ebc[:, slot(jj), :], ALU.mult))
                    then(dve.tensor_tensor(y[:, TP:T], y[:, TP:T], inter[:, j, :], ALU.add))
                    then(dve.tensor_tensor(y, y, proj[:, Z + j, :], ALU.mult), n_["scaled"])

                diff(0)
                for h in range(HM):
                    if h + 1 < HM:
                        diff(h + 1)
                    score(h)
                    if h >= 2 and h % 2 == 1:
                        take(h // 2 - 1)
                take(7)
                for i, (a, m) in enumerate(TILES):
                    v = xt[0:m, i, :].rearrange("p (h n) -> p h n", h=HM)
                    then(dve.tensor_tensor(v, v, dtt[0:m, i, 32:48].unsqueeze(2).broadcast_to([m, HM, 64]), ALU.mult), n_["xw"])
                then(dve.tensor_tensor(bbd, bt[0:TS, 2, :].unsqueeze(1).broadcast_to([TS, NB, 256]),
                                       k.const("batch_of")[0:TS, :].unsqueeze(2).broadcast_to([TS, NB, 256]), ALU.mult), n_["by_sample"])
                dve.wait_ge(*n_["state_dot"].at(1))
                dve.tensor_copy(statep[:, :, :], k.ps[:, 5, :].rearrange("p (j n) -> p j n", j=8)).then_inc(*n_["statep"].up())
                last = ebc[:, :, :].rearrange("p j (b t) -> p b j t", t=NT)[:, :, :, NT - 1:NT]
                then(dve.tensor_tensor(state[:, :, :, :], state[:, :, :, :], last.broadcast_to([P, NB, 8, 64]), ALU.mult), n_["state_new"])
                for j in range(8):
                    dve.wait_ge(*n_["state_dot"].at(j + 2))
                    dve.tensor_tensor(state[:, :, slot(j), :], state[:, :, slot(j), :], k.ps[:, j % 2, :].rearrange("p (b n) -> p b n", b=NB),
                                      ALU.add).then_inc(*n_["state_new"].up())
                rs = dta["rs"]
                for g in range(4):
                    dve.wait_ge(*n_["sum"].at(g + 1))
                    dve.tensor_scalar(rs[:, g, :], k.ps[:, SUM_BANKS[g], 0:T], 1.0 / 256, EPS, ALU.mult, ALU.add).then_inc(*n_["mean"].up())
                dve.wait_ge(*n_["root"].at(2))
                for j in range(8):
                    y = mixed_out[:, first_out + j, :]
                    dve.scalar_tensor_tensor(y, y, k.vec[:, 52 + j:53 + j], rs[:, j // 2, :], ALU.mult, ALU.mult).then_inc(*n_["out"].up())

            @block.scalar
            def _(act):
                act.wait_ge(*n_["ebc_dot"].at(1))
                act.activation(ebc[:, :, :], k.ps[:, 2, 0:TP].rearrange("p (j t) -> p j t", t=TS), ACT.Exp).then_inc(*n_["ebc_exp"].up())

                def square(j):
                    act.wait_ge(*n_["scaled"].at(j + 1))
                    act.activation(dta["sq"][:, j, :], mixed_out[:, first_out + j, :], ACT.Square).then_inc(*n_["sq"].up())

                for h in range(HM):
                    act.wait_ge(*n_["diff"].at(3 * h + 3))
                    d = dec[h % 2]
                    act.activation(d[:, 0:384], d[:, 0:384], ACT.Exp).then_inc(*n_["exp"].up())
                    act.activation(d[0:TS, 384:416], d[0:TS, 384:416], ACT.Exp).then_inc(*n_["exp"].up())
                    if h >= 4 and h % 2 == 0:
                        square(h // 2 - 2)
                square(6)
                square(7)
                rs = dta["rs"]
                act.wait_ge(*n_["mean"].at(4))
                act.activation(rs[:, :, :], rs[:, :, :], ACT.Ln).then_inc(*n_["root"].up())
                act.wait_ge(*n_["root"].at(1))
                act.activation(rs[:, :, :], rs[:, :, :], ACT.Exp, scale=-0.5).then_inc(*n_["root"].up())



def stage_route(k, moe):
    nc = k.nc
    I = MAX_ITEMS + 1
    with ExitStack() as s:
        wr = k.sb(s, "w_router", [P, DC, NE])
        lg = k.sb(s, "logits", [P, 3, NE])
        gt = k.sb(s, "greater", [P, 3, NE, NE])
        eq = k.sb(s, "equal", [P, 3, NE, NE])
        chosen = k.sb(s, "chosen", [P, 3, NE])
        gate = k.sb(s, "gate", [P, 3, NE])
        place = k.sb(s, "place", [P, 3, NE])
        cnt = k.sb(s, "cnt", [P, 4, NE])
        one = k.sb(s, "item_expert", [P, I, NE])
        blk = k.sb(s, "item_block", [P, I, NE])
        tmp = k.sb(s, "item_tmp", [P, I, NE])
        tmp2 = k.sb(s, "item_tmp2", [P, I, NE])
        ids = k.sb(s, "item_ids", [P, I + 1])
        small = k.sb(s, "small", [P, 3, 2])
        wr_in, logit, turned, copied, exp_in, exped, chose, ranked = (k.count(n) for n in (
            "router_in", "scored", "turned", "copied", "diff", "exped", "chosen", "ranked"))
        dve_step = k.count("dve_step")
        with k.stage() as block:
            @block.sync
            def _(sp):
                sp.dma_start(wr[:, :, :], k.ins["w_router"][0].rearrange("(c p) e -> p c e", p=P)).then_inc(*wr_in.up(16))

            @block.tensor
            def _(pe):
                pe.wait_ge(*wr_in.at(16))
                for i, (a, n) in enumerate(TILES):
                    for c in range(DC):
                        mm = pe.matmul(k.ps[0:n, 0, NE * i:NE * i + NE], k.act[:, c, a:a + n], wr[:, c, :], start=c == 0, stop=c == DC - 1)
                mm.then_inc(*logit.up())
                for i, (a, n) in enumerate(TILES):
                    for u in range(2):
                        for c in range(4):
                            mm = pe.transpose(k.ps[0:n, 2 + 2 * i + u, P * c:P * c + P], k.act[:, 4 * u + c, a:a + n], k.const("ident"))
                        mm.then_inc(*turned.up())
                pe.wait_ge(*chose.at(1))
                for i in range(3):
                    for e in range(i + 1):
                        pe.matmul(k.ps[:, 1, NE * i:NE * i + NE], k.const("ones") if e < i else k.const("before"), chosen[:, e, :],
                                  start=e == 0, stop=e == i)
                for i in range(3):
                    mm = pe.matmul(k.ps[:, 1, 32:32 + NE], k.const("ones"), chosen[:, i, :], start=i == 0, stop=i == 2)
                mm.then_inc(*ranked.up())

            @block.scalar
            def _(act):
                for n in range(6):
                    act.wait_ge(*turned.at(n + 1))
                    rows = TILES[n // 2][1]
                    act.copy(moe["tokens_hi"][0:rows, n // 2, 512 * (n % 2):512 * (n % 2) + 512], k.ps[0:rows, 2 + n, :]).then_inc(*copied.up())
                act.wait_ge(*exp_in.at(1))
                act.activation(gate[:, :, :], gate[:, :, :], ACT.Exp).then_inc(*exped.up())

            @block.vector
            def _(dve):
                def then(ins, sig=dve_step):
                    ins.then_inc(*sig.up())
                    dve.wait_ge(*sig.all())
                then(dve.memset(lg[:, :, :], 0.0))
                dve.wait_ge(*logit.at(1))
                dve.tensor_copy(lg[0:TS, 2, :], k.ps[0:TS, 0, 16:24]).then_inc(*dve_step.up())
                then(dve.tensor_copy(lg[:, 0:2, :], k.ps[:, 0, 0:16].rearrange("p (i e) -> p i e", i=2)))
                other = lg[:, :, :].unsqueeze(2).broadcast_to([P, 3, NE, NE])
                mine = lg[:, :, :].unsqueeze(3).broadcast_to([P, 3, NE, NE])
                then(dve.tensor_tensor(gt[:, :, :, :], other, mine, ALU.is_gt))
                then(dve.tensor_tensor(eq[:, :, :, :], other, mine, ALU.is_equal))
                earlier = k.const("earlier_expert").rearrange("p (e f) -> p e f", e=NE).unsqueeze(1).broadcast_to([P, 3, NE, NE])
                then(dve.tensor_tensor(eq[:, :, :, :], eq[:, :, :, :], earlier, ALU.mult))
                then(dve.tensor_tensor(gt[:, :, :, :], gt[:, :, :, :], eq[:, :, :, :], ALU.add))
                then(dve.tensor_reduce(chosen[:, :, :], gt[:, :, :, :], AX, ALU.add))
                then(dve.tensor_scalar(chosen[:, :, :], chosen[:, :, :], 2.0, None, ALU.is_lt))
                valid = k.const("valid").rearrange("p (i e) -> p i e", i=3)
                then(dve.tensor_tensor(chosen[:, :, :], chosen[:, :, :], valid, ALU.mult), chose)
                for n in range(6):
                    dve.wait_ge(*copied.at(n + 1))
                    rows, at = TILES[n // 2][1], slice(512 * (n % 2), 512 * (n % 2) + 512)
                    dve.tensor_tensor(moe["tokens_lo"][0:rows, n // 2, at], k.ps[0:rows, 2 + n, :],
                                      moe["tokens_hi"][0:rows, n // 2, at].bitcast(F32), ALU.subtract).then_inc(*dve_step.up())
                then(dve.tensor_reduce(small[:, :, 0:1], lg[:, :, :], AX, ALU.max))
                then(dve.tensor_tensor(gate[:, :, :], lg[:, :, :], small[:, :, 0:1].broadcast_to([P, 3, NE]), ALU.subtract), exp_in)
                dve.wait_ge(*exped.at(1))
                then(dve.tensor_tensor(gate[:, :, :], gate[:, :, :], chosen[:, :, :], ALU.mult))
                then(dve.tensor_reduce(small[:, :, 1:2], gate[:, :, :], AX, ALU.add))
                then(dve.tensor_scalar(small[:, :, 1:2], small[:, :, 1:2], 1e-30, None, ALU.max))
                then(dve.reciprocal(small[:, :, 1:2], small[:, :, 1:2]))
                then(dve.tensor_tensor(gate[:, :, :], gate[:, :, :], small[:, :, 1:2].broadcast_to([P, 3, NE]), ALU.mult))
                dve.wait_ge(*ranked.at(1))
                then(dve.tensor_copy(cnt[:, 0, :], k.ps[:, 1, 32:32 + NE]))
                then(dve.scalar_tensor_tensor(place[:, :, :], k.ps[:, 1, 0:24].rearrange("p (i e) -> p i e", i=3), 1.0, chosen[:, :, :],
                                              ALU.add, ALU.mult))
                then(dve.tensor_scalar(cnt[:, 1, :], cnt[:, 0, :], 0.0, None, ALU.is_gt))
                for edge in (128.0, 256.0):
                    then(dve.scalar_tensor_tensor(cnt[:, 1, :], cnt[:, 0, :], edge, cnt[:, 1, :], ALU.is_gt, ALU.add))
                then(dve.tensor_tensor_scan(cnt[:, 2, :], k.ones_wide[:, 0:NE], cnt[:, 1, :], 0.0, ALU.mult, ALU.add))
                then(dve.tensor_tensor(cnt[:, 3, :], cnt[:, 2, :], cnt[:, 1, :], ALU.subtract))
                item = k.const("items").unsqueeze(2).broadcast_to([P, I, NE])
                per = lambda ap: ap.unsqueeze(1).broadcast_to([P, I, NE])
                then(dve.tensor_tensor(blk[:, :, :], item, per(cnt[:, 3, :]), ALU.subtract))
                then(dve.tensor_tensor(tmp[:, :, :], item, per(cnt[:, 2, :]), ALU.is_lt))
                then(dve.scalar_tensor_tensor(one[:, :, :], blk[:, :, :], 0.0, tmp[:, :, :], ALU.is_ge, ALU.mult))
                then(dve.scalar_tensor_tensor(blk[:, :, :], blk[:, :, :], float(P), one[:, :, :], ALU.mult, ALU.mult))
                then(dve.tensor_tensor(tmp[:, :, :], one[:, :, :], per(k.const("expert_ids")), ALU.mult))
                then(dve.tensor_reduce(ids[:, 0:I], tmp[:, :, :], AX, ALU.add))
                then(dve.tensor_copy(ids[:, I:I + 1], cnt[:, 2, NE - 1:NE]))
                then(dve.tensor_copy(moe["table"][:, :], ids[0:1, :]))
                for i in range(3):
                    then(dve.tensor_tensor(tmp[:, :, :], one[:, :, :], per(place[:, i, :]), ALU.mult))
                    then(dve.tensor_tensor(tmp2[:, :, :], blk[:, :, :], per(chosen[:, i, :]), ALU.mult))
                    then(dve.tensor_tensor(tmp[:, :, :], tmp[:, :, :], tmp2[:, :, :], ALU.subtract))
                    then(dve.tensor_reduce(moe["slot"][:, i, :], tmp[:, :, :], AX, ALU.add))
                    then(dve.tensor_tensor(tmp[:, :, :], one[:, :, :], per(gate[:, i, :]), ALU.mult))
                    then(dve.tensor_reduce(moe["gate"][:, i, :], tmp[:, :, :], AX, ALU.add))
                then(dve.tensor_scalar(moe["slot"][:, :, :], moe["slot"][:, :, :], -1.0, None, ALU.add))


def stage_experts(k, moe):
    GROUPS = FE // WCOLS
    UP = 4 * GROUPS
    BLOCKS = UP + FEC // 2
    HALF = SLOT // 2
    PARTS = 3
    I = MAX_ITEMS + 1
    GATHER = BLOCKS - 5
    slot_of, gate_of, table, tok_hi, tok_lo = (moe[x] for x in ("slot", "gate", "table", "tokens_hi", "tokens_lo"))
    ins = k.ins
    with ExitStack() as s:
        ring = k.sb(s, "moe_ring", [P, MOE_SLOTS, HALF])
        w_hi = k.sb(s, "moe_w_hi", [P, PARTS, HALF], F32R)
        w_lo = k.sb(s, "moe_w_lo", [P, PARTS, HALF], F32R)
        pick = k.sb(s, "pick", [P, 3, P], F32R)
        weigh = k.sb(s, "weigh", [P, 3, P])
        weighT = k.sb(s, "weigh_t", [P, T])
        xg = [k.sb(s, "item_tokens" + x, [P, DC, P], F32R) for x in ("_hi", "_lo")]
        hidT = [k.sb(s, "hid_t" + x, [P, FEC, P], F32R) for x in ("_hi", "_lo")]
        hid = k.sb(s, "hid", [P, 2, WCOLS])
        free = k.act[:, :, :].rearrange("p c t -> p (c t)")
        gated = free[:, 0:2 * WCOLS].rearrange("p (a n) -> p a n", a=2)
        y = free[:, 2 * WCOLS:2 * WCOLS + D]
        names = ("slot_free", "part_free", "hi_ready", "pick_ready", "gathered", "xg_act", "xg_dve", "silu_done", "hid_done",
                 "hid_turned", "hidt_hi", "hidt_lo", "weigh_turned", "weigh_copied", "y_low", "y_high", "spread", "added", "zeroed")
        n_ = {x: k.count("m_" + x).sem for x in names}
        loaded = [k.count(f"m_loaded{x}").sem for x in range(MOE_SLOTS)]

        def used(i, b):
            return n_["part_free"], i * BLOCKS + (PARTS + b + 1)

        def count_of(eng):
            return eng.value_load(table[0:1, I:I + 1], min_val=1, max_val=MAX_ITEMS)

        def shaped(buf, b):
            return buf.rearrange("p (c f) -> p c f", c=4 if b < UP else 2)

        with k.stage() as block:
            @block.sync
            def _(sp):
                n_items = count_of(sp)
                with sp.Fori(0, n_items) as i:
                    e = sp.value_load(table[0:1, bass.ds(i, 1)], min_val=0, max_val=NE - 1)
                    for b in range(BLOCKS):
                        sp.wait_ge(n_["slot_free"], i * BLOCKS + (b + 1))
                        if b < UP:
                            w = ins["we3" if b // 2 % 2 else "we1"][0, bass.ds(e, 1)].rearrange("a (c p) f -> p (a c) f", p=P)
                            src = w[:, 4 * (b % 2):4 * (b % 2) + 4, WCOLS * (b // 4):WCOLS * (b // 4) + WCOLS]
                        else:
                            w = ins["we2"][0, bass.ds(e, 1)].rearrange("a (f p) d -> p (a f) d", p=P)
                            src = w[:, 2 * (b - UP):2 * (b - UP) + 2, :]
                        sp.dma_start(shaped(ring[:, b % MOE_SLOTS, :], b), src).then_inc(loaded[b % MOE_SLOTS], 16)

            @block.gpsimd
            def _(pool):
                pool.sem_inc(n_["slot_free"], MOE_SLOTS)
                pool.sem_inc(n_["part_free"], PARTS)

            @block.tensor
            def _(pe):
                ident = k.const("ident")

                def gather():
                    for tok, first_bank in ((tok_hi, 6), (tok_lo, 0)):
                        for c in range(DC):
                            for t, (_, n) in enumerate(TILES):
                                mm = pe.matmul(k.ps[:, first_bank + c // 4, P * (c % 4):P * (c % 4) + P],
                                               tok[0:n, t, P * c:P * c + P], pick[0:n, t, :], start=t == 0, stop=t == 2)
                    mm.then_inc(n_["gathered"], 1)

                def turn(i, n):
                    pe.wait_ge(n_["hid_done"], i * GROUPS + (n + 1))
                    if n >= 2:
                        pe.wait_ge(n_["hidt_hi"], i * GROUPS + (n - 1))
                        pe.wait_ge(n_["hidt_lo"], i * GROUPS + (n - 1))
                    for j in range(4):
                        mm = pe.transpose(k.ps[:, 6 + n % 2, P * j:P * j + P], hid[:, n % 2, P * j:P * j + P], ident)
                    mm.then_inc(n_["hid_turned"], 1)

                def spread(i, m):
                    if m == 0:
                        pe.wait_ge(n_["y_low"], i + 1)
                        pe.wait_ge(n_["y_high"], i + 1)
                    if m >= 2:
                        pe.wait_ge(n_["added"], i * DC + (m - 1))
                    pe.matmul(k.ps[:, 4 + m % 2, 0:T], y[:, P * m:P * m + P], weighT[:, :], start=True, stop=True)\
                      .then_inc(n_["spread"], 1)

                def use(i, b, products):
                    hi, lo = shaped(w_hi[:, b % PARTS, :], b), shaped(w_lo[:, b % PARTS, :], b)
                    x = xg if b < UP else hidT
                    pe.wait_ge(n_["hi_ready"], i * BLOCKS + (b + 1))
                    for part in (0, 1):
                        for out, c, (r, cols), first, last in products:
                            pe.matmul(out, x[part][:, c, :], hi[:, r, cols], start=first and part == 0, stop=False)
                    pe.wait_ge(n_["slot_free"], i * BLOCKS + (MOE_SLOTS + b + 1))
                    for out, c, (r, cols), first, last in products:
                        mm = pe.matmul(out, x[0][:, c, :], lo[:, r, cols], start=False, stop=last)
                    mm.then_inc(n_["part_free"], 1)

                pe.wait_ge(n_["zeroed"], 2)
                for u in range(2):
                    mm = pe.matmul(k.ps[:, 4 + u, :], hid[:, 0, 0:P], k.core[:, 0:512], start=True, stop=True)
                pe.wait_ge(n_["pick_ready"], 1)
                gather()
                n_items = count_of(pe)
                with pe.Fori(0, n_items) as i:
                    pe.wait_ge(n_["xg_act"], i + 1)
                    pe.wait_ge(n_["xg_dve"], i + 1)
                    for n in range(GROUPS):
                        if n >= 2:
                            pe.wait_ge(n_["hid_done"], i * GROUPS + (n - 1))
                        for b in range(4 * n, 4 * n + 4):
                            out = k.ps[:, 2 * (b // 2 % 2) + n % 2, :]
                            use(i, b, [(out, 4 * (b % 2) + c, (c, slice(0, WCOLS)), b % 2 == 0 and c == 0, b % 2 == 1 and c == 3)
                                       for c in range(4)])
                        if n < 4:
                            spread(i, 2 * n)
                            spread(i, 2 * n + 1)
                        if n == 4:
                            pe.wait_ge(n_["added"], i * DC + (DC - 1))
                            for t, (a, m) in enumerate(TILES):
                                mm = pe.transpose(k.ps[:, 4, a:a + m], weigh[0:m, t, :], ident[0:m, 0:m])
                            mm.then_inc(n_["weigh_turned"], 1)
                        if n >= 1:
                            turn(i, n - 1)
                    pe.wait_ge(n_["weigh_copied"], i + 1)
                    pe.wait_ge(n_["added"], i * DC + DC)
                    for b in range(UP, BLOCKS):
                        r = b - UP
                        if r % 2 == 0:
                            pe.wait_ge(n_["hidt_hi"], i * GROUPS + (r // 2 + 1))
                            pe.wait_ge(n_["hidt_lo"], i * GROUPS + (r // 2 + 1))
                        use(i, b, [(k.ps[:, 4 + u, :], 2 * r + j, (j, slice(512 * u, 512 * u + 512)), r == 0 and j == 0,
                                    b == BLOCKS - 1 and j == 1) for j in range(2) for u in range(2)])
                        if b == UP + 3:
                            turn(i, GROUPS - 1)
                        if b == GATHER:
                            pe.wait_ge(n_["pick_ready"], i + 2)
                            pe.wait_ge(n_["hidt_hi"], i * GROUPS + GROUPS)
                            pe.wait_ge(n_["hidt_lo"], i * GROUPS + GROUPS)
                            gather()
                for m in range(DC):
                    spread(n_items, m)

            @block.vector
            def _(dve):
                def picks(col):
                    for t, (_, n) in enumerate(TILES):
                        at = slot_of[0:n, t, col]
                        dve.tensor_scalar(pick[0:n, t, :], k.const("slots")[0:n, :], at, None, ALU.is_equal)
                        ins_ = dve.tensor_scalar(weigh[0:n, t, :], k.const("slots")[0:n, :], at, gate_of[0:n, t, col],
                                                 ALU.is_equal, ALU.mult)
                    ins_.then_inc(n_["pick_ready"], 1)

                def take_tokens(n):
                    dve.wait_ge(n_["gathered"], n)
                    dve.tensor_copy(xg[0][:, 4:8, :], k.ps[:, 7, :].rearrange("p (c n) -> p c n", c=4))
                    dve.tensor_copy(xg[1][:, 4:8, :], k.ps[:, 1, :].rearrange("p (c n) -> p c n", c=4)).then_inc(n_["xg_dve"], 1)

                def take_y(i):
                    dve.wait_ge(*used(i, -1))
                    dve.tensor_copy(y[:, 512:1024], k.ps[:, 5, :]).then_inc(n_["y_high"], 1)

                def add(i, m):
                    dve.wait_ge(n_["spread"], i * DC + (m + 1))
                    dve.tensor_tensor(k.residual[:, m, :], k.residual[:, m, :], k.ps[:, 4 + m % 2, 0:T], ALU.add).then_inc(n_["added"], 1)

                dve.memset(weighT[:, :], 0.0).then_inc(n_["zeroed"], 1)
                dve.memset(hid[:, 0, 0:P], 0.0).then_inc(n_["zeroed"], 1)
                picks(slice(0, 1))
                take_tokens(1)
                n_items = count_of(dve)
                with dve.Fori(0, n_items) as i:
                    for b in range(BLOCKS):
                        dve.wait_ge(n_["hi_ready"], i * BLOCKS + (b + 1))
                        dve.tensor_tensor(w_lo[:, b % PARTS, :], ring[:, b % MOE_SLOTS, :], w_hi[:, b % PARTS, :].bitcast(F32),
                                          ALU.subtract).then_inc(n_["slot_free"], 1)
                        if b == 2:
                            take_y(i)
                        n = (b - 5) // 4
                        if b % 4 == 1 and 0 <= n < GROUPS:
                            dve.wait_ge(n_["silu_done"], i * GROUPS + (n + 1))
                            if n >= 2:
                                dve.wait_ge(n_["hid_turned"], i * GROUPS + (n - 1))
                            dve.tensor_tensor(hid[:, n % 2, :], gated[:, n % 2, :], k.ps[:, 2 + n % 2, :], ALU.mult).then_inc(n_["hid_done"], 1)
                            if n < 4:
                                add(i, 2 * n)
                                add(i, 2 * n + 1)
                            if n == 4:
                                dve.wait_ge(n_["weigh_turned"], i + 1)
                                dve.tensor_copy(weighT[:, :], k.ps[:, 4, 0:T]).then_inc(n_["weigh_copied"], 1)
                            if n == 5:
                                picks(bass.ds(i + 1, 1))
                        n = (b - 9) // 4
                        if b % 4 == 1 and 0 <= n < GROUPS:
                            dve.wait_ge(n_["hidt_hi"], i * GROUPS + (n + 1))
                            dve.tensor_tensor(hidT[1][:, 4 * n:4 * n + 4, :], k.ps[:, 6 + n % 2, :].rearrange("p (f n) -> p f n", f=4),
                                              hidT[0][:, 4 * n:4 * n + 4, :].bitcast(F32), ALU.subtract).then_inc(n_["hidt_lo"], 1)
                        if b == GATHER + 3:
                            take_tokens(i + 2)
                take_y(n_items)
                for m in range(DC):
                    add(n_items, m)

            @block.scalar
            def _(act):
                def take_tokens(n):
                    act.wait_ge(n_["gathered"], n)
                    act.copy(xg[0][:, 0:4, :], k.ps[:, 6, :].rearrange("p (c n) -> p c n", c=4))
                    act.copy(xg[1][:, 0:4, :], k.ps[:, 0, :].rearrange("p (c n) -> p c n", c=4)).then_inc(n_["xg_act"], 1)

                def take_y(i):
                    act.wait_ge(*used(i, -1))
                    act.copy(y[:, 0:512], k.ps[:, 4, :]).then_inc(n_["y_low"], 1)

                take_tokens(1)
                n_items = count_of(act)
                with act.Fori(0, n_items) as i:
                    for b in range(BLOCKS):
                        act.wait_ge(loaded[b % MOE_SLOTS], i * (16 * BLOCKS // MOE_SLOTS) + 16 * (b // MOE_SLOTS + 1))
                        act.wait_ge(n_["part_free"], i * BLOCKS + (b + 1))
                        act.copy(w_hi[:, b % PARTS, :], ring[:, b % MOE_SLOTS, :]).then_inc(n_["hi_ready"], 1)
                        if b == 2:
                            take_y(i)
                        n = (b - 5) // 4
                        if b % 4 == 1 and 0 <= n < GROUPS:
                            act.wait_ge(*used(i, 4 * n + 3))
                            if n >= 2:
                                act.wait_ge(n_["hid_done"], i * GROUPS + (n - 1))
                            act.activation(gated[:, n % 2, :], k.ps[:, n % 2, :], ACT.Silu).then_inc(n_["silu_done"], 1)
                        n = (b - 9) // 4
                        if b % 4 == 1 and 0 <= n < GROUPS:
                            act.wait_ge(n_["hid_turned"], i * GROUPS + (n + 1))
                            act.copy(hidT[0][:, 4 * n:4 * n + 4, :], k.ps[:, 6 + n % 2, :].rearrange("p (f n) -> p f n", f=4)).then_inc(n_["hidt_hi"], 1)
                        if b == GATHER + 3:
                            take_tokens(i + 2)
                take_y(n_items)


def stage_store_tokens(k):
    with ExitStack() as s:
        tok = k.sb(s, "out_tokens", [P, 3, D])
        turned, copied, stored = k.count("turned"), (k.count("copied"), k.count("copied_odd")), k.count("out_stored")
        with k.stage() as block:
            @block.tensor
            def _(pe):
                for n in range(6):
                    i, u = n // 2, n % 2
                    a, rows = TILES[i]
                    for c in range(4):
                        mm = pe.transpose(k.ps[0:rows, n, P * c:P * c + P], k.act[:, 4 * u + c, a:a + rows], k.const("ident"))
                    mm.then_inc(*turned.up())

            def copier(eng, u):
                for i in range(3):
                    rows = TILES[i][1]
                    eng.wait_ge(*turned.at(2 * i + u + 1))
                    copy(eng, tok[0:rows, i, 512 * u:512 * u + 512], k.ps[0:rows, 2 * i + u, :]).then_inc(*copied[u].up())

            @block.scalar
            def _(act):
                copier(act, 0)

            @block.vector
            def _(dve):
                copier(dve, 1)

            @block.sync
            def _(sp):
                for i, (a, rows) in enumerate(TILES):
                    for u in range(2):
                        sp.wait_ge(*copied[u].at(i + 1))
                    dst = k.outs[0][0, a:a + rows, :] if i < 2 else k.outs[1].rearrange("b t d -> (b t) d")
                    sp.dma_start(dst, tok[0:rows, i, :]).then_inc(*stored.up(16))
                sp.wait_ge(*stored.at(48))


def program(nc, ins, outs, core, attn):
    with ExitStack() as ctx:
        k = Kernel(nc, ctx, ins, outs, core, attn)
        with ExitStack() as early:
            k.ring = k.sb(early, "ring", [P, EARLY_SLOTS, SLOT])
            stage_load(k)
            stage_norm(k, "norm_mix_even")
            with ExitStack() as s:
                qkv = k.sb(s, "qkv", [P, 24, T])
                with ExitStack() as g:
                    stage_qkv(k, qkv, split(k, g, "_qkv", k.act, DC))
                kv = k.sb(s, "kv", [P, 3, 2048])
                k.attn = k.sb(s, "attn", [P, k.attn_n])
                stage_kv_tokens(k, qkv, kv)
                for mixer in "AB":
                    stage_prompt_attention(k, mixer, qkv, kv)
                    for group in range(2):
                        stage_sample_attention(k, mixer, group, qkv, kv)
            with ExitStack() as g:
                stage_out_even(k, split(k, g, "_out_even", k.act, DC))
            stage_norm(k, "norm_ffn_even")
            with ExitStack() as s:
                hidden = [k.sb(s, f"hidden{n}", [P, FC, T], F32R) for n in ("_hi", "_lo")]
                with ExitStack() as g:
                    stage_ffn_up(k, split(k, g, "_up", k.act, DC), *hidden)
                gemm_rows(k, "_down", 19, FC, hidden)
            stage_norm(k, "norm_mix_odd")
            with ExitStack() as s:
                proj = k.sb(s, "proj", [P, 24, T])
                dt = k.sb(s, "dt", [HM, T])
                xc = k.sb(s, "xc", [P, CC, T])
                with ExitStack() as c:
                    conv_in = k.sb(c, "conv_in", [P, CC, TP + 3])
                    conv_in_s = k.sb(c, "conv_in_s", [P, CC, NB, NT + 3])
                    with ExitStack() as g:
                        stage_in_odd(k, split(k, g, "_in_odd", k.act, DC), proj, conv_in, conv_in_s, dt)
                    stage_conv(k, conv_in, conv_in_s, xc)
                mixed_out = k.sb(s, "mixed_out", [P, 12, T])
                with ExitStack() as c:
                    hg = {"k": k.sb(c, "one_minus_f", [P, 4, T]), "g": k.sb(c, "log_f_sums", [P, 4, T])}
                    stage_hgrn_gates(k, proj, hg)
                    stage_hgrn(k, proj, hg, mixed_out)
                with ExitStack() as c:
                    dta = {"acum": k.sb(c, "acum", [HM, T]), "wend": k.sb(c, "wend", [HM, T]), "tok": k.sb(c, "dt_tokens", [P, 3, 48]),
                           "skip": k.sb(c, "skip", [P, 8]), "sq": k.act, "rs": k.sb(c, "group_rstd", [P, 4, T])}
                    stage_dt(k, dt, dta)
                    stage_ssd(k, proj, xc, dt, dta, mixed_out)
                with ExitStack() as c:
                    parts = split(k, c, "_out_odd", mixed_out, 12)
                    gemm_rows(k, "_out_odd", 35, 12, parts)
        stage_norm(k, "norm_ffn_odd")
        with ExitStack() as s:
            moe = {"tokens_hi": k.sb(s, "tokens_hi", [P, 3, D], F32R), "tokens_lo": k.sb(s, "tokens_lo", [P, 3, D], F32R),
                   "slot": k.sb(s, "item_slot", [P, 3, MAX_ITEMS + 1]),
                   "gate": k.sb(s, "item_gate", [P, 3, MAX_ITEMS + 1]), "table": k.sb(s, "item_table", [1, MAX_ITEMS + 2], I32)}
            stage_route(k, moe)
            stage_experts(k, moe)
        stage_norm(k, "norm_final")
        stage_store_tokens(k)


_INS = ['x_prompt', 'x_sample', 'cache_win_k', 'cache_win_v', 'cache_sb_k', 'cache_sb_v', 'page_table',
        'state_hgrn', 'state_ssm', 'state_conv', 'norm_mix_even', 'w_in_even', 'w_out_even', 'sb_bias',
        'norm_ffn_even', 'w1_ffn', 'w3_ffn', 'w2_ffn', 'norm_mix_odd', 'w_in_odd', 'hgrn_lb_logits',
        'hgrn_gain', 'conv_w', 'conv_b', 'dt_bias', 'a_log', 'd_skip', 'ssm_gain', 'w_out_odd',
        'norm_ffn_odd', 'w_router', 'we1', 'we3', 'we2', 'norm_final']
_OUTS = [(1, TP, D), (NB, NT, D), (1, 1, TP, 8, HD), (1, 1, TP, 8, HD), (NB, 1, NT, 8, HD), (NB, 1, NT, 8, HD),
         (1, 1, TP, 8, HD), (1, 1, TP, 8, HD), (NB, 1, NT, 8, HD), (NB, 1, NT, 8, HD),
         (1, 1, HC, P, P), (NB, 1, HC, P, P), (1, 1, HM, 64, 64), (NB, 1, HM, 64, 64), (1, 1, 3, 1536), (NB, 1, 3, 1536)]


def kernel(**inputs):
    import numpy as _np
    import concourse.bacc as _bacc
    from concourse import mybir as _mybir
    from concourse.bass_utils import run_bass_kernel_spmd as _run

    nc = _bacc.Bacc("TRN2", target_bir_lowering=False, num_devices=1)
    core, attn = shape_constants()
    arrays, ins, outs = {}, {}, []
    given = {name: _np.ascontiguousarray(inputs[name]) for name in _INS}
    given["core_tables"] = _np.concatenate(list(core.values()), 1)
    given["attn_tables"] = _np.concatenate(list(attn.values()), 1)
    for name, a in given.items():
        arrays[f"in_{name}_dram"] = a
        ins[name] = nc.dram_tensor(f"in_{name}_dram", a.shape, _mybir.dt.from_np(a.dtype), kind="ExternalInput").ap()
    for i, shape in enumerate(_OUTS):
        outs.append(nc.dram_tensor(f"out_{i}_dram", shape, F32, kind="ExternalOutput").ap())
    program(nc, ins, outs, core, attn)
    r = _run(nc, [arrays], core_ids=[0])
    return tuple(r.results[0][f"out_{i}_dram"] for i in range(len(_OUTS)))
```

```python
from contextlib import ExitStack

import concourse.bass as bass
import numpy as np
from concourse import mybir

F32 = mybir.dt.float32
F32R = mybir.dt.float32r
I32 = mybir.dt.int32
ALU = mybir.AluOpType
ACT = mybir.ActivationFunctionType
AX = mybir.AxisListType.X

P = 128
D = 1024
DC = D // P
TP = 256
NB, NT = 8, 4
TS = NB * NT
T = TP + TS
TILES = ((0, P), (P, P), (TP, TS))
HD = 64
PAST = 256
PAGE = 128
SCALE = HD ** -0.5
NEG = -1.0e30
FF = 2816
FC = FF // P
HC = 4
HM = 16
NE = 8
FE = 3584
FEC = FE // P
EPS = 1e-6
WCOLS = 512
SLOT = DC * WCOLS
EARLY_SLOTS = 3
MOE_SLOTS = 7
MAX_ITEMS = NE + 2 * T // P
IN_ODD_BLOCKS = (6, 7, 8, 9, 1, 0, 2, 3, 4, 5)
DIL_PATTERNS = ((128, 1), (512, 4), (2048, 16))

VEC = {"norm_mix_even": 0, "norm_ffn_even": 8, "norm_mix_odd": 16, "norm_ffn_odd": 24, "norm_final": 32,
       "hgrn_lb_logits": 40, "hgrn_gain": 48, "ssm_gain": 52, "conv_w": 60, "conv_b": 108}
NVEC = 120
CC = 12


def shape_constants():
    p = np.arange(P)
    c = {}
    c["ident"] = np.eye(P)
    c["ones"] = np.ones((P, P))
    run = np.ones(T)
    run[[0] + [TP + NT * b for b in range(NB)]] = 0
    c["running"] = np.tile(run, (P, 1))
    c["before"] = (p[:, None] < p[None, :]) * 1.0
    c["slots"] = np.tile(p, (P, 1))
    c["items"] = np.tile(np.arange(MAX_ITEMS + 1), (P, 1))
    c["valid"] = np.repeat(np.stack([p < n for _, n in TILES], 1), NE, 1) * 1.0
    e = np.arange(NE)
    c["earlier_expert"] = np.tile(((e[None, :] < e[:, None]) * 1.0).reshape(1, -1), (P, 1))
    c["expert_ids"] = np.tile(e, (P, 1))
    c["batch_of"] = (p[:, None] // NT == np.arange(NB)[None, :]) * 1.0
    pair = np.zeros((P, 8, P))
    for h in range(HM):
        pair[h, h // 2, 64 * (h % 2):64 * (h % 2) + 64] = 1
    c["head_pair"] = pair.reshape(P, -1)
    future = np.where(p[:, None] <= p[None, :], 0.0, NEG)
    c["ssd_future"] = np.concatenate([future, np.zeros((P, P))], 1)
    t = np.arange(TS)
    fs = np.full((P, TS), NEG)
    fs[:TS] = np.where((t[:, None] // NT == t[None, :] // NT) & (t[:, None] <= t[None, :]), 0.0, NEG)
    c["ssd_future_s"] = fs
    lv = []
    for l in range(7):
        h = 1 << l
        s, q = p[:, None], p[None, :]
        lv.append((s // (2 * h) == q // (2 * h)) & (s % (2 * h) < h) & (q % (2 * h) >= h))
    c["level"] = np.stack(lv, 1).reshape(P, -1)
    core = {k: np.asarray(v, np.float32) for k, v in c.items()}

    def log_count(dist):
        n = np.zeros(dist.shape)
        for window, dil in DIL_PATTERNS:
            n += (dist >= 0) & (dist <= window) & (dist % dil == 0)
        return np.where(n > 0, np.log(np.maximum(n, 1)), NEG)

    a = {}
    slope = 2.0 ** (-8.0 * np.arange(1, 9) / 8)
    d = p[:, None] + P - np.arange(2 * P)[None, :]
    lc = log_count(d)
    order = [0, 2, 1, 3, 4, 6, 5, 7]
    a["alibi"] = np.stack([np.where(lc > NEG, lc - slope[h] * d, NEG) for h in order], 1).reshape(P, -1)
    a["stick_on"] = (d > 0) * 1.0
    a["stick_off"] = np.where(d > 0, 0.0, NEG)
    key = np.arange(PAST + TS)
    al, on = [], []
    for g in range(2):
        b, h, t = 4 * g + p // 32, (p % 32) // NT, p % NT
        new = key >= PAST
        kb, kt = (key - PAST) // NT, (key - PAST) % NT
        pos = np.where(new, PAST + kt, key)
        dist = PAST + t[:, None] - pos[None, :]
        mine = ~new[None, :] | (kb[None, :] == b[:, None])
        lc = np.where(mine, log_count(dist), NEG)
        al.append(np.where(lc > NEG, lc - slope[h][:, None] * dist, NEG))
        on.append(mine & (dist > 0))
    a["alibi_s"] = np.concatenate(al, 1)
    a["stick_on_s"] = np.concatenate(on, 1) * 1.0
    a["stick_off_s"] = np.where(np.concatenate(on, 1), 0.0, NEG)
    a["own_head"] = ((p[:, None] % 32) // NT == np.arange(8)[None, :]) * 1.0
    a["row_token"] = (NT * (p[:, None] // 32) + p[:, None] % NT == np.arange(16)[None, :]) * 1.0
    rh = np.zeros((P, P))
    rh[(p % 32) // NT, p] = 1
    a["row_head"] = rh
    attn = {k: np.asarray(v, np.float32) for k, v in a.items()}
    return core, attn


def columns(tables):
    at, out = 0, {}
    for k, v in tables.items():
        out[k] = (at, at + v.shape[1])
        at += v.shape[1]
    return out, at


class Count:

    def __init__(self, sem):
        self.sem, self.total, self.base = sem, 0, 0

    def up(self, by=1):
        self.total += by
        return self.sem, by

    def at(self, n):
        assert self.base + n > 0
        return self.sem, self.base + n

    def all(self):
        return self.sem, self.total


class Kernel:

    def __init__(self, nc, ctx, ins, outs, core, attn):
        self.nc, self.ins, self.outs = nc, ins, outs
        self.ctx = ctx
        self.counts = {}
        self.core_at, self.core_n = columns(core)
        self.attn_at, self.attn_n = columns(attn)
        self.ps = ctx.enter_context(nc.psum_tensor("ps", [P, 8, 512], F32))
        self.residual = self.sb(ctx, "residual", [P, DC, T])
        self.act = self.sb(ctx, "act", [P, DC, T])
        self.core = self.sb(ctx, "core", [P, self.core_n])
        self.vec = self.sb(ctx, "vec", [P, NVEC])
        self.ones_wide = self.sb(ctx, "ones_wide", [P, T])
        self.blocks = self.weight_blocks()
        self.issued, self.landed, self.freed = 0, {}, {}

    def sb(self, ctx, name, shape, dt=F32):
        return ctx.enter_context(self.nc.sbuf_tensor(name, shape, dt))

    def count(self, name):
        if name not in self.counts:
            self.counts[name] = Count(self.ctx.enter_context(self.nc.semaphore(name)))
        return self.counts[name]

    def stage(self):
        for c in self.counts.values():
            c.base = c.total
        return self.nc.Block()

    def const(self, name):
        a, b = self.core_at[name]
        return self.core[:, a:b]

    def table(self, name):
        a, b = self.attn_at[name]
        return self.attn[:, a:b]

    def weight_blocks(self):
        i = self.ins
        cols = lambda w, a, n: (w[0].rearrange("(k p) n -> p k n", p=P)[:, :, a:a + n], "cols", n)
        rows = lambda w, a, n: (w[0].rearrange("(k p) n -> p k n", p=P)[:, a:a + n, :], "rows", n)
        blocks = [cols(i["w_in_even"], WCOLS * n, WCOLS) for n in range(6)]
        blocks += [cols(i["w_out_even"], WCOLS * n, WCOLS) for n in range(2)]
        for n in range(FF // 256):
            blocks.append((n, "pair", 256))
        blocks += [rows(i["w2_ffn"], 4 * n, min(4, FC - 4 * n)) for n in range(-(-FC // 4))]
        blocks += [cols(i["w_in_odd"], WCOLS * n, min(WCOLS, 4624 - WCOLS * n)) for n in IN_ODD_BLOCKS]
        blocks += [rows(i["w_out_odd"], 4 * n, 4) for n in range(3)]
        return blocks

    def slot(self, n, how, width):
        flat = self.ring[:, n % EARLY_SLOTS, :]
        if how == "cols":
            return flat[:, 0:DC * width].rearrange("p (k n) -> p k n", k=DC)
        if how == "rows":
            return flat[:, 0:width * D].rearrange("p (k n) -> p k n", k=width)
        return flat.rearrange("p (k w n) -> p k w n", k=DC, w=2)

    def stream(self, sp, upto):
        for n in range(self.issued, min(upto, len(self.blocks))):
            src, how, width = self.blocks[n]
            if n >= EARLY_SLOTS:
                sp.wait_ge(*self.freed[n - EARLY_SLOTS])
            loaded = self.count(f"block_loaded{n % EARLY_SLOTS}")
            dst = self.slot(n, how, width)
            if how == "pair":
                for w, name in enumerate(("w1_ffn", "w3_ffn")):
                    part = self.ins[name][0].rearrange("(k p) n -> p k n", p=P)[:, :, 256 * src:256 * src + 256]
                    sp.dma_start(dst[:, :, w, :], part).then_inc(*loaded.up(16))
            else:
                sp.dma_start(dst, src).then_inc(*loaded.up(16))
            self.landed[n] = loaded.sem, loaded.total
            self.issued = n + 1

    def arrived(self, n):
        return self.landed[n]


def stage_load(k, bias, bias8, pages):
    ins = k.ins
    with ExitStack() as s:
        tok = k.sb(s, "tok", [P, 3, D])
        rows = k.sb(s, "rows", [P, P])
        const_in, vec_in, x_in = k.count("const_in"), k.count("vec_in"), k.count("x_in")
        turned, copied = k.count("turned"), k.count("copied")
        with k.stage() as block:
            @block.sync
            def _(sp):
                sp.dma_start(k.core[:, :], ins["core_tables"]).then_inc(*const_in.up(16))
                sp.dma_start(tok[:, 0:2, :], ins["x_prompt"][0].rearrange("(t p) d -> p t d", p=P)).then_inc(*x_in.up(16))
                sp.dma_start(tok[0:TS, 2, :], ins["x_sample"].rearrange("b t d -> (b t) d")).then_inc(*x_in.up(16))
                k.stream(sp, 1)
                sp.dma_start(k.attn[:, :], ins["attn_tables"]).then_inc(*k.count("tables_in").up(16))
                sp.dma_start(pages[:, :], ins["page_table"].rearrange("b j -> (b j)").unsqueeze(0)).then_inc(*k.count("pages_in").up(16))
                sp.dma_start(bias8[:, :], ins["sb_bias"].rearrange("a h -> h a")).then_inc(*k.count("bias_in").up(16))
                sp.dma_start(bias[:, :], ins["sb_bias"].broadcast_to([P, 8])).then_inc(*k.count("bias_in").up(16))
                k.stream(sp, EARLY_SLOTS)

            @block.scalar
            def _(act):
                act.dma_start(rows[0:NVEC, :], ins["vectors"]).then_inc(*vec_in.up(16))

            @block.tensor
            def _(pe):
                pe.wait_ge(*const_in.at(16))
                ident = k.const("ident")
                pe.wait_ge(*x_in.at(32))
                for c in range(DC):
                    if c >= 4:
                        pe.wait_ge(*copied.at(c - 3))
                    for i, (a, n) in enumerate(TILES):
                        mm = pe.transpose(k.ps[:, c % 4, a:a + n], tok[0:n, i, P * c:P * c + P], ident[0:n, 0:n])
                    mm.then_inc(*turned.up())
                pe.wait_ge(*vec_in.at(16))
                pe.transpose(k.ps[:, 4, 0:NVEC], rows[0:NVEC, :], ident[0:NVEC, 0:NVEC]).then_inc(*turned.up())

            @block.vector
            def _(dve):
                dve.memset(k.ones_wide[:, :], 1.0).then_inc(*k.count("zeroed").up())
                for c in range(DC):
                    dve.wait_ge(*turned.at(c + 1))
                    dve.tensor_copy(k.residual[:, c, :], k.ps[:, c % 4, 0:T]).then_inc(*copied.up())
                dve.wait_ge(*turned.at(DC + 1))
                dve.tensor_copy(k.vec[:, :], k.ps[:, 4, 0:NVEC]).then_inc(*copied.up())


class Norm:

    def __init__(self, k, s, gain, parts=None, sq=None):
        self.k, self.gain, self.parts = k, gain, parts
        self.sq = k.sb(s, f"sq_{gain}", [P, DC, T]) if sq is None else sq
        self.rstd = k.sb(s, f"rstd_{gain}", [P, T])
        self.squared, self.summed, self.mean, self.root = (k.count(n) for n in ("squared", "summed", "mean", "root"))
        self.normed, self.rounded, self.rest = k.count("normed"), k.count("x_rounded"), k.count("x_rest")

    def squares(self, act):
        for c in range(DC):
            act.activation(self.sq[:, c, :], self.k.residual[:, c, :], ACT.Square).then_inc(*self.squared.up())

    def sums(self, pe):
        for c in range(DC):
            pe.wait_ge(*self.squared.at(c + 1))
            mm = pe.matmul(self.k.ps[:, 0, 0:T], self.k.const("ones"), self.sq[:, c, :], start=c == 0, stop=c == DC - 1)
        mm.then_inc(*self.summed.up())

    def roots(self, act):
        rstd = self.rstd[:, :]
        act.wait_ge(*self.mean.at(1))
        act.activation(rstd, rstd, ACT.Ln).then_inc(*self.root.up())
        act.wait_ge(*self.root.at(1))
        act.activation(rstd, rstd, ACT.Exp, scale=-0.5).then_inc(*self.root.up())
        if self.parts:
            for c in range(DC):
                act.wait_ge(*self.normed.at(c + 1))
                act.copy(self.parts[0][:, c, :], self.k.act[:, c, :]).then_inc(*self.rounded.up())

    def apply(self, dve):
        k, parts = self.k, self.parts

        def take_rest(c):
            dve.wait_ge(*self.rounded.at(c + 1))
            dve.tensor_tensor(parts[1][:, c, :], k.act[:, c, :], parts[0][:, c, :].bitcast(F32), ALU.subtract).then_inc(*self.rest.up())

        dve.wait_ge(*self.summed.at(1))
        dve.tensor_scalar(self.rstd[:, :], k.ps[:, 0, 0:T], 1.0 / D, EPS, ALU.mult, ALU.add).then_inc(*self.mean.up())
        dve.wait_ge(*self.root.at(2))
        for c in range(DC):
            g = VEC[self.gain] + c
            dve.scalar_tensor_tensor(k.act[:, c, :], k.residual[:, c, :], k.vec[:, g:g + 1], self.rstd[:, :],
                                     ALU.mult, ALU.mult).then_inc(*self.normed.up())
            if parts and c >= 2:
                take_rest(c - 2)
        if parts:
            take_rest(DC - 2)
            take_rest(DC - 1)

    def await_chunk(self, pe, c):
        pe.wait_ge(*(self.rest if self.parts else self.normed).at(c + 1))


def parts_of(k, s, tag, chunks):
    return [k.sb(s, f"x{n}{tag}", [P, chunks, T], F32R) for n in ("_hi", "_lo")]


class SplitInput:

    def __init__(self, k, s, tag, x, chunks):
        self.x, self.parts, self.chunks = x, parts_of(k, s, tag, chunks), chunks
        self.rounded, self.rest = k.count("x_rounded"), k.count("x_rest")

    def round_pair(self, act, n):
        act.copy(self.parts[0][:, 2 * n:2 * n + 2, :], self.x[:, 2 * n:2 * n + 2, :]).then_inc(*self.rounded.up())

    def take_pair(self, dve, n):
        at = slice(2 * n, 2 * n + 2)
        dve.wait_ge(*self.rounded.at(n + 1))
        dve.tensor_tensor(self.parts[1][:, at, :], self.x[:, at, :], self.parts[0][:, at, :].bitcast(F32), ALU.subtract)\
           .then_inc(*self.rest.up())

    def await_chunk(self, pe, c):
        pe.wait_ge(*self.rest.at(c // 2 + 1))


class Split:

    def __init__(self, k, s, tag, halves, used):
        self.k, self.halves, self.used = k, halves, used
        self.hi = [k.sb(s, f"w_hi{n}{tag}", [P, SLOT // 2], F32R) for n in range(2)]
        self.lo = [k.sb(s, f"w_lo{n}{tag}", [P, SLOT // 2], F32R) for n in range(2)]
        self.hi_done, self.lo_done = k.count("hi_done"), k.count("lo_done")

    def view(self, buf, h):
        a, b = self.halves[h][3]
        return buf[h % 2][:, 0:a * b].rearrange("p (a b) -> p a b", a=a)

    def start(self):
        for h, (n, _, _, _) in enumerate(self.halves):
            self.k.freed[n] = self.lo_done.at(h + 1)

    def round_hi(self, act, h):
        if h >= len(self.halves):
            return
        n, first, raw, _ = self.halves[h]
        if first:
            act.wait_ge(*self.k.arrived(n))
        if h >= 2:
            act.wait_ge(*self.used(h - 2))
        act.copy(self.view(self.hi, h), raw).then_inc(*self.hi_done.up())

    def take_lo(self, dve, h):
        if h >= len(self.halves):
            return
        dve.wait_ge(*self.hi_done.at(h + 1))
        dve.tensor_tensor(self.view(self.lo, h), self.halves[h][2], self.view(self.hi, h).bitcast(F32), ALU.subtract)\
           .then_inc(*self.lo_done.up())

    def products(self, pe, out, h, cols, rows, x, first, last, norm=None):
        hi, lo = self.view(self.hi, h), self.view(self.lo, h)
        for c, r in enumerate(rows):
            if norm:
                norm.await_chunk(pe, r)
            pe.matmul(out, hi[:, c, cols], x[0][:, r, :], start=first and c == 0, stop=False)
            pe.matmul(out, hi[:, c, cols], x[1][:, r, :], start=False, stop=False)
        pe.wait_ge(*self.lo_done.at(h + 1))
        for c, r in enumerate(rows):
            mm = pe.matmul(out, lo[:, c, cols], x[0][:, r, :], start=False, stop=last and c == len(rows) - 1)
        return mm


def gemm(k, tag, first, widths, x, copy_out, by_vector=False, upto=None, load_more=None, gain=None):
    done, out = k.count("product_done"), (k.count("even_out"), k.count("odd_out"))
    halves = [(first + n, j == 0, k.slot(first + n, "cols", w)[:, :, 256 * j:256 * j + 256], (DC, 256))
              for n, w in enumerate(widths) for j in range(w // 256)]
    chunks = 2 * len(halves)
    with ExitStack() as s:
        sp_ = Split(k, s, tag, halves, lambda h: done.at(2 * h + 2))
        norm = Norm(k, s, gain, x) if gain else None
        source = norm or x
        x = x if norm else x.parts
        with k.stage() as block:
            sp_.start()

            @block.sync
            def _(sp):
                k.stream(sp, upto or first + len(widths) + EARLY_SLOTS)
                if load_more:
                    load_more(sp)

            @block.tensor
            def _(pe):
                if norm:
                    norm.sums(pe)
                for m in range(chunks):
                    h = m // 2
                    if m % 2 == 0:
                        pe.wait_ge(*sp_.hi_done.at(h + 1))
                    if m >= 8:
                        pe.wait_ge(*out[m % 2].at(m // 2 - 3))
                    sp_.products(pe, k.ps[:, m % 8, 0:T], h, slice(P * (m % 2), P * (m % 2) + P), range(DC), x, True, True,
                                 source if m == 0 else None).then_inc(*done.up())

            @block.scalar
            def _(act):
                if norm:
                    norm.squares(act)
                sp_.round_hi(act, 0)
                if norm:
                    norm.roots(act)
                else:
                    for n in range(DC // 2):
                        source.round_pair(act, n)
                sp_.round_hi(act, 1)
                for h in range(len(halves)):
                    if not by_vector:
                        act.wait_ge(*done.at(2 * h + 1))
                        copy_out(act, 2 * h).then_inc(*out[0].up())
                    sp_.round_hi(act, h + 2)

            @block.vector
            def _(dve):
                sp_.take_lo(dve, 0)
                if norm:
                    norm.apply(dve)
                else:
                    for n in range(DC // 2):
                        source.take_pair(dve, n)
                for h in range(len(halves)):
                    sp_.take_lo(dve, h + 1)
                    for m in range(2 * h + (not by_vector), 2 * h + 2):
                        dve.wait_ge(*done.at(m + 1))
                        copy_out(dve, m).then_inc(*out[m % 2].up())


def gemm_rows(k, tag, first, total, x, source=None):
    half_done, added = k.count("row_half_done"), k.count("residual_added")
    nblocks = -(-total // 4)
    halves = [(first + n, j == 0, k.slot(first + n, "rows", min(4, total - 4 * n))[:, 2 * j:2 * j + 2, :], (2, D))
              for n in range(nblocks) for j in range(min(4, total - 4 * n) // 2)]
    with ExitStack() as s:
        sp_ = Split(k, s, tag, halves, lambda h: half_done.at(h + 1))
        with k.stage() as block:
            sp_.start()

            @block.sync
            def _(sp):
                k.stream(sp, first + nblocks + EARLY_SLOTS)

            @block.tensor
            def _(pe):
                for h in range(len(halves)):
                    pe.wait_ge(*sp_.hi_done.at(h + 1))
                    for m in range(DC):
                        mm = sp_.products(pe, k.ps[:, m, 0:T], h, slice(P * m, P * m + P), range(2 * h, 2 * h + 2), x,
                                          h == 0, h == len(halves) - 1, source if m == 0 else None)
                    mm.then_inc(*half_done.up())

            @block.scalar
            def _(act):
                for h in range(len(halves)):
                    if source:
                        source.round_pair(act, h)
                    sp_.round_hi(act, h)

            @block.vector
            def _(dve):
                for h in range(len(halves)):
                    if source:
                        source.take_pair(dve, h)
                    sp_.take_lo(dve, h)
                dve.wait_ge(*half_done.at(len(halves)))
                for m in range(DC):
                    dve.tensor_tensor(k.residual[:, m, :], k.residual[:, m, :], k.ps[:, m, 0:T],
                                      ALU.add).then_inc(*added.up())


def copy(eng, out, in_):
    return eng.copy(out, in_) if eng.engine == mybir.EngineType.Activation else eng.tensor_copy(out, in_)



def stage_qkv(k, qkv, x, keys):
    def copy_out(eng, m):
        return copy(eng, qkv[:, m, :], k.ps[:, m % 8, 0:T])

    def load_keys(sp):
        sp.wait_ge(*k.freed[5])
        load_window(k, sp, "cache_win_k", keys, 0, [k.count(f"keys_in{b}") for b in range(4)])
    gemm(k, "_qkv", 0, [WCOLS] * 6, x, copy_out, upto=8, load_more=load_keys, gain="norm_mix_even")


def load_window(k, sp, name, dst, u, landed):
    for b in range(4):
        sp.dma_start(dst[:, b, :, :], k.ins[name][4 * u + b, 0].rearrange("(j p) h d -> p j (h d)", p=P)).then_inc(*landed[b].up(16))


def stage_kv_tokens(k, qkv, k_tokens, v_tokens):
    ins, outs = k.ins, k.outs
    jobs = [(i, c0) for i in range(3) for c0 in range(0, 16, 4)]
    turned, copied = k.count("turned"), (k.count("copied"), k.count("copied_odd"))
    stored = k.count("kv_stored")
    with k.stage() as block:
        @block.tensor
        def _(pe):
            for j, (i, c0) in enumerate(jobs):
                a, n = TILES[i]
                if j >= 8:
                    pe.wait_ge(*copied[j % 2].at((j - 8) // 2 + 1))
                for c in range(4):
                    mm = pe.transpose(k.ps[0:n, j % 8, P * c:P * c + P], qkv[:, 8 + c0 + c, a:a + n], k.const("ident"))
                mm.then_inc(*turned.up())

        def copier(eng, odd):
            for j, (i, c0) in enumerate(jobs):
                if j % 2 == odd:
                    n = TILES[i][1]
                    dst = (k_tokens if c0 < 8 else v_tokens)[0:n, i, P * (c0 % 8):P * (c0 % 8) + 4 * P]
                    eng.wait_ge(*turned.at(j + 1))
                    copy(eng, dst, k.ps[0:n, j % 8, :]).then_inc(*copied[odd].up())

        @block.scalar
        def _(act):
            copier(act, 0)

        @block.vector
        def _(dve):
            copier(dve, 1)

        @block.sync
        def _(sp):
            sp.wait_ge(*copied[0].at(len(jobs) // 2))
            sp.wait_ge(*copied[1].at(len(jobs) // 2))
            for out_p, out_s, src, col in ((2, 4, k_tokens, 0), (6, 8, k_tokens, 512), (3, 5, v_tokens, 0), (7, 9, v_tokens, 512)):
                sp.dma_start(outs[out_p][0, 0].rearrange("(i p) h d -> p i (h d)", p=P),
                               src[:, 0:2, col:col + 512]).then_inc(*stored.up(16))
                sp.dma_start(outs[out_s].rearrange("b a t h d -> (b a t) (h d)"),
                               src[0:TS, 2, col:col + 512]).then_inc(*stored.up(16))


def stage_attention(k, qkv, v_tokens, keys, bias, bias8, pages):
    steps = [(m, t, g) for m in range(2) for t in range(2) for g in range(2)]
    UNITS, B_FIRST = 4, 2
    W_S = PAST + TS
    with ExitStack() as s:
        z = k.sb(s, "z", [P, 2, 4, 2 * P])
        prob = k.sb(s, "prob", [P, 2, 4, 2 * P])
        probT = k.sb(s, "probT", [P, 2, 4, P])
        soft = k.sb(s, "soft", [P, 4, 2 * P])
        stat = k.sb(s, "stat", [P, 2, 12])
        vals = k.sb(s, "vals", [P, 4, 2, 4 * P])
        keysT = k.sb(s, "keysT", [P, 2, 4, PAST])
        qbd = k.sb(s, "qbd", [P, 4, 4, 32])
        zs = k.sb(s, "zs", [P, W_S])
        probs = k.sb(s, "probs", [P, W_S])
        probTs = k.sb(s, "probTs", [P, 3, P])
        softs = k.sb(s, "softs", [P, W_S])
        stats = k.sb(s, "stats", [P, 4])
        own = k.sb(s, "own_head_mix", [P, 4 * P])
        scored, taken, z_ready, exped, shifted, weighed, turned, copied, mixed, out = (k.count(n) for n in (
            "scored", "scores_taken", "z_ready", "exped", "shifted", "weighed", "turned", "copied", "mixed", "mixed_out"))
        placed, keys_turned, scored_s, z_ready_s, exped_s, shifted_s, weighed_s, turned_s, copied_s, mixed_s, masked_s, collected_s, out_s = (k.count(n) for n in (
            "placed", "keys_turned", "scored_s", "z_ready_s", "exped_s", "shifted_s", "weighed_s", "turned_s", "copied_s", "mixed_s",
            "masked_s", "collected_s", "out_s"))
        keys_copied = (k.count("keys_copied_act"), k.count("keys_copied_dve"))
        keys_in = [k.count(f"keys_in{b}") for b in range(4)]
        vals_in, pages_in, bias_in, biased, zeroed = (k.count(n) for n in ("vals_in", "pages_in", "bias_in", "row_bias", "zeroed"))
        act_step, dve_step = k.count("act_step"), k.count("dve_step")
        with k.stage() as block:
            @block.gpsimd
            def _(pool):
                pool.wait_ge(*k.count("kv_stored").all())

            @block.sync
            def _(sp):
                for u in range(UNITS):
                    if u == 2:
                        sp.wait_ge(*pages_in.all())
                    if u >= 2:
                        at = [sp.value_load(pages[0:1, n:n + 1], min_val=0, max_val=k.ins["cache_sb_k"].shape[0] - 1)
                              for n in range(8 * (u % 2), 8 * (u % 2) + 8)]
                    for name, dst in ((("cache_win_k", keys), ("cache_win_v", vals)), (("cache_sb_k", keys), ("cache_sb_v", vals)))[u // 2]:
                        if dst is vals and u >= 1:
                            sp.wait_ge(*mixed_s.at(u))
                        landed = keys_in if dst is keys else [vals_in] * 4
                        if dst is keys and u >= 1:
                            sp.wait_ge(*keys_turned.at(8 * u))
                        if u < 2:
                            if dst is vals or u:
                                load_window(k, sp, name, dst, u, landed)
                            continue
                        for n in range(8):
                            page = k.ins[name][bass.ds(at[n], 1), 0].rearrange("a p h d -> p (a h d)")
                            sp.dma_start(dst[:, n // 2, n % 2, :], page).then_inc(*landed[n // 2].up(16))

            keys_by = (16, 32, 64, 96)
            vals_by = (64, 128, 256, 384)

            @block.tensor
            def _(pe):
                ident = k.const("ident")

                def scores(i):
                    m, t, g = steps[i]
                    if i >= 1:
                        pe.wait_ge(*taken.at(i))
                    for j in range(4):
                        c, r = 4 * m + 2 * g + j % 2, HD * (j // 2)
                        mm = pe.matmul(k.ps[:, j // 2, 256 * (j % 2):256 * (j % 2) + P * (t + 1)],
                                       qkv[r:r + HD, c, P * t:P * t + P], qkv[r:r + HD, 8 + c, 0:P * (t + 1)],
                                       start=True, stop=True)
                    mm.then_inc(*scored.up())

                def turn(i):
                    pe.wait_ge(*weighed.at(i + 1))
                    for kt in range(steps[i][1] + 1):
                        for j in range(4):
                            mm = pe.transpose(k.ps[:, 2 + kt, P * j:P * j + P], prob[:, i % 2, j, P * kt:P * kt + P], ident)
                    mm.then_inc(*turned.up())

                def mix(i):
                    m, t, g = steps[i]
                    pe.wait_ge(*copied.at(i + 1))
                    if i >= 1:
                        pe.wait_ge(*out.at(i))
                    for j in range(4):
                        h, r = 2 * (4 * m + 2 * g + j % 2) + j // 2, HD * (j // 2)
                        for kt in range(t + 1):
                            mm = pe.matmul(k.ps[r:r + HD, 4, P * (j % 2):P * (j % 2) + P],
                                           v_tokens[:, kt, HD * h:HD * h + HD], probT[:, kt, j, :], start=kt == 0, stop=kt == t)
                    mm.then_inc(*mixed.up())

                def turn_keys(u, b):
                    pe.wait_ge(keys_in[b].sem, keys_by[u])
                    for half in range(2):
                        if u or b:
                            pe.wait_ge(*keys_copied[half].at(4 * u + b))
                        for j in range(2):
                            for c in range(2):
                                mm = pe.transpose(k.ps[:, 5 + half, PAST * c + P * j:PAST * c + P * j + P],
                                                  keys[:, b, j, P * (2 * half + c):P * (2 * half + c) + P], ident)
                        mm.then_inc(*keys_turned.up())

                def scores_s(u, b):
                    if b == 0:
                        pe.wait_ge(*placed.at(2 * u + 2))
                        if u:
                            pe.wait_ge(*out_s.at(u))
                        for c in range(4):
                            pe.matmul(k.ps[:, 7, PAST:W_S], qbd[:, c, :, :].rearrange("p b n -> p (b n)"),
                                      qkv[:, 8 + 4 * (u // 2) + c, TP:T], start=c == 0, stop=c == 3)
                    for half in range(2):
                        pe.wait_ge(*keys_copied[half].at(4 * u + b + 1))
                    for c in range(4):
                        mm = pe.matmul(k.ps[32 * b:32 * b + 32, 7, 0:PAST], qbd[:, c, b, :], keysT[:, b % 2, c, :],
                                       start=c == 0, stop=c == 3)
                    mm.then_inc(*scored_s.up())

                def turn_s(u):
                    pe.wait_ge(*weighed_s.at(u + 1))
                    for j, (a, n) in enumerate(TILES):
                        mm = pe.transpose(k.ps[0:n, 7, P * j:P * j + P], probs[:, a:a + n], ident)
                    mm.then_inc(*turned_s.up())

                def mix_s(u):
                    pe.wait_ge(vals_in.sem, vals_by[u])
                    pe.wait_ge(*copied_s.at(u + 1))
                    at = 512 * (u // 2)
                    pe.matmul(k.ps[:, 7, :], probTs[0:TS, 2, :], v_tokens[0:TS, 2, at:at + 512], start=True, stop=False,
                              skip_group_check=True)
                    for b in range(4):
                        for j in range(2):
                            mm = pe.matmul(k.ps[32 * b:32 * b + 32, 7, :], probTs[:, j, 32 * b:32 * b + 32], vals[:, b, j, :],
                                           start=False, stop=j == 1, skip_group_check=True)
                    mm.then_inc(*mixed_s.up())

                def collect_s(u):
                    pe.wait_ge(*masked_s.at(u + 1))
                    for c in range(4):
                        mm = pe.matmul(k.ps[:, 7, 16 * c:16 * c + 16], own[:, P * c:P * c + P], k.table("row_token"), start=True, stop=True)
                    mm.then_inc(*collected_s.up())

                pe.wait_ge(*k.count("tables_in").all())
                pe.wait_ge(*bias_in.all())
                pe.matmul(k.ps[:, 7, 0:1], k.table("row_head")[0:8, :], bias8[:, :], start=True, stop=True).then_inc(*biased.up())
                scores(0)
                turn_keys(0, 0)
                pe.wait_ge(*placed.at(1))
                for u in range(UNITS):
                    scores_s(u, 0)
                    turn_keys(u, 1)
                    scores_s(u, 1)
                    turn_keys(u, 2)
                    if u < B_FIRST:
                        turn(2 * u)
                    scores_s(u, 2)
                    turn_keys(u, 3)
                    scores(2 * u + 1)
                    scores_s(u, 3)
                    if u >= B_FIRST:
                        turn(2 * u)
                    mix(2 * u)
                    turn(2 * u + 1)
                    if 2 * u + 2 < len(steps):
                        scores(2 * u + 2)
                    turn_s(u)
                    mix(2 * u + 1)
                    mix_s(u)
                    if u + 1 < UNITS:
                        turn_keys(u + 1, 0)
                    collect_s(u)

            @block.vector
            def _(dve):
                def then(ins, sig=dve_step):
                    ins.then_inc(*sig.up())
                    dve.wait_ge(*sig.all())

                def parts(i):
                    m, t, g = steps[i]
                    W, x0 = P * (t + 1), P * (1 - t)
                    return m, t, g, W, x0, z[:, i % 2, :, 0:W], prob[:, i % 2, :, 0:W]

                def logits(i):
                    m, t, g, W, x0, zz, _ = parts(i)
                    raw = k.ps[:, 0:2, :].rearrange("p a (b n) -> p (a b) n", b=2)[:, :, 0:W]
                    dve.wait_ge(*scored.at(i + 1))
                    if i >= 2:
                        dve.wait_ge(*weighed.at(i - 1))
                    if m == 0:
                        tab = k.table("alibi").rearrange("p (h n) -> p h n", h=8)[:, 4 * g:4 * g + 4, x0:2 * P]
                        then(dve.scalar_tensor_tensor(zz, raw, SCALE, tab, ALU.mult, ALU.add), taken)
                        dve.tensor_reduce(stat[:, i % 2, 0:4], zz, AX, ALU.max, negate=True).then_inc(*z_ready.up())
                    else:
                        b = bias[:, 4 * g:4 * g + 4].rearrange("p (q a) -> p a q", a=2).unsqueeze(3).broadcast_to([P, 2, 2, W])
                        z4 = z[:, i % 2, :, :].rearrange("p (a q) n -> p a q n", a=2)[:, :, :, 0:W]
                        then(dve.tensor_scalar(zz, raw, SCALE, None, ALU.mult), taken)
                        dve.tensor_tensor(z4, z4, b, ALU.add).then_inc(*z_ready.up())

                def weights(i):
                    m, t, g, W, x0, zz, pp = parts(i)
                    dve.wait_ge(*exped.at(i + 1))
                    if m == 0:
                        then(dve.reciprocal(stat[:, i % 2, 8:12], stat[:, i % 2, 4:8]))
                        dve.tensor_tensor(pp, pp, stat[:, i % 2, 8:12].unsqueeze(2).broadcast_to([P, 4, W]), ALU.mult).then_inc(*weighed.up())
                        return
                    ss = soft[:, :, 0:W]
                    on = k.table("stick_on")[:, x0:2 * P].unsqueeze(1).broadcast_to([P, 4, W])
                    offm = k.table("stick_off")[:, x0:2 * P].unsqueeze(1).broadcast_to([P, 4, W])
                    then(dve.scalar_tensor_tensor(ss, zz, 0.0, ss, ALU.max, ALU.add))
                    then(dve.tensor_tensor(ss, ss, on, ALU.mult))
                    dve.wait_ge(*turned.at(i - 1))
                    for j in range(4):
                        ins = dve.tensor_tensor_scan(prob[:, i % 2, j, 0:W][:, ::-1], k.ones_wide[:, 0:W], soft[:, j, 0:W][:, ::-1],
                                                     0.0, ALU.mult, ALU.add)
                    then(ins)
                    then(dve.tensor_tensor(zz, zz, pp, ALU.subtract))
                    dve.tensor_tensor(zz, zz, offm, ALU.add).then_inc(*shifted.up())

                def take_turned(i):
                    t = steps[i][1]
                    dve.wait_ge(*turned.at(i + 1))
                    if i >= 1:
                        dve.wait_ge(*mixed.at(i))
                    if t:
                        then(dve.tensor_copy(probT[:, 1, :, :], k.ps[:, 3, :].rearrange("p (h n) -> p h n", h=4)))
                    dve.tensor_copy(probT[:, 0, :, :], k.ps[:, 2, :].rearrange("p (h n) -> p h n", h=4)).then_inc(*copied.up())

                def take_out(i):
                    m, t, g = steps[i]
                    at = 4 * m + 2 * g
                    dve.wait_ge(*mixed.at(i + 1))
                    dve.tensor_copy(k.act[:, at:at + 2, P * t:P * t + P], k.ps[:, 4, 0:2 * P].rearrange("p (c n) -> p c n", c=2))\
                       .then_inc(*out.up())

                def place(u):
                    for r in range(2):
                        for c in range(4):
                            dst = qbd[HD * r:HD * r + HD, c, :, 4 * (2 * c + r):4 * (2 * c + r) + 4]
                            src = qkv[HD * r:HD * r + HD, 4 * (u // 2) + c, TP + 16 * (u % 2):TP + 16 * (u % 2) + 16]
                            ins = dve.tensor_copy(dst, src.rearrange("p (b t) -> p b t", t=NT))
                        ins.then_inc(*placed.up())

                def take_keys(u, b):
                    dve.wait_ge(*keys_turned.at(8 * u + 2 * b + 2))
                    if 4 * u + b >= 2:
                        dve.wait_ge(*scored_s.at(4 * u + b - 1))
                    dve.tensor_copy(keysT[:, b % 2, 2:4, :], k.ps[:, 6, :].rearrange("p (c n) -> p c n", c=2)).then_inc(*keys_copied[1].up())

                part = lambda name, u: k.table(name)[:, W_S * (u % 2):W_S * (u % 2) + W_S]

                def logits_s(u):
                    dve.wait_ge(*scored_s.at(4 * u + 4))
                    raw = k.ps[:, 7, 0:W_S]
                    if u < 2:
                        then(dve.scalar_tensor_tensor(zs[:, :], raw, SCALE, part("alibi_s", u), ALU.mult, ALU.add))
                        dve.tensor_reduce(stats[:, 0:1], zs[:, :], AX, ALU.max, negate=True).then_inc(*z_ready_s.up())
                    else:
                        dve.tensor_scalar(zs[:, :], raw, SCALE, stats[:, 3:4], ALU.mult, ALU.add).then_inc(*z_ready_s.up())

                def weights_s(u):
                    dve.wait_ge(*exped_s.at(u + 1))
                    if u < 2:
                        then(dve.reciprocal(stats[:, 2:3], stats[:, 1:2]))
                        dve.tensor_scalar(probs[:, :], probs[:, :], stats[:, 2:3], None, ALU.mult).then_inc(*weighed_s.up())
                        return
                    then(dve.scalar_tensor_tensor(softs[:, :], zs[:, :], 0.0, softs[:, :], ALU.max, ALU.add))
                    then(dve.tensor_tensor(softs[:, :], softs[:, :], part("stick_on_s", u), ALU.mult))
                    then(dve.tensor_tensor_scan(probs[:, ::-1], k.ones_wide[:, :], softs[:, ::-1], 0.0, ALU.mult, ALU.add))
                    then(dve.tensor_tensor(zs[:, :], zs[:, :], probs[:, :], ALU.subtract))
                    dve.tensor_tensor(zs[:, :], zs[:, :], part("stick_off_s", u), ALU.add).then_inc(*shifted_s.up())

                def take_turned_s(u):
                    dve.wait_ge(*turned_s.at(u + 1))
                    dve.tensor_copy(probTs[:, 0:2, :], k.ps[:, 7, 0:2 * P].rearrange("p (j n) -> p j n", j=2)).then_inc(*dve_step.up())
                    then(dve.tensor_copy(probTs[0:TS, 2, :], k.ps[0:TS, 7, 2 * P:3 * P]), copied_s)

                def mask_s(u):
                    dve.wait_ge(*mixed_s.at(u + 1))
                    dve.tensor_tensor(own[:, :].rearrange("p (h d) -> p h d", h=8), k.ps[:, 7, :].rearrange("p (h d) -> p h d", h=8),
                                      k.table("own_head").unsqueeze(2).broadcast_to([P, 8, HD]), ALU.mult).then_inc(*masked_s.up())

                def take_out_s(u):
                    dve.wait_ge(*collected_s.at(u + 1))
                    at, col = 4 * (u // 2), TP + 16 * (u % 2)
                    dve.tensor_copy(k.act[:, at:at + 4, col:col + 16], k.ps[:, 7, 0:64].rearrange("p (c n) -> p c n", c=4)).then_inc(*out_s.up())

                then(dve.memset(qbd[:, :, :, :], 0.0), zeroed)
                dve.wait_ge(*k.count("tables_in").all())
                dve.wait_ge(*biased.at(1))
                then(dve.tensor_copy(stats[:, 3:4], k.ps[:, 7, 0:1]))
                place(0)
                logits(0)
                take_keys(0, 0)
                for u in range(UNITS):
                    take_keys(u, 1)
                    weights(2 * u)
                    take_keys(u, 2)
                    if u < B_FIRST:
                        take_turned(2 * u)
                    take_keys(u, 3)
                    logits(2 * u + 1)
                    if u < B_FIRST:
                        take_out(2 * u)
                    logits_s(u)
                    if u >= B_FIRST:
                        take_turned(2 * u)
                        take_out(2 * u)
                    if u + 1 < UNITS:
                        place(u + 1)
                    weights(2 * u + 1)
                    weights_s(u)
                    if 2 * u + 2 < len(steps):
                        logits(2 * u + 2)
                    take_turned(2 * u + 1)
                    take_turned_s(u)
                    take_out(2 * u + 1)
                    mask_s(u)
                    if u + 1 < UNITS:
                        take_keys(u + 1, 0)
                    take_out_s(u)

            @block.scalar
            def _(act):
                def then(ins, sig=act_step):
                    ins.then_inc(*sig.up())
                    act.wait_ge(*sig.all())

                def take_keys(u, b):
                    act.wait_ge(*keys_turned.at(8 * u + 2 * b + 1))
                    if 4 * u + b >= 2:
                        act.wait_ge(*scored_s.at(4 * u + b - 1))
                    act.copy(keysT[:, b % 2, 0:2, :], k.ps[:, 5, :].rearrange("p (c n) -> p c n", c=2)).then_inc(*keys_copied[0].up())

                def exps(i):
                    m, t, g = steps[i]
                    W = P * (t + 1)
                    act.wait_ge(*z_ready.at(i + 1))
                    if m == 0:
                        if i >= 2:
                            act.wait_ge(*turned.at(i - 1))
                        for j in range(4):
                            ins = act.activation(prob[:, i % 2, j, 0:W], z[:, i % 2, j, 0:W], ACT.Exp, bias=stat[:, i % 2, j:j + 1],
                                                 accum_out=stat[:, i % 2, 4 + j:5 + j])
                        ins.then_inc(*exped.up())
                    else:
                        if i >= 5:
                            act.wait_ge(*shifted.at(i - 4))
                        then(act.activation(soft[:, :, 0:W], z[:, i % 2, :, 0:W], ACT.Abs))
                        then(act.activation(soft[:, :, 0:W], soft[:, :, 0:W], ACT.Exp, scale=-1.0))
                        act.activation(soft[:, :, 0:W], soft[:, :, 0:W], ACT.Ln, bias=1.0).then_inc(*exped.up())

                def stick(i):
                    if steps[i][0] == 1:
                        W = P * (steps[i][1] + 1)
                        act.wait_ge(*shifted.at(i - 3))
                        act.activation(prob[:, i % 2, :, 0:W], z[:, i % 2, :, 0:W], ACT.Exp).then_inc(*weighed.up())

                def exps_s(u):
                    act.wait_ge(*z_ready_s.at(u + 1))
                    if u < 2:
                        act.activation(probs[:, :], zs[:, :], ACT.Exp, bias=stats[:, 0:1], accum_out=stats[:, 1:2]).then_inc(*exped_s.up())
                    else:
                        then(act.activation(softs[:, :], zs[:, :], ACT.Abs))
                        then(act.activation(softs[:, :], softs[:, :], ACT.Exp, scale=-1.0))
                        act.activation(softs[:, :], softs[:, :], ACT.Ln, bias=1.0).then_inc(*exped_s.up())

                def stick_s(u):
                    if u >= 2:
                        act.wait_ge(*shifted_s.at(u - 1))
                        act.activation(probs[:, :], zs[:, :], ACT.Exp).then_inc(*weighed_s.up())

                take_keys(0, 0)
                exps(0)
                for u in range(UNITS):
                    take_keys(u, 1)
                    take_keys(u, 2)
                    stick(2 * u)
                    take_keys(u, 3)
                    exps(2 * u + 1)
                    exps_s(u)
                    stick(2 * u + 1)
                    stick_s(u)
                    if 2 * u + 2 < len(steps):
                        exps(2 * u + 2)
                    if u + 1 < UNITS:
                        take_keys(u + 1, 0)


def stage_out_even(k, x):
    def copy_out(eng, m):
        return eng.tensor_tensor(k.residual[:, m, :], k.residual[:, m, :], k.ps[:, m, 0:T], ALU.add)
    gemm(k, "_out_even", 6, [WCOLS] * 2, x, copy_out, by_vector=True)



def stage_ffn_up(k, x, hidden_hi, hidden_lo):
    first = 8
    pair_done, gated, made, rounded, rest = (k.count(n) for n in ("pair_done", "gated", "hidden_made", "rounded", "rest"))
    halves = [(first + m // 2, m % 2 == 0, k.slot(first + m // 2, "pair", 256)[:, :, :, P * (m % 2):P * (m % 2) + P], (2 * DC, P))
              for m in range(FC)]
    halves = [(n, f, raw.rearrange("p k w n -> p (k w) n"), shape) for n, f, raw, shape in halves]
    with ExitStack() as s:
        gate = [k.sb(s, f"gate{n}", [P, T]) for n in range(2)]
        full = [k.sb(s, f"hidden_full{n}", [P, T]) for n in range(2)]
        sp_ = Split(k, s, "_up", halves, lambda h: pair_done.at(h + 1))
        norm = Norm(k, s, "norm_ffn_even", x)
        with k.stage() as block:
            sp_.start()

            @block.sync
            def _(sp):
                k.stream(sp, first + FC // 2 + EARLY_SLOTS)

            @block.tensor
            def _(pe):
                norm.sums(pe)
                for m in range(FC):
                    pe.wait_ge(*sp_.hi_done.at(m + 1))
                    if m >= 4:
                        pe.wait_ge(*made.at(m - 3))
                    hi, lo = (sp_.view(b, m).rearrange("p (c w) n -> p c w n", w=2) for b in (sp_.hi, sp_.lo))
                    outs = [k.ps[:, 2 * (m % 4) + w, 0:T] for w in range(2)]
                    for w in range(2):
                        for c in range(DC):
                            if m == 0 and w == 0:
                                norm.await_chunk(pe, c)
                            pe.matmul(outs[w], hi[:, c, w, :], x[0][:, c, :], start=c == 0, stop=False)
                            pe.matmul(outs[w], hi[:, c, w, :], x[1][:, c, :], start=False, stop=False)
                    pe.wait_ge(*sp_.lo_done.at(m + 1))
                    for w in range(2):
                        for c in range(DC):
                            mm = pe.matmul(outs[w], lo[:, c, w, :], x[0][:, c, :], start=False, stop=c == DC - 1)
                    mm.then_inc(*pair_done.up())

            @block.scalar
            def _(act):
                norm.squares(act)
                sp_.round_hi(act, 0)
                norm.roots(act)
                sp_.round_hi(act, 1)
                for m in range(FC):
                    act.wait_ge(*pair_done.at(m + 1))
                    if m >= 2:
                        act.wait_ge(*made.at(m - 1))
                    act.activation(gate[m % 2][:, :], k.ps[:, 2 * (m % 4), 0:T], ACT.Silu).then_inc(*gated.up())
                    sp_.round_hi(act, m + 2)
                    act.wait_ge(*made.at(m + 1))
                    act.copy(hidden_hi[:, m, :], full[m % 2][:, :]).then_inc(*rounded.up())

            @block.vector
            def _(dve):
                def take_rest(m):
                    dve.wait_ge(*rounded.at(m + 1))
                    dve.tensor_tensor(hidden_lo[:, m, :], full[m % 2][:, :], hidden_hi[:, m, :].bitcast(F32), ALU.subtract)\
                       .then_inc(*rest.up())
                sp_.take_lo(dve, 0)
                norm.apply(dve)
                for m in range(FC):
                    sp_.take_lo(dve, m + 1)
                    if m >= 1:
                        take_rest(m - 1)
                    if m >= 2:
                        dve.wait_ge(*rest.at(m - 1))
                    dve.wait_ge(*gated.at(m + 1))
                    dve.tensor_tensor(full[m % 2][:, :], gate[m % 2][:, :], k.ps[:, 2 * (m % 4) + 1, 0:T],
                                      ALU.mult).then_inc(*made.up())
                take_rest(FC - 1)



Q, F_, V, G, Z, X, DT = 0, 4, 8, 12, 16, 24, 36


IN_ODD_ORDER = [m for n in IN_ODD_BLOCKS for m in range(4 * n, min(4 * n + 4, DT + 1))]
IN_ODD_GROUPS = [(p,) if IN_ODD_ORDER[p] == DT else (p, p + 1)
                 for p in [*range(0, CC, 2), CC, *range(CC + 1, DT, 2)]]


def stage_in_odd(k, x, proj, conv_in, conv_in_s, dt, xc, hg, dta, par):
    first = 25
    done, out = k.count("product_done"), (k.count("even_out"), k.count("odd_out"))
    ring_blocks = [b for b, n in enumerate(IN_ODD_BLOCKS) if n != 9]
    dt_block = IN_ODD_BLOCKS.index(9)
    halves = [(first + b, j == 0, k.slot(first + b, "cols", WCOLS)[:, :, 256 * j:256 * j + 256], (DC, 256))
              for b in ring_blocks for j in range(2)]
    half_ends = [g[1] + 1 for g in IN_ODD_GROUPS if len(g) == 2]
    silus = set(range(Q, Q + 4)) | set(range(G, G + 4)) | set(range(Z, Z + 8))
    on_act = [p for p, m in enumerate(IN_ODD_ORDER) if m in silus or m % 4 == 1 and m < 36]
    on_dve = [p for p in range(DT + 1) if p not in on_act]
    past_in, past_turned, past, past_zeroed, placed = (k.count(n) for n in ("past_in", "past_turned", "past_placed", "zeroed", "placed"))
    first_tap, tapped, silued = (k.count(n) for n in ("tap_first", "taps", "gated"))
    lb_max, lb_exp, sigmoids, forget, logged = (k.count(n) for n in ("lb_max", "lb_exp", "sigmoids", "forget", "log_forget"))
    par_in, raw_ready, log_ready, a_ready, dt_done, sums, ended, diffed = (k.count("d_" + n) for n in (
        "par_in", "raw", "log", "a", "dt", "sums", "ended", "diff"))
    act_step, dve_step = k.count("act_step"), k.count("dve_step")
    acum, wend = dta["acum"], dta["wend"]
    f, keep = proj[:, F_:F_ + 4, :], hg["k"]
    w = lambda j, c: k.vec[:, 60 + CC * j + c:61 + CC * j + c]
    bias = lambda c: k.vec[:, 108 + c:109 + c]
    outp = lambda c: xc[:, c, 0:TP]
    outs = lambda c: xc[:, c, TP:T].rearrange("p (b t) -> p b t", t=NT)
    with ExitStack() as s:
        old = k.sb(s, "old_conv", [NB * 3, CC * P])
        lb = k.sb(s, "lb", [P, 20])
        u = k.sb(s, "dt_u", [HM, T])
        sp_ = Split(k, s, "_in_odd", halves, lambda h: done.at(half_ends[h]))
        norm = Norm(k, s, "norm_mix_odd", x, xc[:, 0:DC, :])
        with k.stage() as block:
            sp_.start()
            k.freed[first + dt_block] = done.at(IN_ODD_ORDER.index(DT) + 1)

            def place(p):
                return out[0].at(on_act.index(p) + 1) if p in on_act else out[1].at(on_dve.index(p) + 1)

            def await_chunks(eng, chunks):
                for m in chunks:
                    eng.wait_ge(*place(IN_ODD_ORDER.index(m)))

            @block.sync
            def _(sp):
                for n, name in enumerate(("dt_bias", "a_log", "d_skip")):
                    sp.dma_start(par[:, n:n + 1], k.ins[name].rearrange("a h -> h a")).then_inc(*par_in.up(16))
                k.stream(sp, first + 10 + EARLY_SLOTS)

            @block.gpsimd
            def _(pool):
                pool.dma_start(old[:, :], k.ins["state_conv"].rearrange("b a r c -> (b a r) c")).then_inc(*past_in.up(16))
                pool.memset(conv_in[:, :, 0:3], 0.0).then_inc(*past_zeroed.up())

            @block.tensor
            def _(pe):
                norm.sums(pe)
                pe.wait_ge(*past_in.at(16))
                for c in range(CC):
                    mm = pe.transpose(k.ps[:, 7, 24 * c:24 * c + 24], old[:, P * c:P * c + P], k.const("ident")[0:24, 0:24])
                mm.then_inc(*past_turned.up())
                half = 0
                for group in IN_ODD_GROUPS:
                    for j, p in enumerate(group):
                        if p >= 7:
                            pe.wait_ge(*place(p - 7))
                        if len(group) == 2:
                            if j == 0:
                                pe.wait_ge(*sp_.hi_done.at(half + 1))
                            mm = sp_.products(pe, k.ps[:, p % 7, 0:T], half, slice(P * j, P * j + P), range(DC), x, True, True,
                                              norm if p == 0 else None)
                        else:
                            pe.wait_ge(*k.arrived(first + dt_block))
                            slot = k.slot(first + dt_block, "cols", HM)
                            for c in range(DC):
                                mm = pe.matmul(k.ps[0:HM, p % 7, 0:T], slot[:, c, :], k.act[:, c, :], start=c == 0, stop=c == DC - 1)
                        mm.then_inc(*done.up())
                    half += len(group) == 2

            def leave(eng, p):
                bank, m = k.ps[:, p % 7, :], IN_ODD_ORDER[p]
                if m in silus:
                    return eng.activation(proj[:, m, :], bank[:, 0:T], ACT.Silu)
                if m < X:
                    return copy(eng, proj[:, m, :], bank[:, 0:T])
                if m < DT:
                    copy(eng, conv_in_s[:, m - X, :, 3:3 + NT], bank[:, TP:T].rearrange("p (b t) -> p b t", t=NT)).then_inc(*placed.up())
                    return copy(eng, conv_in[:, m - X, 3:3 + TP], bank[:, 0:TP])
                return copy(eng, dt[:, :], bank[0:HM, 0:T])

            @block.scalar
            def _(act):
                def then(ins):
                    ins.then_inc(*act_step.up())
                    act.wait_ge(*act_step.all())

                def tap(c):
                    act.activation(outs(c), conv_in_s[:, c, :, 0:NT], ACT.Identity, scale=w(0, c), bias=bias(c)).then_inc(*first_tap.up())
                    act.activation(outp(c), conv_in[:, c, 0:TP], ACT.Identity, scale=w(0, c), bias=bias(c)).then_inc(*first_tap.up())

                def silu(c):
                    act.wait_ge(*tapped.at(c + 1))
                    act.activation(xc[:, c, :], xc[:, c, :], ACT.Silu).then_inc(*silued.up())

                def extra(g):
                    if g == 3:
                        act.wait_ge(*lb_max.at(1))
                        act.activation(lb[:, 4:12], lb[:, 4:12], ACT.Exp).then_inc(*lb_exp.up())
                        act.wait_ge(*par_in.at(48))
                        act.activation(par[:, 3:4], par[:, 1:2], ACT.Exp).then_inc(*a_ready.up())
                    if g == 6:
                        await_chunks(act, range(X, DT))
                        act.wait_ge(*placed.at(CC))
                        act.wait_ge(*past.at(1))
                        act.wait_ge(*past_zeroed.at(1))
                    if 6 <= g < 12:
                        tap(2 * (g - 6))
                        tap(2 * (g - 6) + 1)
                    if g == 8:
                        act.wait_ge(*raw_ready.at(1))
                        then(act.activation(u[:, :], dt[:, :], ACT.Abs))
                        then(act.activation(u[:, :], u[:, :], ACT.Exp, scale=-1.0))
                        act.activation(u[:, :], u[:, :], ACT.Ln, bias=1.0).then_inc(*log_ready.up())
                    if g == 9:
                        await_chunks(act, range(F_, F_ + 4))
                        act.activation(keep, f, ACT.Sigmoid, scale=-1.0).then_inc(*sigmoids.up())
                        act.wait_ge(*sigmoids.at(1))
                        act.activation(f, f, ACT.Sigmoid).then_inc(*sigmoids.up())
                    if g == 12:
                        act.wait_ge(*diffed.at(2))
                        act.activation(wend[:, :], wend[:, :], ACT.Exp).then_inc(*ended.up())
                    if g == 13:
                        act.wait_ge(*forget.at(1))
                        act.activation(f, f, ACT.Ln).then_inc(*logged.up())
                    if 12 <= g < 18:
                        silu(2 * (g - 12))
                        silu(2 * (g - 12) + 1)

                norm.squares(act)
                sp_.round_hi(act, 0)
                norm.roots(act)
                sp_.round_hi(act, 1)
                half = 0
                for g, group in enumerate(IN_ODD_GROUPS):
                    for p in group:
                        if p in on_act:
                            act.wait_ge(*done.at(p + 1))
                            leave(act, p).then_inc(*out[0].up())
                    if len(group) == 2:
                        sp_.round_hi(act, half + 2)
                        half += 1
                    extra(g)

            @block.vector
            def _(dve):
                def then(ins, sig=dve_step):
                    ins.then_inc(*sig.up())
                    dve.wait_ge(*sig.all())

                def conv(c0):
                    for j in range(1, 4):
                        for c in (c0, c0 + 1):
                            if j == 1:
                                dve.wait_ge(*first_tap.at(2 * c + 2))
                            else:
                                dve.wait_ge(dve_step.sem, dve_step.total - (1 if j == 3 and c > c0 else 2))
                            dve.scalar_tensor_tensor(outs(c), conv_in_s[:, c, :, j:j + NT], w(j, c), outs(c), ALU.mult, ALU.add)\
                               .then_inc(*dve_step.up())
                            dve.scalar_tensor_tensor(outp(c), conv_in[:, c, j:j + TP], w(j, c), outp(c), ALU.mult, ALU.add)\
                               .then_inc(*(tapped if j == 3 else dve_step).up())

                low, rest = lb[:, 0:4], lb[:, 16:20]
                wide = lambda v: v.unsqueeze(2).broadcast_to([P, 4, T])

                def extra(g):
                    if g == 2:
                        l0, l1 = k.vec[:, 40:44], k.vec[:, 44:48]
                        then(dve.tensor_tensor(lb[:, 0:4], l0, l1, ALU.max))
                        then(dve.tensor_tensor(lb[:, 4:8], l0, lb[:, 0:4], ALU.subtract))
                        dve.tensor_tensor(lb[:, 8:12], l1, lb[:, 0:4], ALU.subtract).then_inc(*lb_max.up())
                    if g == 5:
                        dve.wait_ge(*lb_exp.at(1))
                        then(dve.tensor_tensor(lb[:, 12:16], lb[:, 4:8], lb[:, 8:12], ALU.add))
                        then(dve.reciprocal(lb[:, 12:16], lb[:, 12:16]))
                        then(dve.tensor_tensor(low, lb[:, 8:12], lb[:, 12:16], ALU.mult))
                        then(dve.tensor_tensor(rest, lb[:, 4:8], lb[:, 12:16], ALU.mult))
                    if g == 7:
                        await_chunks(dve, (DT,))
                        dve.wait_ge(*par_in.at(48))
                        dve.tensor_scalar(dt[:, :], dt[:, :], par[:, 0:1], None, ALU.add).then_inc(*raw_ready.up())
                    if 7 <= g < 13:
                        conv(2 * (g - 7))
                    if g == 10:
                        dve.wait_ge(*log_ready.at(1))
                        then(dve.scalar_tensor_tensor(dt[:, :], dt[:, :], 0.0, u[:, :], ALU.max, ALU.add), dt_done)
                        dve.wait_ge(*a_ready.at(1))
                        then(dve.tensor_scalar(u[:, :], dt[:, :], par[:, 3:4], -1.0, ALU.mult, ALU.mult))
                        then(dve.tensor_tensor_scan(acum[:, :], k.const("running")[0:HM, :], u[:, :], 0.0, ALU.mult, ALU.add), sums)
                        dve.tensor_tensor(wend[:, 0:TP], acum[:, TP - 1:TP].broadcast_to([HM, TP]), acum[:, 0:TP], ALU.subtract)\
                           .then_inc(*diffed.up())
                        ac = acum[:, TP:T].rearrange("p (b t) -> p b t", t=NT)
                        dve.tensor_tensor(wend[:, TP:T].rearrange("p (b t) -> p b t", t=NT), ac[:, :, NT - 1:NT].broadcast_to([HM, NB, NT]),
                                          ac, ALU.subtract).then_inc(*diffed.up())
                    if g == 11:
                        dve.wait_ge(*sigmoids.at(2))
                        then(dve.tensor_tensor(f, f, wide(rest), ALU.mult))
                        dve.tensor_tensor(f, f, wide(low), ALU.add).then_inc(*forget.up())
                        dve.tensor_tensor(keep, keep, wide(rest), ALU.mult).then_inc(*dve_step.up())
                    if g == 13:
                        dve.wait_ge(*ended.at(1))
                        dve.tensor_tensor(wend[:, :], wend[:, :], dt[:, :], ALU.mult).then_inc(*ended.up())
                    if g == 15:
                        dve.wait_ge(*logged.at(1))
                        for c in range(4):
                            dve.tensor_tensor_scan(hg["g"][:, c, :], k.const("running"), proj[:, F_ + c, :], 0.0, ALU.mult, ALU.add)\
                               .then_inc(*dve_step.up())

                sp_.take_lo(dve, 0)
                norm.apply(dve)
                dve.wait_ge(*past_turned.at(1))
                dve.tensor_copy(conv_in_s[:, :, :, 0:3],
                                k.ps[:, 7, 0:24 * CC].rearrange("p (c b r) -> p c b r", c=CC, r=3)).then_inc(*past.up())
                half = 0
                for g, group in enumerate(IN_ODD_GROUPS):
                    if len(group) == 2:
                        sp_.take_lo(dve, half + 1)
                        half += 1
                    for p in group:
                        if p in on_dve:
                            dve.wait_ge(*done.at(p + 1))
                            leave(dve, p).then_inc(*out[1].up())
                    extra(g)


def stage_hgrn(k, proj, hg, mixed_out):
    q, v, gate = proj[:, Q:Q + 4, :], proj[:, V:V + 4, :], proj[:, G:G + 4, :]
    kk, g = hg["k"], hg["g"]
    levels = [1 << l for l in range(8)]
    act_step, dve_step = k.count("act_step"), k.count("dve_step")
    with ExitStack() as s:
        X2 = [k.sb(s, f"level_x{n}", [P, 4, T]) for n in range(2)]
        att = k.sb(s, "att", [P, 2, 4, P])
        attx = k.sb(s, "attx", [P, 4, P])
        atts = k.sb(s, "atts", [TS, 4, TS])
        vt = k.sb(s, "hgrn_v_tokens", [P, 3, 4 * P])
        kd = k.sb(s, "k_decayed", [P, 4, T])
        kdt = k.sb(s, "kd_tokens", [P, 3, 4 * P])
        qe = k.sb(s, "q_decayed", [P, 4, TS])
        vbd = k.sb(s, "v_by_sample", [TS, NB, 4 * P])
        eg = k.sb(s, "state_decay", [P, 4, TS])
        state = k.sb(s, "hgrn_state", [P, NB, 4, P])
        statep = k.sb(s, "hgrn_state_p", [P, 4, P])
        names = ("diff", "level_exp", "level_x", "level_dot", "level_in", "diag_dot", "state_in", "tokens_turned", "tokens_copied",
                 "kd_diff", "exp", "kd_done", "kd_turned", "kd_copied", "by_sample", "decays", "qe_done",
                 "state_dot", "state_new", "y_dot", "y_taken", "sq", "sum", "mean", "root", "out", "stored", "statep")
        n_ = {x: k.count(x) for x in names}

        def halves(x, H, n):
            b = x[:, :, 0:n]
            if n == T:
                b = b.rearrange("p c (b u) -> p (c b) u", u=2 * H)
                return b[:, :, 0:H], b[:, :, H:2 * H], b[:, :, H - 1:H].broadcast_to([P, 4 * n // (2 * H), H])
            b = b.rearrange("p c (b u) -> p c b u", u=2 * H)
            return b[:, :, :, 0:H], b[:, :, :, H:2 * H], b[:, :, :, H - 1:H].broadcast_to([P, 4, n // (2 * H), H])

        span = lambda H: T if H <= 2 else TP
        with k.stage() as block:
            @block.sync
            def _(sp):
                sp.dma_start(state[:, :, :, :].rearrange("p b c v -> p (b c) v"),
                               k.ins["state_hgrn"].rearrange("b a c k v -> k (b a c) v")).then_inc(*n_["state_in"].up(16))
                sp.wait_ge(*n_["statep"].at(1))
                sp.dma_start(k.outs[10][0, 0].rearrange("c k v -> k c v"), statep[:, :, :]).then_inc(*n_["stored"].up(16))
                sp.wait_ge(*n_["state_new"].at(8))
                sp.dma_start(k.outs[11].rearrange("b a c k v -> k (b a c) v"),
                               state[:, :, :, :].rearrange("p b c v -> p (b c) v")).then_inc(*n_["stored"].up(16))
                sp.wait_ge(*n_["stored"].at(32))

            @block.vector
            def _(dve):
                def then(ins, sig=dve_step):
                    ins.then_inc(*sig.up())
                    dve.wait_ge(*sig.all())

                def diff(l):
                    H, x = levels[l], X2[l % 2]
                    n = span(H)
                    if l >= 2:
                        dve.wait_ge(*n_["level_dot"].at(l - 1))
                    g1, g2, ref = halves(g, H, n)
                    x1, x2, _ = halves(x, H, n)
                    then(dve.tensor_tensor(x1, ref, g1, ALU.subtract))
                    dve.tensor_tensor(x2, g2, ref, ALU.subtract).then_inc(*n_["diff"].up())

                def scale(l):
                    H, x = levels[l], X2[l % 2]
                    n = span(H)
                    dve.wait_ge(*n_["level_exp"].at(l + 1))
                    x1, x2, _ = halves(x, H, n)
                    k1 = halves(kk, H, n)[0]
                    q2 = halves(q, H, n)[1]
                    then(dve.tensor_tensor(x1, x1, k1, ALU.mult))
                    dve.tensor_tensor(x2, x2, q2, ALU.mult).then_inc(*n_["level_x"].up())

                def gather(l):
                    H = levels[l]
                    dve.wait_ge(*n_["level_dot"].at(l + 1))
                    bank = 3 * (l % 2)
                    if H == P:
                        then(dve.tensor_copy(attx[:, :, :], k.ps[:, bank, :].rearrange("p (c n) -> p c n", c=4)), n_["level_in"])
                        return
                    m0, _ = k.core_at["level"]
                    mask = k.core[:, m0 + P * l:m0 + P * l + P].bitcast(I32)
                    if H <= 2:
                        then(dve.copy_predicated(atts[:, :, :], mask[0:TS, 0:TS].unsqueeze(1).broadcast_to([TS, 4, TS]),
                                                 k.ps[0:TS, bank + 2, 0:4 * TS].rearrange("p (c n) -> p c n", c=4)))
                    then(dve.copy_predicated(att[:, :, :, :].rearrange("p i c n -> p (i c) n"), mask.unsqueeze(1).broadcast_to([P, 8, P]),
                                             k.ps[:, bank:bank + 2, :].rearrange("p i (c n) -> p (i c) n", c=4)), n_["level_in"])

                diff(0)
                diff(1)
                dve.wait_ge(*n_["diag_dot"].at(1))
                eye = k.const("ident")
                then(dve.tensor_tensor(att[:, :, :, :].rearrange("p i c n -> p (i c) n"),
                                       k.ps[:, 6:8, :].rearrange("p i (c n) -> p (i c) n", c=4),
                                       eye.unsqueeze(1).broadcast_to([P, 8, P]), ALU.mult))
                then(dve.tensor_tensor(atts[:, :, :], k.ps[0:TS, 5, 0:4 * TS].rearrange("p (c n) -> p c n", c=4),
                                       eye[0:TS, 0:TS].unsqueeze(1).broadcast_to([TS, 4, TS]), ALU.mult), n_["level_in"])
                scale(0)
                for l in range(8):
                    if l + 1 < 8:
                        scale(l + 1)
                    if l + 2 < 8:
                        diff(l + 2)
                    gather(l)
                for c in range(4):
                    dve.wait_ge(*n_["y_dot"].at(c + 1))
                    dve.tensor_copy(mixed_out[:, c, :], k.ps[:, c, 0:T]).then_inc(*n_["y_taken"].up())
                dve.wait_ge(*n_["state_dot"].at(1))
                dve.tensor_copy(statep[:, :, :], k.ps[:, 4, :].rearrange("p (c v) -> p c v", c=4)).then_inc(*n_["statep"].up())
                for c in range(4):
                    for hf in range(2):
                        i = 2 * c + hf
                        dve.wait_ge(*n_["state_dot"].at(i + 2))
                        for b in range(4 * hf, 4 * hf + 4):
                            last = NT * b + NT - 1
                            ins = dve.scalar_tensor_tensor(state[:, b, c, :], state[:, b, c, :], eg[:, c, last:last + 1],
                                                           k.ps[:, 5 + i % 3, P * (b % 4):P * (b % 4) + P], ALU.mult, ALU.add)
                        ins.then_inc(*n_["state_new"].up())
                rs = X2[1]
                for c in range(4):
                    dve.wait_ge(*n_["sum"].at(c + 1))
                    then(dve.tensor_scalar(rs[:, c, :], k.ps[:, c, 0:T], 1.0 / P, EPS, ALU.mult, ALU.add), n_["mean"])
                dve.wait_ge(*n_["root"].at(2))
                for c in range(4):
                    then(dve.scalar_tensor_tensor(rs[:, c, :], rs[:, c, :], k.vec[:, 48 + c:49 + c], gate[:, c, :], ALU.mult, ALU.mult))
                    then(dve.tensor_tensor(mixed_out[:, c, :], mixed_out[:, c, :], rs[:, c, :], ALU.mult), n_["out"])

            @block.gpsimd
            def _(pool):
                pool.tensor_tensor(kd[:, :, 0:TP], g[:, :, TP - 1:TP].broadcast_to([P, 4, TP]), g[:, :, 0:TP], ALU.subtract)\
                    .then_inc(*n_["kd_diff"].up())
                kds = kd[:, :, TP:T].rearrange("p c (b t) -> p c b t", t=NT)
                gs4 = g[:, :, TP:T].rearrange("p c (b t) -> p c b t", t=NT)
                pool.tensor_tensor(kds, gs4[:, :, :, NT - 1:NT].broadcast_to([P, 4, NB, NT]), gs4, ALU.subtract).then_inc(*n_["kd_diff"].up())
                pool.wait_ge(*n_["tokens_copied"].at(3))
                pool.tensor_tensor(vbd[:, :, :], vt[0:TS, 2, :].unsqueeze(1).broadcast_to([TS, NB, 4 * P]),
                                   k.const("batch_of")[0:TS, :].unsqueeze(2).broadcast_to([TS, NB, 4 * P]), ALU.mult).then_inc(*n_["by_sample"].up())
                pool.wait_ge(*n_["exp"].at(1))
                pool.tensor_tensor(kd[:, :, :], kd[:, :, :], kk[:, :, :], ALU.mult).then_inc(*n_["kd_done"].up())
                pool.wait_ge(*n_["decays"].at(1))
                pool.tensor_tensor(qe[:, :, :], eg[:, :, :], q[:, :, TP:T], ALU.mult).then_inc(*n_["qe_done"].up())

            @block.scalar
            def _(act):
                for l in range(8):
                    act.wait_ge(*n_["diff"].at(l + 1))
                    x = X2[l % 2][:, :, 0:span(levels[l])]
                    act.activation(x, x, ACT.Exp).then_inc(*n_["level_exp"].up())
                    if l == 0:
                        for i, (a, n) in enumerate(TILES):
                            act.wait_ge(*n_["tokens_turned"].at(i + 1))
                            act.copy(vt[0:n, i, :], k.ps[0:n, i, :]).then_inc(*n_["tokens_copied"].up())
                    if l == 2:
                        act.activation(eg[:, :, :], g[:, :, TP:T], ACT.Exp).then_inc(*n_["decays"].up())
                        act.wait_ge(*n_["kd_diff"].at(2))
                        act.activation(kd[:, :, :], kd[:, :, :], ACT.Exp).then_inc(*n_["exp"].up())
                for i, (a, n) in enumerate(TILES):
                    act.wait_ge(*n_["kd_turned"].at(i + 1))
                    act.copy(kdt[0:n, i, :], k.ps[0:n, 5 + i, :]).then_inc(*n_["kd_copied"].up())
                for c in range(4):
                    act.wait_ge(*n_["y_taken"].at(c + 1))
                    act.activation(X2[0][:, c, :], mixed_out[:, c, :], ACT.Square).then_inc(*n_["sq"].up())
                rs = X2[1]
                act.wait_ge(*n_["mean"].at(4))
                act.activation(rs[:, :, :], rs[:, :, :], ACT.Ln).then_inc(*n_["root"].up())
                act.wait_ge(*n_["root"].at(1))
                act.activation(rs[:, :, :], rs[:, :, :], ACT.Exp, scale=-0.5).then_inc(*n_["root"].up())

            @block.tensor
            def _(pe):
                ident = k.const("ident")
                for i, (a, n) in enumerate(TILES):
                    for c in range(4):
                        mm = pe.transpose(k.ps[0:n, i, P * c:P * c + P], v[:, c, a:a + n], ident)
                    mm.then_inc(*n_["tokens_turned"].up())
                for i in range(2):
                    for c in range(4):
                        mm = pe.matmul(k.ps[:, 6 + i, P * c:P * c + P], kk[:, c, P * i:P * i + P], q[:, c, P * i:P * i + P], start=True, stop=True)
                for c in range(4):
                    mm = pe.matmul(k.ps[0:TS, 5, TS * c:TS * c + TS], kk[:, c, TP:T], q[:, c, TP:T], start=True, stop=True)
                mm.then_inc(*n_["diag_dot"].up())
                for l, H in enumerate(levels):
                    x, bank = X2[l % 2], 3 * (l % 2)
                    pe.wait_ge(*n_["level_x"].at(l + 1))
                    if l == 0:
                        pe.wait_ge(*n_["tokens_copied"].at(3))
                    if l >= 1:
                        pe.wait_ge(*n_["level_in"].at(max(l, 1)))
                    if H == P:
                        for c in range(4):
                            mm = pe.matmul(k.ps[:, bank, P * c:P * c + P], x[:, c, 0:P], x[:, c, P:2 * P], start=True, stop=True)
                    else:
                        for i in range(2):
                            for c in range(4):
                                tile = x[:, c, P * i:P * i + P]
                                mm = pe.matmul(k.ps[:, bank + i, P * c:P * c + P], tile, tile, start=True, stop=True)
                        if H <= 2:
                            for c in range(4):
                                mm = pe.matmul(k.ps[0:TS, bank + 2, TS * c:TS * c + TS], x[:, c, TP:T], x[:, c, TP:T], start=True, stop=True)
                    mm.then_inc(*n_["level_dot"].up())
                pe.wait_ge(*n_["kd_done"].at(1))
                pe.wait_ge(*n_["level_in"].at(3))
                for i, (a, n) in enumerate(TILES):
                    for c in range(4):
                        mm = pe.transpose(k.ps[0:n, 5 + i, P * c:P * c + P], kd[:, c, a:a + n], ident)
                    mm.then_inc(*n_["kd_turned"].up())
                pe.wait_ge(*n_["level_in"].at(9))
                pe.wait_ge(*n_["state_in"].at(16))
                pe.wait_ge(*n_["qe_done"].at(1))
                for c in range(4):
                    cols = slice(P * c, P * c + P)
                    pe.matmul(k.ps[:, c, 0:P], vt[:, 0, cols], att[:, 0, c, :], start=True, stop=True)
                    pe.matmul(k.ps[:, c, P:TP], vt[:, 1, cols], att[:, 1, c, :], start=True, stop=False)
                    pe.matmul(k.ps[:, c, P:TP], vt[:, 0, cols], attx[:, c, :], start=False, stop=True)
                    pe.matmul(k.ps[:, c, TP:T], vt[0:TS, 2, cols], atts[:, c, :], start=True, stop=False, skip_group_check=True)
                    for b in range(NB):
                        mm = pe.matmul(k.ps[:, c, TP + NT * b:TP + NT * b + NT], state[:, b, c, :],
                                       qe[:, c, NT * b:NT * b + NT], start=False, stop=b == NB - 1, skip_group_check=True)
                    mm.then_inc(*n_["y_dot"].up())
                pe.wait_ge(*n_["kd_copied"].at(3))
                for c in range(4):
                    for i in range(2):
                        mm = pe.matmul(k.ps[:, 4, P * c:P * c + P], kdt[:, i, P * c:P * c + P], vt[:, i, P * c:P * c + P],
                                       start=i == 0, stop=i == 1)
                mm.then_inc(*n_["state_dot"].up())
                pe.wait_ge(*n_["by_sample"].at(1))
                for i in range(8):
                    c, hf = i // 2, i % 2
                    if i >= 3:
                        pe.wait_ge(*n_["state_new"].at(i - 2))
                    pe.matmul(k.ps[:, 5 + i % 3, :], kdt[0:TS, 2, P * c:P * c + P], vbd[:, 4 * hf:4 * hf + 4, P * c:P * c + P],
                              start=True, stop=True).then_inc(*n_["state_dot"].up())
                sq = X2[0]
                for c in range(4):
                    pe.wait_ge(*n_["sq"].at(c + 1))
                    pe.matmul(k.ps[:, c, 0:T], k.const("ones"), sq[:, c, :], start=True, stop=True).then_inc(*n_["sum"].up())


def stage_turn_decays(k, conv_in, conv_in_s, dt, dta, par):
    acum, wend, dtt = dta["acum"], dta["wend"], dta["tok"]
    with ExitStack() as s:
        rows_p = k.sb(s, "conv_rows_p", [3, CC * P])
        rows_s = k.sb(s, "conv_rows_s", [3 * NB, CC * P])
        last3 = k.sb(s, "conv_last3", [P, CC, 3 * NB])
        packed, rows_turned, rows_copied, stored = (k.count(n) for n in ("placed", "turned", "copied", "stored"))
        dt_turned, dt_copied = k.count("d_turned"), k.count("d_copied")
        with k.stage() as block:
            @block.sync
            def _(sp):
                sp.wait_ge(*rows_copied.at(1))
                sp.dma_start(k.outs[14][0, 0], rows_p[:, :]).then_inc(*stored.up(16))
                sp.wait_ge(*rows_copied.at(2))
                sp.dma_start(k.outs[15].rearrange("b a r c -> (b a r) c"), rows_s[:, :]).then_inc(*stored.up(16))
                sp.wait_ge(*stored.at(32))

            @block.vector
            def _(dve):
                dve.tensor_copy(last3[:, :, :].rearrange("p c (b r) -> p c b r", r=3), conv_in_s[:, :, :, NT:NT + 3]).then_inc(*packed.up())
                for n, (dst, rows) in enumerate(((rows_p, 3), (rows_s, 24))):
                    dve.wait_ge(*rows_turned.at(n + 1))
                    dve.tensor_copy(dst[:, :].rearrange("r (b n) -> r b n", b=3), k.ps[0:rows, 3 * n:3 * n + 3, :]).then_inc(*rows_copied.up())

            @block.scalar
            def _(act):
                act.wait_ge(*dt_turned.at(1))
                act.copy(dtt[:, 0:2, :], k.ps[:, 6, 0:96].rearrange("p (i n) -> p i n", i=2)).then_inc(*dt_copied.up())
                act.copy(dtt[0:TS, 2, :], k.ps[0:TS, 6, 96:144]).then_inc(*dt_copied.up())
                act.copy(dta["skip"][:, :], k.ps[:, 7, 0:8]).then_inc(*dt_copied.up())

            @block.tensor
            def _(pe):
                ident = k.const("ident")
                pe.wait_ge(*packed.at(1))
                for n in range(2):
                    for c in range(CC):
                        in_ = last3[:, c, :] if n else conv_in[:, c, TP:TP + 3]
                        mm = pe.transpose(k.ps[0:24 if n else 3, 3 * n + c // 4, P * (c % 4):P * (c % 4) + P], in_, ident)
                    mm.then_inc(*rows_turned.up())
                pairs = k.const("head_pair")
                for j in range(8):
                    pe.matmul(k.ps[:, 7, j:j + 1], pairs[0:HM, P * j:P * j + P], par[:, 2:3], start=True, stop=True)
                for i, (a, n) in enumerate(TILES):
                    for m, src in enumerate((acum, dt, wend)):
                        mm = pe.transpose(k.ps[0:n, 6, 48 * i + 16 * m:48 * i + 16 * m + 16], src[:, a:a + n], ident[0:HM, 0:HM])
                mm.then_inc(*dt_turned.up())


SUM_BANKS = (2, 3, 4, 6)
TURN_BANKS = (0, 1, 6, 7)


def stage_ssd(k, proj, xc, dt, dta, mixed_out):
    acum, dtt = dta["acum"], dta["tok"]
    first_out = 4
    act_step, dve_step = k.count("act_step"), k.count("dve_step")
    with ExitStack() as s:
        xt = k.sb(s, "x_tokens", [P, 3, D])
        bt = k.sb(s, "b_tokens", [P, 3, 256])
        gm = k.sb(s, "cb", [P, 4, 416])
        dec = [k.sb(s, f"decay{n}", [P, 416]) for n in range(2)]
        sc = [k.sb(s, f"scores{n}", [P, 416]) for n in range(2)]
        state = k.sb(s, "ssm_state", [P, NB, 8, 64])
        stT = k.sb(s, "ssm_state_t", [P, NB, 4, P])
        statep = k.sb(s, "ssm_state_p", [P, 8, 64])
        ebc = k.sb(s, "ebc", [P, 8, TS])
        inter = k.sb(s, "inter", [P, 8, TS])
        bbd = proj[0:TS, 0:NB, 0:256]
        c_by_sample = [proj[:, V + b // 2, P * (b % 2):P * (b % 2) + P].rearrange("p (g z) -> p g z", g=2) for b in range(NB)]
        inter_tok = proj[0:2 * TS, G:G + 2, 0:TP]
        names = ("state_in", "tokens_turned", "cb_dot", "cb_copied", "row", "diff", "exp", "scores", "y_dot", "y_taken",
                 "st_turned", "ebc_dot", "ebc_exp", "inter_dot", "inter_tok", "inter_taken", "zeroed", "placed", "xw", "by_sample", "state_dot", "state_new",
                 "statep", "stored", "scaled", "sq", "sum", "mean", "root", "out")
        n_ = {x: k.count(x) for x in names}
        tokens_copied = (k.count("tokens_copied"), k.count("odd_tokens_copied"))
        st_copied = (k.count("st_copied"), k.count("odd_st_copied"))

        def slot(j):
            return 4 * (j // 4) + 2 * (j % 2) + (j // 2) % 2

        by_part = (0, 4, 1, 5, 2, 6, 3, 7)

        def parts(x):
            y = x[:, :, :, :].rearrange("p b (J w v) n -> p (b J) w v n", w=2, v=2)
            return [y[:, :, w, v, :] for v in range(2) for w in range(2)]

        def dram_parts(x):
            y = x.rearrange("b a (J v w u) p n -> v w (u p) (b a J) n", v=2, w=2, u=2)
            return [y[v, w] for v in range(2) for w in range(2)]

        def brow(g):
            return slice(64 * (g % 2), 64 * (g % 2) + 64)

        def take_tokens(eng, odd):
            for n in range(odd, 9, 2):
                i, u = n // 3, n % 3
                m = TILES[i][1]
                dst = xt[0:m, i, 512 * u:512 * u + 512] if u < 2 else bt[0:m, i, :]
                eng.wait_ge(*n_["tokens_turned"].at(n + 1))
                copy(eng, dst, k.ps[0:m, TURN_BANKS[n % 4], 0:dst.shape[1]]).then_inc(*tokens_copied[odd].up())

        def take_states(eng, odd):
            for b in range(odd, NB, 2):
                eng.wait_ge(*n_["st_turned"].at(b + 1))
                copy(eng, stT[:, b, :, :], k.ps[:, TURN_BANKS[b % 4], :].rearrange("p (q n) -> p q n", q=4)).then_inc(*st_copied[odd].up())

        with k.stage() as block:
            @block.sync
            def _(sp):
                for dst, src in zip(parts(state), dram_parts(k.ins["state_ssm"])):
                    sp.dma_start(dst, src).then_inc(*n_["state_in"].up(16))
                sp.wait_ge(*n_["statep"].at(1))
                sp.dma_start(k.outs[12][0, 0].rearrange("(j u) p n -> (u p) j n", u=2), statep[:, :, :]).then_inc(*n_["stored"].up(16))
                for n, (src, dst) in enumerate(zip(parts(state), dram_parts(k.outs[13]))):
                    sp.wait_ge(*n_["state_new"].at(2 * n + 3))
                    sp.dma_start(dst, src).then_inc(*n_["stored"].up(16))
                sp.wait_ge(*n_["stored"].at(80))

            @block.tensor
            def _(pe):
                ident = k.const("ident")

                def row(h):
                    if h >= 2:
                        pe.wait_ge(*n_["diff"].at(3 * (h - 1)))
                    pe.matmul(k.ps[:, h % 2, 0:T], ident[0:HM, h:h + 1].broadcast_to([HM, P]), acum[:, :], start=True, stop=True)\
                      .then_inc(*n_["row"].up())

                n = 0
                for i, (a, m) in enumerate(TILES):
                    for u in range(3):
                        if n >= 4:
                            pe.wait_ge(*tokens_copied[n % 2].at(n // 2 - 1))
                        for c in range(4 if u < 2 else 2):
                            mm = pe.transpose(k.ps[0:m, TURN_BANKS[n % 4], P * c:P * c + P], xc[:, 4 * u + c, a:a + m], ident)
                        mm.then_inc(*n_["tokens_turned"].up())
                        n += 1
                for g in range(4):
                    b, c, r = xc[:, 8 + g // 2, :], xc[:, 10 + g // 2, :], brow(g)
                    if g >= 1:
                        pe.wait_ge(*n_["cb_copied"].at(g))
                    pe.matmul(k.ps[:, 2, 0:TP], b[r, 0:P], c[r, 0:TP], start=True, stop=True)
                    pe.matmul(k.ps[:, 2, TP:TP + P], b[r, P:TP], c[r, P:TP], start=True, stop=True)
                    pe.matmul(k.ps[0:TS, 2, 384:416], b[r, TP:T], c[r, TP:T], start=True, stop=True).then_inc(*n_["cb_dot"].up())
                pe.wait_ge(*n_["state_in"].at(64))
                pe.wait_ge(*tokens_copied[0].at(5))
                pe.wait_ge(*tokens_copied[1].at(4))
                for b in range(NB):
                    if b >= 4:
                        pe.wait_ge(*st_copied[b % 2].at(b // 2 - 1))
                    for q in range(4):
                        mm = pe.transpose(k.ps[:, TURN_BANKS[b % 4], P * q:P * q + P], state[:, b, 2 * q:2 * q + 2, :].rearrange("p v n -> p (v n)"), ident)
                    mm.then_inc(*n_["st_turned"].up())
                pe.wait_ge(*n_["cb_copied"].at(4))
                pairs = k.const("head_pair")
                for j in range(8):
                    mm = pe.matmul(k.ps[:, 2, TS * slot(j):TS * slot(j) + TS], pairs[0:HM, P * j:P * j + P], acum[:, TP:T], start=True, stop=True)
                mm.then_inc(*n_["ebc_dot"].up())
                for copied in st_copied:
                    pe.wait_ge(*copied.at(NB // 2))
                row(0)
                row(1)
                pe.wait_ge(*n_["placed"].at(2))
                for gg in range(2):
                    for b in range(NB):
                        mm = pe.matmul(k.ps[0:2 * TS, 3, TP * gg:TP * gg + TP], c_by_sample[b][:, gg, :],
                                       stT[:, b, 2 * gg:2 * gg + 2, :].rearrange("p q n -> p (q n)"), start=b == 0, stop=b == NB - 1)
                mm.then_inc(*n_["inter_tok"].up())
                pe.wait_ge(*n_["inter_taken"].at(1))
                for par in range(2):
                    for j in range(8):
                        g = j // 2
                        if g % 2 == par:
                            rows = slice(TS * par, TS * par + TS)
                            mm = pe.transpose(k.ps[:, 3 + par, TS * j:TS * j + TS], inter_tok[rows, g // 2, P * (j % 2):P * (j % 2) + P],
                                              ident[rows, rows])
                mm.then_inc(*n_["inter_dot"].up())

                for h in range(HM):
                    if h + 2 < HM:
                        row(h + 2)
                    pe.wait_ge(*n_["scores"].at(3 * h + 3))
                    if h % 2 == 0 and h >= 4:
                        pe.wait_ge(*n_["y_taken"].at(h // 2 - 1))
                    r, bank, x = slice(64 * (h % 2), 64 * (h % 2) + 64), 6 + (h // 2) % 2, slice(64 * h, 64 * h + 64)
                    m = sc[h % 2]
                    pe.matmul(k.ps[r, bank, 0:TP], xt[:, 0, x], m[:, 0:TP], start=True, stop=False, skip_group_check=True)
                    pe.matmul(k.ps[r, bank, P:TP], xt[:, 1, x], m[:, TP:TP + P], start=False, stop=True, skip_group_check=True)
                    pe.matmul(k.ps[r, bank, TP:T], xt[0:TS, 2, x], m[0:TS, 384:416], start=True, stop=True).then_inc(*n_["y_dot"].up())
                for g in range(4):
                    pe.wait_ge(*n_["sq"].at(2 * g + 2))
                    for u in range(2):
                        mm = pe.matmul(k.ps[:, SUM_BANKS[g], 0:T], k.const("ones"),
                                       dta["sq"][:, 2 * g + u, :], start=u == 0, stop=u == 1)
                    mm.then_inc(*n_["sum"].up())
                pe.wait_ge(*n_["xw"].at(3))
                for j in range(8):
                    for i in range(2):
                        mm = pe.matmul(k.ps[:, 5, 64 * j:64 * j + 64], xt[:, i, P * j:P * j + P], bt[:, i, 64 * (j // 2):64 * (j // 2) + 64],
                                       start=i == 0, stop=i == 1)
                mm.then_inc(*n_["state_dot"].up())
                pe.wait_ge(*n_["by_sample"].at(1))
                for n, j in enumerate(by_part):
                    if n >= 2:
                        pe.wait_ge(*n_["state_new"].at(n))
                    g = j // 2
                    pe.matmul(k.ps[:, n % 2, :], xt[0:TS, 2, P * j:P * j + P], bbd[:, :, 64 * g:64 * g + 64],
                              start=True, stop=True).then_inc(*n_["state_dot"].up())

            @block.vector
            def _(dve):
                def then(ins, sig=dve_step):
                    ins.then_inc(*sig.up())
                    dve.wait_ge(*sig.all())
                take_tokens(dve, 0)
                for g in range(4):
                    dve.wait_ge(*n_["cb_dot"].at(g + 1))
                    dve.tensor_copy(gm[0:TS, g, 384:416], k.ps[0:TS, 2, 384:416]).then_inc(*dve_step.up())
                    dve.tensor_copy(gm[:, g, 0:384], k.ps[:, 2, 0:384]).then_inc(*n_["cb_copied"].up())
                take_states(dve, 0)
                dve.wait_ge(*n_["cb_copied"].at(4))
                for copied in tokens_copied:
                    dve.wait_ge(*copied.all())


                def diff(h):
                    bank, d = k.ps[:, h % 2, :], dec[h % 2]
                    dve.wait_ge(*n_["row"].at(h + 1))
                    if h >= 2:
                        dve.wait_ge(*n_["scores"].at(3 * (h - 1)))
                    fut = k.const("ssd_future")
                    for rows, dcol, bcol, w, i, mask in ((P, 0, 0, TP, 0, fut[:, 0:TP]), (P, TP, P, P, 1, fut[:, 0:P]),
                                                         (TS, 384, TP, TS, 2, k.const("ssd_future_s")[0:TS, :])):
                        dve.scalar_tensor_tensor(d[0:rows, dcol:dcol + w], bank[0:rows, bcol:bcol + w], dtt[0:rows, i, h:h + 1], mask,
                                                 ALU.subtract, ALU.add).then_inc(*n_["diff"].up())

                def score(h):
                    d, m, g = dec[h % 2], sc[h % 2], h // 4
                    dve.wait_ge(*n_["exp"].at(2 * h + 2))
                    if h >= 2:
                        dve.wait_ge(*n_["y_dot"].at(h - 1))
                    for rows, col, w, i in ((P, 0, TP, 0), (P, TP, P, 1), (TS, 384, TS, 2)):
                        dve.scalar_tensor_tensor(m[0:rows, col:col + w], d[0:rows, col:col + w], dtt[0:rows, i, 16 + h:17 + h],
                                                 gm[0:rows, g, col:col + w], ALU.mult, ALU.mult).then_inc(*n_["scores"].up())

                def take(j):
                    bank = k.ps[:, 6 + j % 2, :]
                    y = mixed_out[:, first_out + j, :]
                    dve.wait_ge(*n_["y_dot"].at(2 * j + 2))
                    then(dve.scalar_tensor_tensor(y, xc[:, j, :], dta["skip"][:, j:j + 1], bank[:, 0:T], ALU.mult, ALU.add), n_["y_taken"])
                    if j == 0:
                        dve.wait_ge(*n_["ebc_exp"].at(1))
                        dve.wait_ge(*n_["inter_dot"].at(1))
                        for par in range(2):
                            pv = k.ps[:, 3 + par, 0:TP].rearrange("p (j t) -> p j t", t=TS)
                            for jj in (0, 1, 4, 5) if par == 0 else (2, 3, 6, 7):
                                then(dve.tensor_tensor(inter[:, jj, :], pv[:, jj, :], ebc[:, slot(jj), :], ALU.mult))
                    then(dve.tensor_tensor(y[:, TP:T], y[:, TP:T], inter[:, j, :], ALU.add))
                    then(dve.tensor_tensor(y, y, proj[:, Z + j, :], ALU.mult), n_["scaled"])

                diff(0)
                dve.wait_ge(*n_["inter_tok"].at(1))
                dve.tensor_copy(inter_tok[:, :, :], k.ps[0:2 * TS, 3, :].rearrange("p (g n) -> p g n", g=2)).then_inc(*n_["inter_taken"].up())
                for h in range(HM):
                    if h + 1 < HM:
                        diff(h + 1)
                    score(h)
                    if h >= 2 and h % 2 == 1:
                        take(h // 2 - 1)
                take(7)
                for i, (a, m) in enumerate(TILES):
                    v = xt[0:m, i, :].rearrange("p (h n) -> p h n", h=HM)
                    then(dve.tensor_tensor(v, v, dtt[0:m, i, 32:48].unsqueeze(2).broadcast_to([m, HM, 64]), ALU.mult), n_["xw"])
                rs = dta["rs"]
                for g in range(4):
                    dve.wait_ge(*n_["sum"].at(g + 1))
                    dve.tensor_scalar(rs[:, g, :], k.ps[:, SUM_BANKS[g], 0:T], 1.0 / 256, EPS, ALU.mult, ALU.add).then_inc(*n_["mean"].up())
                dve.wait_ge(*n_["root"].at(2))
                for j in range(8):
                    y = mixed_out[:, first_out + j, :]
                    dve.scalar_tensor_tensor(y, y, k.vec[:, 52 + j:53 + j], rs[:, j // 2, :], ALU.mult, ALU.mult).then_inc(*n_["out"].up())
                dve.wait_ge(*n_["state_dot"].at(1))
                dve.tensor_copy(statep[:, :, :], k.ps[:, 5, :].rearrange("p (j n) -> p j n", j=8)).then_inc(*n_["statep"].up())
                dve.wait_ge(*n_["state_new"].at(1))
                for n, j in enumerate(by_part):
                    dve.wait_ge(*n_["state_dot"].at(n + 2))
                    dve.tensor_tensor(state[:, :, slot(j), :], state[:, :, slot(j), :], k.ps[:, n % 2, :].rearrange("p (b n) -> p b n", b=NB),
                                      ALU.add).then_inc(*n_["state_new"].up())

            @block.gpsimd
            def _(pool):
                pool.memset(proj[:, V:V + 4, 0:256], 0.0).then_inc(*n_["zeroed"].up())
                pool.wait_ge(*n_["zeroed"].at(1))
                for par in range(2):
                    r = brow(par)
                    for b in range(NB):
                        ins = pool.tensor_copy(c_by_sample[b][r, :, TS * par + NT * b:TS * par + NT * b + NT],
                                               xc[r, 10:12, TP + NT * b:TP + NT * b + NT])
                    ins.then_inc(*n_["placed"].up())
                    pool.wait_ge(*n_["placed"].at(par + 1))
                pool.wait_ge(*tokens_copied[0].at(5))
                pool.tensor_tensor(bbd, bt[0:TS, 2, :].unsqueeze(1).broadcast_to([TS, NB, 256]),
                                   k.const("batch_of")[0:TS, :].unsqueeze(2).broadcast_to([TS, NB, 256]), ALU.mult).then_inc(*n_["by_sample"].up())
                pool.wait_ge(*n_["ebc_exp"].at(1))
                pool.wait_ge(*n_["st_turned"].at(NB))
                last = ebc[:, :, :].rearrange("p j (b t) -> p b j t", t=NT)[:, :, :, NT - 1:NT]
                pool.tensor_tensor(state[:, :, :, :], state[:, :, :, :], last.broadcast_to([P, NB, 8, 64]), ALU.mult).then_inc(*n_["state_new"].up())

            @block.scalar
            def _(act):
                take_tokens(act, 1)
                take_states(act, 1)
                act.wait_ge(*n_["ebc_dot"].at(1))
                act.activation(ebc[:, :, :], k.ps[:, 2, 0:TP].rearrange("p (j t) -> p j t", t=TS), ACT.Exp).then_inc(*n_["ebc_exp"].up())

                def square(j):
                    act.wait_ge(*n_["scaled"].at(j + 1))
                    act.activation(dta["sq"][:, j, :], mixed_out[:, first_out + j, :], ACT.Square).then_inc(*n_["sq"].up())

                for h in range(HM):
                    act.wait_ge(*n_["diff"].at(3 * h + 3))
                    d = dec[h % 2]
                    act.activation(d[:, 0:384], d[:, 0:384], ACT.Exp).then_inc(*n_["exp"].up())
                    act.activation(d[0:TS, 384:416], d[0:TS, 384:416], ACT.Exp).then_inc(*n_["exp"].up())
                    if h >= 4 and h % 2 == 0:
                        square(h // 2 - 2)
                square(6)
                square(7)
                rs = dta["rs"]
                act.wait_ge(*n_["mean"].at(4))
                act.activation(rs[:, :, :], rs[:, :, :], ACT.Ln).then_inc(*n_["root"].up())
                act.wait_ge(*n_["root"].at(1))
                act.activation(rs[:, :, :], rs[:, :, :], ACT.Exp, scale=-0.5).then_inc(*n_["root"].up())



def stage_route(k, moe):
    I = MAX_ITEMS + 1
    with ExitStack() as s:
        wr = k.sb(s, "w_router", [P, DC, NE])
        lg = k.sb(s, "logits", [P, 3, NE])
        gt = k.sb(s, "greater", [P, 3, NE, NE])
        eq = k.sb(s, "equal", [P, 3, NE, NE])
        chosen = k.sb(s, "chosen", [P, 3, NE])
        gate = k.sb(s, "gate", [P, 3, NE])
        place = k.sb(s, "place", [P, 3, NE])
        cnt = k.sb(s, "cnt", [P, 4, NE])
        one = k.sb(s, "item_expert", [P, I, NE])
        blk = k.sb(s, "item_block", [P, I, NE])
        tmp = k.sb(s, "item_tmp", [P, 3, I, NE])
        tmp2 = k.sb(s, "item_tmp2", [P, 3, I, NE])
        norm = Norm(k, s, "norm_ffn_odd")
        ids = k.sb(s, "item_ids", [P, I + 1])
        small = k.sb(s, "small", [P, 3, 2])
        wr_in, logit, turned, copied, exp_in, exped, chose, ranked = (k.count(n) for n in (
            "router_in", "scored", "turned", "copied", "diff", "exped", "chosen", "ranked"))
        dve_step = k.count("dve_step")
        with k.stage() as block:
            @block.sync
            def _(sp):
                sp.dma_start(wr[:, :, :], k.ins["w_router"][0].rearrange("(c p) e -> p c e", p=P)).then_inc(*wr_in.up(16))

            @block.tensor
            def _(pe):
                norm.sums(pe)
                pe.wait_ge(*wr_in.at(16))
                for i, (a, n) in enumerate(TILES):
                    for c in range(DC):
                        if i == 0:
                            norm.await_chunk(pe, c)
                        mm = pe.matmul(k.ps[0:n, 0, NE * i:NE * i + NE], k.act[:, c, a:a + n], wr[:, c, :], start=c == 0, stop=c == DC - 1)
                mm.then_inc(*logit.up())
                for i, (a, n) in enumerate(TILES):
                    for u in range(2):
                        for c in range(4):
                            mm = pe.transpose(k.ps[0:n, 2 + 2 * i + u, P * c:P * c + P], k.act[:, 4 * u + c, a:a + n], k.const("ident"))
                        mm.then_inc(*turned.up())
                pe.wait_ge(*chose.at(1))
                for i in range(3):
                    for e in range(i + 1):
                        pe.matmul(k.ps[:, 1, NE * i:NE * i + NE], k.const("ones") if e < i else k.const("before"), chosen[:, e, :],
                                  start=e == 0, stop=e == i)
                for i in range(3):
                    mm = pe.matmul(k.ps[:, 1, 32:32 + NE], k.const("ones"), chosen[:, i, :], start=i == 0, stop=i == 2)
                mm.then_inc(*ranked.up())

            @block.scalar
            def _(act):
                norm.squares(act)
                norm.roots(act)
                for n in range(6):
                    act.wait_ge(*turned.at(n + 1))
                    rows = TILES[n // 2][1]
                    act.copy(moe["tokens_hi"][0:rows, n // 2, 512 * (n % 2):512 * (n % 2) + 512], k.ps[0:rows, 2 + n, :]).then_inc(*copied.up())
                act.wait_ge(*exp_in.at(1))
                act.activation(gate[:, :, :], gate[:, :, :], ACT.Exp).then_inc(*exped.up())

            @block.vector
            def _(dve):
                def then(ins, sig=dve_step):
                    ins.then_inc(*sig.up())
                    dve.wait_ge(*sig.all())
                then(dve.memset(lg[:, :, :], 0.0))
                norm.apply(dve)
                dve.wait_ge(*logit.at(1))
                dve.tensor_copy(lg[0:TS, 2, :], k.ps[0:TS, 0, 16:24]).then_inc(*dve_step.up())
                then(dve.tensor_copy(lg[:, 0:2, :], k.ps[:, 0, 0:16].rearrange("p (i e) -> p i e", i=2)))
                other = lg[:, :, :].unsqueeze(2).broadcast_to([P, 3, NE, NE])
                mine = lg[:, :, :].unsqueeze(3).broadcast_to([P, 3, NE, NE])
                then(dve.tensor_tensor(gt[:, :, :, :], other, mine, ALU.is_gt))
                then(dve.tensor_tensor(eq[:, :, :, :], other, mine, ALU.is_equal))
                earlier = k.const("earlier_expert").rearrange("p (e f) -> p e f", e=NE).unsqueeze(1).broadcast_to([P, 3, NE, NE])
                then(dve.tensor_tensor(eq[:, :, :, :], eq[:, :, :, :], earlier, ALU.mult))
                then(dve.tensor_tensor(gt[:, :, :, :], gt[:, :, :, :], eq[:, :, :, :], ALU.add))
                then(dve.tensor_reduce(chosen[:, :, :], gt[:, :, :, :], AX, ALU.add))
                then(dve.tensor_scalar(chosen[:, :, :], chosen[:, :, :], 2.0, None, ALU.is_lt))
                valid = k.const("valid").rearrange("p (i e) -> p i e", i=3)
                then(dve.tensor_tensor(chosen[:, :, :], chosen[:, :, :], valid, ALU.mult), chose)
                for n in range(6):
                    dve.wait_ge(*copied.at(n + 1))
                    rows, at = TILES[n // 2][1], slice(512 * (n % 2), 512 * (n % 2) + 512)
                    dve.tensor_tensor(moe["tokens_lo"][0:rows, n // 2, at], k.ps[0:rows, 2 + n, :],
                                      moe["tokens_hi"][0:rows, n // 2, at].bitcast(F32), ALU.subtract).then_inc(*dve_step.up())
                then(dve.tensor_reduce(small[:, :, 0:1], lg[:, :, :], AX, ALU.max))
                then(dve.tensor_tensor(gate[:, :, :], lg[:, :, :], small[:, :, 0:1].broadcast_to([P, 3, NE]), ALU.subtract), exp_in)
                dve.wait_ge(*exped.at(1))
                then(dve.tensor_tensor(gate[:, :, :], gate[:, :, :], chosen[:, :, :], ALU.mult))
                then(dve.tensor_reduce(small[:, :, 1:2], gate[:, :, :], AX, ALU.add))
                then(dve.tensor_scalar(small[:, :, 1:2], small[:, :, 1:2], 1e-30, None, ALU.max))
                then(dve.reciprocal(small[:, :, 1:2], small[:, :, 1:2]))
                then(dve.tensor_tensor(gate[:, :, :], gate[:, :, :], small[:, :, 1:2].broadcast_to([P, 3, NE]), ALU.mult))
                dve.wait_ge(*ranked.at(1))
                then(dve.tensor_copy(cnt[:, 0, :], k.ps[:, 1, 32:32 + NE]))
                then(dve.scalar_tensor_tensor(place[:, :, :], k.ps[:, 1, 0:24].rearrange("p (i e) -> p i e", i=3), 1.0, chosen[:, :, :],
                                              ALU.add, ALU.mult))
                then(dve.tensor_scalar(cnt[:, 1, :], cnt[:, 0, :], 0.0, None, ALU.is_gt))
                for edge in (128.0, 256.0):
                    then(dve.scalar_tensor_tensor(cnt[:, 1, :], cnt[:, 0, :], edge, cnt[:, 1, :], ALU.is_gt, ALU.add))
                then(dve.tensor_tensor_scan(cnt[:, 2, :], k.ones_wide[:, 0:NE], cnt[:, 1, :], 0.0, ALU.mult, ALU.add))
                then(dve.tensor_tensor(cnt[:, 3, :], cnt[:, 2, :], cnt[:, 1, :], ALU.subtract))
                item = k.const("items").unsqueeze(2).broadcast_to([P, I, NE])
                per = lambda ap: ap.unsqueeze(1).broadcast_to([P, I, NE])
                then(dve.tensor_tensor(blk[:, :, :], item, per(cnt[:, 3, :]), ALU.subtract))
                then(dve.tensor_tensor(tmp[:, 0, :, :], item, per(cnt[:, 2, :]), ALU.is_lt))
                then(dve.scalar_tensor_tensor(one[:, :, :], blk[:, :, :], 0.0, tmp[:, 0, :, :], ALU.is_ge, ALU.mult))
                then(dve.scalar_tensor_tensor(blk[:, :, :], blk[:, :, :], float(P), one[:, :, :], ALU.mult, ALU.mult))
                then(dve.tensor_tensor(tmp[:, 0, :, :], one[:, :, :], per(k.const("expert_ids")), ALU.mult))
                then(dve.tensor_reduce(ids[:, 0:I], tmp[:, 0, :, :], AX, ALU.add))
                then(dve.tensor_copy(ids[:, I:I + 1], cnt[:, 2, NE - 1:NE]))
                then(dve.tensor_copy(moe["table"][:, :], ids[0:1, :]))
                items_of = lambda ap: ap.unsqueeze(1).broadcast_to([P, 3, I, NE])
                tiles_of = lambda ap: ap.unsqueeze(2).broadcast_to([P, 3, I, NE])
                dve.tensor_tensor(tmp[:, :, :, :], items_of(one[:, :, :]), tiles_of(place[:, :, :]), ALU.mult).then_inc(*dve_step.up())
                then(dve.tensor_tensor(tmp2[:, :, :, :], items_of(blk[:, :, :]), tiles_of(chosen[:, :, :]), ALU.mult))
                then(dve.tensor_tensor(tmp[:, :, :, :], tmp[:, :, :, :], tmp2[:, :, :, :], ALU.subtract))
                then(dve.tensor_tensor(tmp2[:, :, :, :], items_of(one[:, :, :]), tiles_of(gate[:, :, :]), ALU.mult))
                dve.tensor_reduce(moe["gate"][:, :, :], tmp2[:, :, :, :], AX, ALU.add).then_inc(*dve_step.up())
                then(dve.tensor_reduce(moe["slot"][:, :, :], tmp[:, :, :, :], AX, ALU.add))
                then(dve.tensor_scalar(moe["slot"][:, :, :], moe["slot"][:, :, :], -1.0, None, ALU.add))


def stage_experts(k, moe):
    GROUPS = FE // WCOLS
    UP = 4 * GROUPS
    BLOCKS = UP + FEC // 2
    HALF = SLOT // 2
    PARTS = 3
    I = MAX_ITEMS + 1
    GATHER = BLOCKS - 5
    slot_of, gate_of, table, tok_hi, tok_lo = (moe[x] for x in ("slot", "gate", "table", "tokens_hi", "tokens_lo"))
    ins = k.ins
    with ExitStack() as s:
        ring = k.sb(s, "moe_ring", [P, MOE_SLOTS, HALF])
        w_hi = k.sb(s, "moe_w_hi", [P, PARTS, HALF], F32R)
        w_lo = k.sb(s, "moe_w_lo", [P, PARTS, HALF], F32R)
        pick = k.sb(s, "pick", [P, 3, P], F32R)
        weigh = k.sb(s, "weigh", [P, 3, P])
        weighT = k.sb(s, "weigh_t", [P, T])
        xg = [k.sb(s, "item_tokens" + x, [P, DC, P], F32R) for x in ("_hi", "_lo")]
        hidT = [k.sb(s, "hid_t" + x, [P, FEC, P], F32R) for x in ("_hi", "_lo")]
        hid = k.sb(s, "hid", [P, 2, WCOLS])
        free = k.act[:, :, :].rearrange("p c t -> p (c t)")
        gated = free[:, 0:2 * WCOLS].rearrange("p (a n) -> p a n", a=2)
        y = free[:, 2 * WCOLS:2 * WCOLS + D]
        names = ("slot_free", "part_free", "hi_ready", "pick_ready", "gathered", "xg_act", "xg_dve", "silu_done", "hid_done",
                 "hid_turned", "hidt_hi", "hidt_lo", "weigh_turned", "weigh_copied", "y_low", "y_high", "spread", "added", "zeroed")
        n_ = {x: k.count("m_" + x).sem for x in names}
        loaded = [k.count(f"m_loaded{x}").sem for x in range(MOE_SLOTS)]

        def used(i, b):
            return n_["part_free"], i * BLOCKS + (PARTS + b + 1)

        def count_of(eng):
            return eng.value_load(table[0:1, I:I + 1], min_val=1, max_val=MAX_ITEMS)

        def shaped(buf, b):
            return buf.rearrange("p (c f) -> p c f", c=4 if b < UP else 2)

        with k.stage() as block:
            @block.sync
            def _(sp):
                n_items = count_of(sp)
                with sp.Fori(0, n_items) as i:
                    e = sp.value_load(table[0:1, bass.ds(i, 1)], min_val=0, max_val=NE - 1)
                    for b in range(BLOCKS):
                        sp.wait_ge(n_["slot_free"], i * BLOCKS + (b + 1))
                        if b < UP:
                            w = ins["we3" if b // 2 % 2 else "we1"][0, bass.ds(e, 1)].rearrange("a (c p) f -> p (a c) f", p=P)
                            src = w[:, 4 * (b % 2):4 * (b % 2) + 4, WCOLS * (b // 4):WCOLS * (b // 4) + WCOLS]
                        else:
                            w = ins["we2"][0, bass.ds(e, 1)].rearrange("a (f p) d -> p (a f) d", p=P)
                            src = w[:, 2 * (b - UP):2 * (b - UP) + 2, :]
                        sp.dma_start(shaped(ring[:, b % MOE_SLOTS, :], b), src).then_inc(loaded[b % MOE_SLOTS], 16)

            @block.gpsimd
            def _(pool):
                pool.sem_inc(n_["slot_free"], MOE_SLOTS)
                pool.sem_inc(n_["part_free"], PARTS)

            @block.tensor
            def _(pe):
                ident = k.const("ident")

                def gather():
                    for tok, first_bank in ((tok_hi, 6), (tok_lo, 0)):
                        for c in range(DC):
                            for t, (_, n) in enumerate(TILES):
                                mm = pe.matmul(k.ps[:, first_bank + c // 4, P * (c % 4):P * (c % 4) + P],
                                               tok[0:n, t, P * c:P * c + P], pick[0:n, t, :], start=t == 0, stop=t == 2)
                    mm.then_inc(n_["gathered"], 1)

                def turn(i, n):
                    pe.wait_ge(n_["hid_done"], i * GROUPS + (n + 1))
                    if n >= 2:
                        pe.wait_ge(n_["hidt_hi"], i * GROUPS + (n - 1))
                        pe.wait_ge(n_["hidt_lo"], i * GROUPS + (n - 1))
                    for j in range(4):
                        mm = pe.transpose(k.ps[:, 6 + n % 2, P * j:P * j + P], hid[:, n % 2, P * j:P * j + P], ident)
                    mm.then_inc(n_["hid_turned"], 1)

                def spread(i, m):
                    if m == 0:
                        pe.wait_ge(n_["y_low"], i + 1)
                        pe.wait_ge(n_["y_high"], i + 1)
                    if m >= 2:
                        pe.wait_ge(n_["added"], i * DC + (m - 1))
                    pe.matmul(k.ps[:, 4 + m % 2, 0:T], y[:, P * m:P * m + P], weighT[:, :], start=True, stop=True)\
                      .then_inc(n_["spread"], 1)

                def use(i, b, products):
                    hi, lo = shaped(w_hi[:, b % PARTS, :], b), shaped(w_lo[:, b % PARTS, :], b)
                    x = xg if b < UP else hidT
                    pe.wait_ge(n_["hi_ready"], i * BLOCKS + (b + 1))
                    for part in (0, 1):
                        for out, c, (r, cols), first, last in products:
                            pe.matmul(out, x[part][:, c, :], hi[:, r, cols], start=first and part == 0, stop=False)
                    pe.wait_ge(n_["slot_free"], i * BLOCKS + (MOE_SLOTS + b + 1))
                    for out, c, (r, cols), first, last in products:
                        mm = pe.matmul(out, x[0][:, c, :], lo[:, r, cols], start=False, stop=last)
                    mm.then_inc(n_["part_free"], 1)

                pe.wait_ge(n_["zeroed"], 2)
                for u in range(2):
                    mm = pe.matmul(k.ps[:, 4 + u, :], hid[:, 0, 0:P], k.core[:, 0:512], start=True, stop=True)
                pe.wait_ge(n_["pick_ready"], 1)
                gather()
                n_items = count_of(pe)
                with pe.Fori(0, n_items) as i:
                    pe.wait_ge(n_["xg_act"], i + 1)
                    pe.wait_ge(n_["xg_dve"], i + 1)
                    for n in range(GROUPS):
                        if n >= 2:
                            pe.wait_ge(n_["hid_done"], i * GROUPS + (n - 1))
                        for b in range(4 * n, 4 * n + 4):
                            out = k.ps[:, 2 * (b // 2 % 2) + n % 2, :]
                            use(i, b, [(out, 4 * (b % 2) + c, (c, slice(0, WCOLS)), b % 2 == 0 and c == 0, b % 2 == 1 and c == 3)
                                       for c in range(4)])
                        if n < 4:
                            spread(i, 2 * n)
                            spread(i, 2 * n + 1)
                        if n == 4:
                            pe.wait_ge(n_["added"], i * DC + (DC - 1))
                            for t, (a, m) in enumerate(TILES):
                                mm = pe.transpose(k.ps[:, 4, a:a + m], weigh[0:m, t, :], ident[0:m, 0:m])
                            mm.then_inc(n_["weigh_turned"], 1)
                        if n >= 1:
                            turn(i, n - 1)
                    pe.wait_ge(n_["weigh_copied"], i + 1)
                    pe.wait_ge(n_["added"], i * DC + DC)
                    for b in range(UP, BLOCKS):
                        r = b - UP
                        if r % 2 == 0:
                            pe.wait_ge(n_["hidt_hi"], i * GROUPS + (r // 2 + 1))
                            pe.wait_ge(n_["hidt_lo"], i * GROUPS + (r // 2 + 1))
                        use(i, b, [(k.ps[:, 4 + u, :], 2 * r + j, (j, slice(512 * u, 512 * u + 512)), r == 0 and j == 0,
                                    b == BLOCKS - 1 and j == 1) for j in range(2) for u in range(2)])
                        if b == UP + 3:
                            turn(i, GROUPS - 1)
                        if b == GATHER:
                            pe.wait_ge(n_["pick_ready"], i + 2)
                            pe.wait_ge(n_["hidt_hi"], i * GROUPS + GROUPS)
                            pe.wait_ge(n_["hidt_lo"], i * GROUPS + GROUPS)
                            gather()
                for m in range(DC):
                    spread(n_items, m)

            @block.vector
            def _(dve):
                def picks(col):
                    for t, (_, n) in enumerate(TILES):
                        at = slot_of[0:n, t, col]
                        dve.tensor_scalar(pick[0:n, t, :], k.const("slots")[0:n, :], at, None, ALU.is_equal)
                        ins_ = dve.tensor_scalar(weigh[0:n, t, :], k.const("slots")[0:n, :], at, gate_of[0:n, t, col],
                                                 ALU.is_equal, ALU.mult)
                    ins_.then_inc(n_["pick_ready"], 1)

                def take_tokens(n):
                    dve.wait_ge(n_["gathered"], n)
                    dve.tensor_copy(xg[0][:, 4:8, :], k.ps[:, 7, :].rearrange("p (c n) -> p c n", c=4))
                    dve.tensor_copy(xg[1][:, 4:8, :], k.ps[:, 1, :].rearrange("p (c n) -> p c n", c=4)).then_inc(n_["xg_dve"], 1)

                def take_y(i):
                    dve.wait_ge(*used(i, -1))
                    dve.tensor_copy(y[:, 512:1024], k.ps[:, 5, :]).then_inc(n_["y_high"], 1)

                def add(i, m):
                    dve.wait_ge(n_["spread"], i * DC + (m + 1))
                    dve.tensor_tensor(k.residual[:, m, :], k.residual[:, m, :], k.ps[:, 4 + m % 2, 0:T], ALU.add).then_inc(n_["added"], 1)

                dve.memset(weighT[:, :], 0.0).then_inc(n_["zeroed"], 1)
                dve.memset(hid[:, 0, 0:P], 0.0).then_inc(n_["zeroed"], 1)
                picks(slice(0, 1))
                take_tokens(1)
                n_items = count_of(dve)
                with dve.Fori(0, n_items) as i:
                    for b in range(BLOCKS):
                        dve.wait_ge(n_["hi_ready"], i * BLOCKS + (b + 1))
                        dve.tensor_tensor(w_lo[:, b % PARTS, :], ring[:, b % MOE_SLOTS, :], w_hi[:, b % PARTS, :].bitcast(F32),
                                          ALU.subtract).then_inc(n_["slot_free"], 1)
                        if b == 2:
                            take_y(i)
                        n = (b - 5) // 4
                        if b % 4 == 1 and 0 <= n < GROUPS:
                            dve.wait_ge(n_["silu_done"], i * GROUPS + (n + 1))
                            if n >= 2:
                                dve.wait_ge(n_["hid_turned"], i * GROUPS + (n - 1))
                            dve.tensor_tensor(hid[:, n % 2, :], gated[:, n % 2, :], k.ps[:, 2 + n % 2, :], ALU.mult).then_inc(n_["hid_done"], 1)
                            if n < 4:
                                add(i, 2 * n)
                                add(i, 2 * n + 1)
                            if n == 4:
                                dve.wait_ge(n_["weigh_turned"], i + 1)
                                dve.tensor_copy(weighT[:, :], k.ps[:, 4, 0:T]).then_inc(n_["weigh_copied"], 1)
                            if n == 5:
                                picks(bass.ds(i + 1, 1))
                        n = (b - 9) // 4
                        if b % 4 == 1 and 0 <= n < GROUPS:
                            dve.wait_ge(n_["hidt_hi"], i * GROUPS + (n + 1))
                            dve.tensor_tensor(hidT[1][:, 4 * n:4 * n + 4, :], k.ps[:, 6 + n % 2, :].rearrange("p (f n) -> p f n", f=4),
                                              hidT[0][:, 4 * n:4 * n + 4, :].bitcast(F32), ALU.subtract).then_inc(n_["hidt_lo"], 1)
                        if b == GATHER + 3:
                            take_tokens(i + 2)
                take_y(n_items)
                for m in range(DC):
                    add(n_items, m)

            @block.scalar
            def _(act):
                def take_tokens(n):
                    act.wait_ge(n_["gathered"], n)
                    act.copy(xg[0][:, 0:4, :], k.ps[:, 6, :].rearrange("p (c n) -> p c n", c=4))
                    act.copy(xg[1][:, 0:4, :], k.ps[:, 0, :].rearrange("p (c n) -> p c n", c=4)).then_inc(n_["xg_act"], 1)

                def take_y(i):
                    act.wait_ge(*used(i, -1))
                    act.copy(y[:, 0:512], k.ps[:, 4, :]).then_inc(n_["y_low"], 1)

                take_tokens(1)
                n_items = count_of(act)
                with act.Fori(0, n_items) as i:
                    for b in range(BLOCKS):
                        act.wait_ge(loaded[b % MOE_SLOTS], i * (16 * BLOCKS // MOE_SLOTS) + 16 * (b // MOE_SLOTS + 1))
                        act.wait_ge(n_["part_free"], i * BLOCKS + (b + 1))
                        act.copy(w_hi[:, b % PARTS, :], ring[:, b % MOE_SLOTS, :]).then_inc(n_["hi_ready"], 1)
                        if b == 2:
                            take_y(i)
                        n = (b - 5) // 4
                        if b % 4 == 1 and 0 <= n < GROUPS:
                            act.wait_ge(*used(i, 4 * n + 3))
                            if n >= 2:
                                act.wait_ge(n_["hid_done"], i * GROUPS + (n - 1))
                            act.activation(gated[:, n % 2, :], k.ps[:, n % 2, :], ACT.Silu).then_inc(n_["silu_done"], 1)
                        n = (b - 9) // 4
                        if b % 4 == 1 and 0 <= n < GROUPS:
                            act.wait_ge(n_["hid_turned"], i * GROUPS + (n + 1))
                            act.copy(hidT[0][:, 4 * n:4 * n + 4, :], k.ps[:, 6 + n % 2, :].rearrange("p (f n) -> p f n", f=4)).then_inc(n_["hidt_hi"], 1)
                        if b == GATHER + 3:
                            take_tokens(i + 2)
                take_y(n_items)


def stage_store_tokens(k):
    with ExitStack() as s:
        norm = Norm(k, s, "norm_final")
        tok = k.sb(s, "out_tokens", [P, 3, D])
        turned, copied, stored = k.count("turned"), (k.count("copied"), k.count("copied_odd")), k.count("out_stored")
        with k.stage() as block:
            @block.tensor
            def _(pe):
                norm.sums(pe)
                for n in range(6):
                    i, u = n % 3, n // 3
                    a, rows = TILES[i]
                    for c in range(4):
                        if i == 0:
                            norm.await_chunk(pe, 4 * u + c)
                        mm = pe.transpose(k.ps[0:rows, 1 + n, P * c:P * c + P], k.act[:, 4 * u + c, a:a + rows], k.const("ident"))
                    mm.then_inc(*turned.up())

            def copier(eng, u):
                for i in range(3):
                    rows = TILES[i][1]
                    eng.wait_ge(*turned.at(3 * u + i + 1))
                    copy(eng, tok[0:rows, i, 512 * u:512 * u + 512], k.ps[0:rows, 1 + 3 * u + i, :]).then_inc(*copied[u].up())

            @block.scalar
            def _(act):
                norm.squares(act)
                norm.roots(act)
                copier(act, 0)

            @block.vector
            def _(dve):
                norm.apply(dve)
                copier(dve, 1)

            @block.sync
            def _(sp):
                for i, (a, rows) in enumerate(TILES):
                    for u in range(2):
                        sp.wait_ge(*copied[u].at(i + 1))
                    dst = k.outs[0][0, a:a + rows, :] if i < 2 else k.outs[1].rearrange("b t d -> (b t) d")
                    sp.dma_start(dst, tok[0:rows, i, :]).then_inc(*stored.up(16))
                sp.wait_ge(*stored.at(48))


def program(nc, ins, outs, core, attn):
    with ExitStack() as ctx:
        k = Kernel(nc, ctx, ins, outs, core, attn)
        with ExitStack() as early:
            k.ring = k.sb(early, "ring", [P, EARLY_SLOTS, SLOT])
            with ExitStack() as s:
                k.attn = k.sb(s, "attn", [P, k.attn_n])
                small = k.sb(s, "stick_bias", [P, 8]), k.sb(s, "bias8", [8, 1]), k.sb(s, "pages", [1, NB * 2], I32)
                stage_load(k, *small)
                qkv = k.sb(s, "qkv", [P, 24, T])
                keys = k.ring[:, 2, :].rearrange("p (b j n) -> p b j n", b=4, j=2)
                with ExitStack() as g:
                    parts = parts_of(k, g, "_qkv", DC)
                    stage_qkv(k, qkv, parts, keys)
                v_tokens = k.sb(s, "v_tokens", [P, 3, 1024])
                k_tokens = k.sb(s, "k_tokens", [P, 3, 1024])
                stage_kv_tokens(k, qkv, k_tokens, v_tokens)
                stage_attention(k, qkv, v_tokens, keys, *small)
            with ExitStack() as g:
                stage_out_even(k, SplitInput(k, g, "_out_even", k.act, DC))
            with ExitStack() as s:
                hidden = [k.sb(s, f"hidden{n}", [P, FC, T], F32R) for n in ("_hi", "_lo")]
                with ExitStack() as g:
                    parts = parts_of(k, g, "_up", DC)
                    stage_ffn_up(k, parts, *hidden)
                gemm_rows(k, "_down", 19, FC, hidden)
            with ExitStack() as s:
                proj = k.sb(s, "proj", [P, 24, T])
                dt = k.sb(s, "dt", [HM, T])
                xc = k.sb(s, "xc", [P, CC, T])
                par = k.sb(s, "dt_params", [HM, 4])
                hg = {"k": k.act[:, 0:4, :], "g": k.act[:, 4:8, :]}
                dta = {"acum": k.sb(s, "acum", [HM, T]), "wend": k.sb(s, "wend", [HM, T]), "tok": k.sb(s, "dt_tokens", [P, 3, 48]),
                       "skip": k.sb(s, "skip", [P, 8]), "sq": k.act}
                with ExitStack() as c:
                    conv_in = k.sb(c, "conv_in", [P, CC, TP + 3])
                    conv_in_s = k.sb(c, "conv_in_s", [P, CC, NB, NT + 3])
                    with ExitStack() as g:
                        parts = parts_of(k, g, "_in_odd", DC)
                        stage_in_odd(k, parts, proj, conv_in, conv_in_s, dt, xc, hg, dta, par)
                    stage_turn_decays(k, conv_in, conv_in_s, dt, dta, par)
                mixed_out = k.sb(s, "mixed_out", [P, 12, T])
                with ExitStack() as c:
                    stage_hgrn(k, proj, hg, mixed_out)
                with ExitStack() as c:
                    dta["rs"] = k.sb(c, "group_rstd", [P, 4, T])
                    stage_ssd(k, proj, xc, dt, dta, mixed_out)
                with ExitStack() as c:
                    source = SplitInput(k, c, "_out_odd", mixed_out, 12)
                    gemm_rows(k, "_out_odd", 35, 12, source.parts, source)
        with ExitStack() as s:
            moe = {"tokens_hi": k.sb(s, "tokens_hi", [P, 3, D], F32R), "tokens_lo": k.sb(s, "tokens_lo", [P, 3, D], F32R),
                   "slot": k.sb(s, "item_slot", [P, 3, MAX_ITEMS + 1]),
                   "gate": k.sb(s, "item_gate", [P, 3, MAX_ITEMS + 1]), "table": k.sb(s, "item_table", [1, MAX_ITEMS + 2], I32)}
            stage_route(k, moe)
            stage_experts(k, moe)
        stage_store_tokens(k)


_INS = ['x_prompt', 'x_sample', 'cache_win_k', 'cache_win_v', 'cache_sb_k', 'cache_sb_v', 'page_table',
        'state_hgrn', 'state_ssm', 'state_conv', 'norm_mix_even', 'w_in_even', 'w_out_even', 'sb_bias',
        'norm_ffn_even', 'w1_ffn', 'w3_ffn', 'w2_ffn', 'norm_mix_odd', 'w_in_odd', 'hgrn_lb_logits',
        'hgrn_gain', 'conv_w', 'conv_b', 'dt_bias', 'a_log', 'd_skip', 'ssm_gain', 'w_out_odd',
        'norm_ffn_odd', 'w_router', 'we1', 'we3', 'we2', 'norm_final']
_OUTS = [(1, TP, D), (NB, NT, D), (1, 1, TP, 8, HD), (1, 1, TP, 8, HD), (NB, 1, NT, 8, HD), (NB, 1, NT, 8, HD),
         (1, 1, TP, 8, HD), (1, 1, TP, 8, HD), (NB, 1, NT, 8, HD), (NB, 1, NT, 8, HD),
         (1, 1, HC, P, P), (NB, 1, HC, P, P), (1, 1, HM, 64, 64), (NB, 1, HM, 64, 64), (1, 1, 3, 1536), (NB, 1, 3, 1536)]


def kernel(**inputs):
    import numpy as _np
    import concourse.bacc as _bacc
    from concourse import mybir as _mybir
    from concourse.bass_utils import run_bass_kernel_spmd as _run

    nc = _bacc.Bacc("TRN2", target_bir_lowering=False, num_devices=1)
    core, attn = shape_constants()
    arrays, ins, outs = {}, {}, []
    given = {name: _np.ascontiguousarray(inputs[name]) for name in _INS}
    given["vectors"] = _np.concatenate([given[name].reshape(-1, P) for name in VEC], 0)
    given["core_tables"] = _np.concatenate(list(core.values()), 1)
    given["attn_tables"] = _np.concatenate(list(attn.values()), 1)
    for name, a in given.items():
        arrays[f"in_{name}_dram"] = a
        ins[name] = nc.dram_tensor(f"in_{name}_dram", a.shape, _mybir.dt.from_np(a.dtype), kind="ExternalInput").ap()
    for i, shape in enumerate(_OUTS):
        outs.append(nc.dram_tensor(f"out_{i}_dram", shape, F32, kind="ExternalOutput").ap())
    program(nc, ins, outs, core, attn)
    r = _run(nc, [arrays], core_ids=[0])
    return tuple(r.results[0][f"out_{i}_dram"] for i in range(len(_OUTS)))
```
